# Optimizing a Trainium2 kernel written in Bass

```python
import math
import jax
import jax.numpy as jnp
from jax import lax
import numpy as np

D_MODEL = 1024
BATCH = 1
SEQ = 512
DEPTH = 2
DEC_BATCH = 8
DEC_SEQ = 1
PAST_LEN = 256
PAGE_SIZE = 128

N_EVEN = (DEPTH + 1) // 2
N_ODD = DEPTH // 2
D_MIX = D_MODEL
H_A = 4
DV_A = D_MIX // 2 // H_A
DK_A = DV_A // 2
GLA_RANK = 16
GLA_TAU = 16.0
H_B = 4
DK_B = D_MIX // 2 // H_B
DV_B = DK_B
CONV_W = 4
H_C = 8
HD_C = D_MIX // 2 // H_C
D_RNN = D_MIX // 2
H_D = 8
BD_D = D_RNN // H_D
RG_C = 8.0
D_FF = ((8 * D_MODEL // 3 + 255) // 256) * 256
CHUNK = 64
Q_BLOCK = 128
EPS = 1e-6
EVEN_SIZES = (H_A * DK_A, H_A * DK_A, H_A * DV_A, H_A * DV_A, GLA_RANK, 3 * H_B * DK_B, H_B * DV_B, H_B, H_B)
ODD_SIZES = (H_C * HD_C, H_C * HD_C, H_C * HD_C, D_RNN, D_RNN)
D_IN_EVEN = sum(EVEN_SIZES)
D_IN_ODD = sum(ODD_SIZES)

kernel_name = 'hybrid_gla_gdn_stickbreak_rglru_macaron_step'

def split_cols(x, sizes):
    out, start = [], 0
    for s in sizes:
        out.append(x[..., start:start + s])
        start += s
    return out

def rmsnorm(x, g):
    xf = x.astype(jnp.float32)
    y = xf * lax.rsqrt(jnp.mean(xf * xf, axis=-1, keepdims=True) + EPS)
    return (y * g.astype(jnp.float32)).astype(x.dtype)

def l2norm(x):
    return x * lax.rsqrt(jnp.sum(x * x, axis=-1, keepdims=True) + EPS)

def half_ffn(x, g, w_gate, w_up, w_down):
    h = rmsnorm(x, g)
    return 0.5 * ((jax.nn.silu(h @ w_gate) * (h @ w_up)) @ w_down)

def causal_dwconv(x, hist, w):
    xe = jnp.concatenate([hist.astype(x.dtype), x], axis=1)
    y = lax.conv_general_dilated(xe, w[:, None, :].astype(x.dtype), (1,), 'VALID',
                                 dimension_numbers=('NWC', 'WIO', 'NWC'), feature_group_count=x.shape[-1])
    return y, xe[:, xe.shape[1] - (CONV_W - 1):]

def to_chunks(a, c):
    b, t = a.shape[:2]
    n = -(-t // c)
    a = jnp.pad(a, [(0, 0), (0, n * c - t)] + [(0, 0)] * (a.ndim - 2))
    return jnp.moveaxis(a.reshape((b, n, c) + a.shape[2:]), 1, 0)

def from_chunks(a, t):
    a = jnp.moveaxis(a, 0, 1)
    return a.reshape((a.shape[0], -1) + a.shape[3:])[:, :t]

def gla_chunked(q, k, v, log_g, s0):
    t = q.shape[1]
    c = min(CHUNK, t)
    incl = jnp.tril(jnp.ones((c, c), bool))

    def step(s, inp):
        qi, ki, vi, gi = inp
        g = jnp.cumsum(gi, axis=1)
        rel = jnp.exp(jnp.where(incl[None, :, :, None, None], g[:, :, None] - g[:, None, :], -jnp.inf))
        att = jnp.einsum('bthd,btshd,bshd->bhts', qi, rel, ki)
        o = jnp.einsum('bhts,bshv->bthv', att, vi) + jnp.einsum('bthd,bhdv->bthv', qi * jnp.exp(g), s)
        g_end = g[:, -1]
        s = s * jnp.exp(g_end)[..., None] + jnp.einsum('bshd,bshv->bhdv', ki * jnp.exp(g_end[:, None] - g), vi)
        return s, o

    s, o = lax.scan(step, s0, (to_chunks(q, c), to_chunks(k, c), to_chunks(v, c), to_chunks(log_g, c)))
    return from_chunks(o, t), s

def gdn_chunked(q, k, v, log_g, beta, s0):
    t = q.shape[1]
    c = min(CHUNK, t)
    dk = q.shape[-1]
    incl = jnp.tril(jnp.ones((c, c), bool))
    strict = jnp.tril(jnp.ones((c, c), bool), -1)
    eye = jnp.eye(c, dtype=jnp.float32)

    def step(s, inp):
        qi, ki, vi, gi, bi = inp
        g = jnp.cumsum(gi, axis=1).swapaxes(1, 2)
        bh = bi.swapaxes(1, 2)
        rel = jnp.exp(jnp.where(incl, g[..., :, None] - g[..., None, :], -jnp.inf))
        kk = jnp.einsum('bthd,bshd->bhts', ki, ki)
        m = eye + jnp.where(strict, kk * rel, 0.0) * bh[..., :, None]
        kh = ki.swapaxes(1, 2)
        vh = vi.swapaxes(1, 2)
        rhs = jnp.concatenate([kh * (bh * jnp.exp(g))[..., None], vh * bh[..., None]], axis=-1)
        sol = lax.linalg.triangular_solve(m, rhs, left_side=True, lower=True, unit_diagonal=True)
        w, u = sol[..., :dk], sol[..., dk:]
        v_new = u - jnp.einsum('bhtd,bhdv->bhtv', w, s)
        qk = jnp.einsum('bthd,bshd->bhts', qi, ki) * rel
        o = jnp.einsum('bhts,bhsv->bhtv', qk, v_new) + jnp.einsum('bthd,bht,bhdv->bhtv', qi, jnp.exp(g), s)
        g_end = g[..., -1]
        s = s * jnp.exp(g_end)[..., None, None] + jnp.einsum('bhsd,bhs,bhsv->bhdv', kh, jnp.exp(g_end[..., None] - g), v_new)
        return s, o.swapaxes(1, 2)

    s, o = lax.scan(step, s0, (to_chunks(q, c), to_chunks(k, c), to_chunks(v, c), to_chunks(log_g, c), to_chunks(beta, c)))
    return from_chunks(o, t), s

def stick_breaking(q, k, v, bias, offset):
    bsz, tq, h, d = q.shape
    tk = k.shape[1]
    qb = min(Q_BLOCK, tq)
    nb = -(-tq // qb)
    qp = jnp.moveaxis(jnp.pad(q, ((0, 0), (0, nb * qb - tq), (0, 0), (0, 0))).reshape(bsz, nb, qb, h, d), 1, 0)
    key_idx = jnp.arange(tk)
    scale = d ** -0.5
    bias = bias.astype(jnp.float32)[None, :, None, None]

    def block(args):
        qblk, b = args
        qpos = offset + b * qb + jnp.arange(qb)
        z = jnp.einsum('bqhd,bkhd->bhqk', qblk, k) * scale + bias
        mask = key_idx[None, :] < qpos[:, None]
        log_1mb = jnp.where(mask, jax.nn.log_sigmoid(-z), 0.0)
        acc = lax.cumsum(log_1mb, axis=3, reverse=True) - log_1mb
        wts = jnp.where(mask, jnp.exp(jax.nn.log_sigmoid(z) + acc), 0.0)
        return jnp.einsum('bhqk,bkhd->bqhd', wts, v)

    o = lax.map(block, (qp, jnp.arange(nb)))
    return from_chunks(o, tq)

def rg_lru(x, h0, offset, w_a, b_a, w_x, b_x, lam):
    bsz, t, _ = x.shape
    xb = x.reshape(bsz, t, H_D, BD_D)
    r = jax.nn.sigmoid(jnp.einsum('bthi,hij->bthj', xb, w_a).reshape(bsz, t, D_RNN) + b_a)
    i = jax.nn.sigmoid(jnp.einsum('bthi,hij->bthj', xb, w_x).reshape(bsz, t, D_RNN) + b_x)
    log_a = -RG_C * r * jax.nn.softplus(-lam)
    reset = ((offset + jnp.arange(t)) == 0)[None, :, None]
    a = jnp.where(reset, 0.0, jnp.exp(log_a))
    mult = jnp.where(reset, 1.0, jnp.sqrt(-jnp.expm1(2.0 * log_a)))
    bterm = (mult * (i * x)).at[:, 0].add(a[:, 0] * h0)
    _, hs = lax.associative_scan(lambda l, rr: (l[0] * rr[0], rr[0] * l[1] + rr[1]), (a, bterm), axis=1)
    return hs

def even_mixer(h, s_gla, s_gdn, conv_hist, w_in, gla_w_gate, gla_b_gate, gla_onorm,
               gdn_conv_w, gdn_a_log, gdn_dt_bias, gdn_onorm, w_out):
    bsz, t, _ = h.shape
    f32 = jnp.float32
    qa, ka, va, ra, la, qkv_b, zb, ab, bb = split_cols(h @ w_in, EVEN_SIZES)
    qa = qa.astype(f32).reshape(bsz, t, H_A, DK_A) * DK_A ** -0.5
    ka = ka.astype(f32).reshape(bsz, t, H_A, DK_A)
    va = va.astype(f32).reshape(bsz, t, H_A, DV_A)
    log_g = (jax.nn.log_sigmoid((la @ gla_w_gate).astype(f32) + gla_b_gate) / GLA_TAU).reshape(bsz, t, H_A, DK_A)
    oa, s_gla = gla_chunked(qa, ka, va, log_g, s_gla.astype(f32))
    oa = rmsnorm(oa, gla_onorm) * jax.nn.silu(ra.astype(f32).reshape(bsz, t, H_A, DV_A))
    qkv, conv_hist = causal_dwconv(qkv_b, conv_hist, gdn_conv_w)
    qb, kb, vb = split_cols(jax.nn.silu(qkv.astype(f32)), (H_B * DK_B, H_B * DK_B, H_B * DV_B))
    qb = l2norm(qb.reshape(bsz, t, H_B, DK_B)) * DK_B ** -0.5
    kb = l2norm(kb.reshape(bsz, t, H_B, DK_B))
    vb = vb.reshape(bsz, t, H_B, DV_B)
    log_gb = -jnp.exp(gdn_a_log.astype(f32)) * jax.nn.softplus(ab.astype(f32) + gdn_dt_bias)
    beta = jax.nn.sigmoid(bb.astype(f32))
    ob, s_gdn = gdn_chunked(qb, kb, vb, log_gb, beta, s_gdn.astype(f32))
    ob = rmsnorm(ob, gdn_onorm) * jax.nn.silu(zb.astype(f32).reshape(bsz, t, H_B, DV_B))
    o = jnp.concatenate([oa.reshape(bsz, t, -1), ob.reshape(bsz, t, -1)], axis=-1).astype(h.dtype)
    return o @ w_out, s_gla, s_gdn, conv_hist

def odd_mixer(h, k_past, v_past, h0, conv_hist, w_in, sb_bias, rg_conv_w, rg_conv_b, rg_w_a, rg_b_a,
              rg_w_x, rg_b_x, rg_lambda, w_out):
    bsz, t, _ = h.shape
    f32 = jnp.float32
    qc, kc, vc, xr, yr = split_cols(h @ w_in, ODD_SIZES)
    qc = qc.reshape(bsz, t, H_C, HD_C)
    kc = kc.reshape(bsz, t, H_C, HD_C)
    vc = vc.reshape(bsz, t, H_C, HD_C)
    offset = k_past.shape[1]
    k_all = jnp.concatenate([k_past.astype(f32), kc.astype(f32)], axis=1)
    v_all = jnp.concatenate([v_past.astype(f32), vc.astype(f32)], axis=1)
    oc = stick_breaking(qc.astype(f32), k_all, v_all, sb_bias, offset)
    xc, conv_hist = causal_dwconv(xr, conv_hist, rg_conv_w)
    hs = rg_lru(xc.astype(f32) + rg_conv_b, h0.astype(f32), offset, rg_w_a, rg_b_a, rg_w_x, rg_b_x, rg_lambda)
    od = hs * jax.nn.gelu(yr.astype(f32))
    o = jnp.concatenate([oc.reshape(bsz, t, -1), od], axis=-1).astype(h.dtype)
    return o @ w_out, kc, vc, hs[:, -1], conv_hist

def setup_inputs(seed: int = 0) -> dict:
    key = jax.random.key(seed)
    ks = jax.random.split(key, 40)
    f32 = jnp.float32

    def nrm(i, shape, scale=1.0):
        return scale * jax.random.normal(ks[i], shape, f32)

    n_pages = PAST_LEN // PAGE_SIZE
    n_used = DEC_BATCH * n_pages
    n_pool = n_used + (n_used + 3) // 4
    page_table = jax.random.permutation(ks[9], n_pool)[:n_used].reshape(DEC_BATCH, n_pages).astype(jnp.int32)
    dt = jnp.exp(jax.random.uniform(ks[20], (N_EVEN, H_B), f32, minval=math.log(1e-3), maxval=math.log(1e-1)))
    a_c = jax.random.uniform(ks[32], (N_ODD, D_RNN), f32, minval=0.9, maxval=0.999)
    sig = a_c ** (1.0 / RG_C)
    return {
        'x_prompt': nrm(0, (BATCH, SEQ, D_MODEL)),
        'x_sample': nrm(1, (DEC_BATCH, DEC_SEQ, D_MODEL)),
        'state_gla': nrm(2, (N_EVEN, DEC_BATCH, H_A, DK_A, DV_A)),
        'state_gdn': nrm(3, (N_EVEN, DEC_BATCH, H_B, DK_B, DV_B), 0.5),
        'state_gdn_conv': nrm(4, (N_EVEN, DEC_BATCH, CONV_W - 1, 3 * H_B * DK_B)),
        'cache_sb_k': nrm(5, (N_ODD, n_pool, PAGE_SIZE, H_C, HD_C)),
        'cache_sb_v': nrm(6, (N_ODD, n_pool, PAGE_SIZE, H_C, HD_C)),
        'state_rg_h': nrm(7, (N_ODD, DEC_BATCH, D_RNN), 0.5),
        'state_rg_conv': nrm(8, (N_ODD, DEC_BATCH, CONV_W - 1, D_RNN)),
        'page_table': page_table,
        'ln_ffn': 1.0 + nrm(10, (DEPTH, 2, D_MODEL), 0.02),
        'ffn_w_gate': nrm(11, (DEPTH, 2, D_MODEL, D_FF), D_MODEL ** -0.5),
        'ffn_w_up': nrm(12, (DEPTH, 2, D_MODEL, D_FF), D_MODEL ** -0.5),
        'ffn_w_down': nrm(13, (DEPTH, 2, D_FF, D_MODEL), D_FF ** -0.5),
        'ln_mix_e': 1.0 + nrm(14, (N_EVEN, D_MODEL), 0.02),
        'w_in_e': nrm(15, (N_EVEN, D_MODEL, D_IN_EVEN), D_MODEL ** -0.5),
        'gla_w_gate': nrm(16, (N_EVEN, GLA_RANK, H_A * DK_A), GLA_RANK ** -0.5),
        'gla_b_gate': nrm(17, (N_EVEN, H_A * DK_A), 0.01),
        'gla_onorm': 1.0 + nrm(18, (N_EVEN, DV_A), 0.02),
        'gdn_conv_w': nrm(19, (N_EVEN, CONV_W, 3 * H_B * DK_B), CONV_W ** -0.5),
        'gdn_a_log': jnp.log(jax.random.uniform(ks[21], (N_EVEN, H_B), f32, minval=1.0, maxval=16.0)),
        'gdn_dt_bias': dt + jnp.log(-jnp.expm1(-dt)),
        'gdn_onorm': 1.0 + nrm(22, (N_EVEN, DV_B), 0.02),
        'w_out_e': nrm(23, (N_EVEN, D_MIX, D_MODEL), D_MIX ** -0.5),
        'ln_mix_o': 1.0 + nrm(24, (N_ODD, D_MODEL), 0.02),
        'w_in_o': nrm(25, (N_ODD, D_MODEL, D_IN_ODD), D_MODEL ** -0.5),
        'sb_bias': jax.random.uniform(ks[35], (N_ODD, H_C), f32, minval=-7.5, maxval=-5.5),
        'rg_conv_w': nrm(26, (N_ODD, CONV_W, D_RNN), CONV_W ** -0.5),
        'rg_conv_b': nrm(27, (N_ODD, D_RNN), 0.01),
        'rg_w_a': nrm(28, (N_ODD, H_D, BD_D, BD_D), BD_D ** -0.5),
        'rg_b_a': nrm(29, (N_ODD, D_RNN), 0.01),
        'rg_w_x': nrm(30, (N_ODD, H_D, BD_D, BD_D), BD_D ** -0.5),
        'rg_b_x': nrm(31, (N_ODD, D_RNN), 0.01),
        'rg_lambda': jnp.log(sig) - jnp.log1p(-sig),
        'w_out_o': nrm(33, (N_ODD, D_MIX, D_MODEL), D_MIX ** -0.5),
        'ln_final': 1.0 + nrm(34, (D_MODEL,), 0.02),
    }

def reference(x_prompt, x_sample, state_gla, state_gdn, state_gdn_conv, cache_sb_k, cache_sb_v,
              state_rg_h, state_rg_conv, page_table, ln_ffn, ffn_w_gate, ffn_w_up, ffn_w_down,
              ln_mix_e, w_in_e, gla_w_gate, gla_b_gate, gla_onorm, gdn_conv_w, gdn_a_log, gdn_dt_bias,
              gdn_onorm, w_out_e, ln_mix_o, w_in_o, sb_bias, rg_conv_w, rg_conv_b, rg_w_a, rg_b_a, rg_w_x, rg_b_x,
              rg_lambda, w_out_o, ln_final):
    f32 = jnp.float32
    xp, xs = x_prompt, x_sample
    bp, bs = xp.shape[0], xs.shape[0]
    n_pages = page_table.shape[1]
    page = cache_sb_k.shape[2]
    gla_p, gla_s, gdn_p, gdn_s, gcv_p, gcv_s = [], [], [], [], [], []
    sbk_p, sbk_s, sbv_p, sbv_s, rgh_p, rgh_s, rgc_p, rgc_s = [], [], [], [], [], [], [], []
    for layer in range(DEPTH):
        xp = xp + half_ffn(xp, ln_ffn[layer, 0], ffn_w_gate[layer, 0], ffn_w_up[layer, 0], ffn_w_down[layer, 0])
        xs = xs + half_ffn(xs, ln_ffn[layer, 0], ffn_w_gate[layer, 0], ffn_w_up[layer, 0], ffn_w_down[layer, 0])
        if layer % 2 == 0:
            e = layer // 2
            wts = (w_in_e[e], gla_w_gate[e], gla_b_gate[e], gla_onorm[e], gdn_conv_w[e], gdn_a_log[e],
                   gdn_dt_bias[e], gdn_onorm[e], w_out_e[e])
            mp, s1, s2, s3 = even_mixer(rmsnorm(xp, ln_mix_e[e]), jnp.zeros((bp, H_A, DK_A, DV_A), f32),
                                        jnp.zeros((bp, H_B, DK_B, DV_B), f32),
                                        jnp.zeros((bp, CONV_W - 1, 3 * H_B * DK_B), xp.dtype), *wts)
            ms, t1, t2, t3 = even_mixer(rmsnorm(xs, ln_mix_e[e]), state_gla[e], state_gdn[e], state_gdn_conv[e], *wts)
            gla_p.append(s1); gdn_p.append(s2); gcv_p.append(s3)
            gla_s.append(t1); gdn_s.append(t2); gcv_s.append(t3)
        else:
            o = layer // 2
            wts = (w_in_o[o], sb_bias[o], rg_conv_w[o], rg_conv_b[o], rg_w_a[o], rg_b_a[o], rg_w_x[o], rg_b_x[o],
                   rg_lambda[o], w_out_o[o])
            empty = jnp.zeros((bp, 0, H_C, HD_C), xp.dtype)
            mp, s1, s2, s3, s4 = odd_mixer(rmsnorm(xp, ln_mix_o[o]), empty, empty, jnp.zeros((bp, D_RNN), f32),
                                           jnp.zeros((bp, CONV_W - 1, D_RNN), xp.dtype), *wts)
            k_past = cache_sb_k[o][page_table].reshape(bs, n_pages * page, H_C, HD_C)
            v_past = cache_sb_v[o][page_table].reshape(bs, n_pages * page, H_C, HD_C)
            ms, t1, t2, t3, t4 = odd_mixer(rmsnorm(xs, ln_mix_o[o]), k_past, v_past, state_rg_h[o], state_rg_conv[o], *wts)
            sbk_p.append(s1); sbv_p.append(s2); rgh_p.append(s3); rgc_p.append(s4)
            sbk_s.append(t1); sbv_s.append(t2); rgh_s.append(t3); rgc_s.append(t4)
        xp = xp + mp
        xs = xs + ms
        xp = xp + half_ffn(xp, ln_ffn[layer, 1], ffn_w_gate[layer, 1], ffn_w_up[layer, 1], ffn_w_down[layer, 1])
        xs = xs + half_ffn(xs, ln_ffn[layer, 1], ffn_w_gate[layer, 1], ffn_w_up[layer, 1], ffn_w_down[layer, 1])
    y_prompt = rmsnorm(xp, ln_final)
    y_sample = rmsnorm(xs, ln_final)
    new_gla_p = jnp.stack(gla_p).astype(state_gla.dtype)
    new_gla_s = jnp.stack(gla_s).astype(state_gla.dtype)
    new_gdn_p = jnp.stack(gdn_p).astype(state_gdn.dtype)
    new_gdn_s = jnp.stack(gdn_s).astype(state_gdn.dtype)
    new_gcv_p = jnp.stack(gcv_p).astype(state_gdn_conv.dtype)
    new_gcv_s = jnp.stack(gcv_s).astype(state_gdn_conv.dtype)
    new_sbk_p = jnp.stack(sbk_p).astype(cache_sb_k.dtype)
    new_sbk_s = jnp.stack(sbk_s).astype(cache_sb_k.dtype)
    new_sbv_p = jnp.stack(sbv_p).astype(cache_sb_v.dtype)
    new_sbv_s = jnp.stack(sbv_s).astype(cache_sb_v.dtype)
    new_rgh_p = jnp.stack(rgh_p).astype(state_rg_h.dtype)
    new_rgh_s = jnp.stack(rgh_s).astype(state_rg_h.dtype)
    new_rgc_p = jnp.stack(rgc_p).astype(state_rg_conv.dtype)
    new_rgc_s = jnp.stack(rgc_s).astype(state_rg_conv.dtype)
    return (y_prompt, y_sample, new_gla_p, new_gla_s, new_gdn_p, new_gdn_s, new_gcv_p, new_gcv_s,
            new_sbk_p, new_sbk_s, new_sbv_p, new_sbv_s, new_rgh_p, new_rgh_s, new_rgc_p, new_rgc_s)


_drawn_inputs = setup_inputs


def setup_inputs(seed=0):
    import zlib

    import numpy as np

    out = dict(_drawn_inputs(seed))
    spreads = {}
    factors = {'ln_ffn': 2.667,
     'gla_b_gate': 8.0,
     'gla_onorm': 77.607,
     'gdn_onorm': 79.627,
     'ln_mix_o': 8.132,
     'sb_bias': 200.0,
     'rg_b_a': 33.172,
     'rg_b_x': 27.469,
     'ln_final': 23.087,
     'rg_conv_b': 11.083}
    for name, (base, spread) in spreads.items():
        noise = np.random.default_rng([zlib.crc32(name.encode()), seed]).standard_normal(out[name].shape)
        drawn = base * np.exp(spread * noise) if base else spread * noise
        out[name] = jnp.asarray(drawn.astype(out[name].dtype))
    for name, factor in factors.items():
        out[name] = (out[name] * factor).astype(out[name].dtype)
    return out
```

```python
from contextlib import ExitStack

import concourse.bass as bass
from concourse import mybir

F32 = mybir.dt.float32
F32R = mybir.dt.float32r
I32 = mybir.dt.int32
ACT = mybir.ActivationFunctionType
ALU = mybir.AluOpType
AX = mybir.AxisListType

P = 128
EPS = 1e-6
GLA_TAU = 16.0
RG_C = 8.0
CLAMP = 80.0
LOOKAHEAD = 3
SPLIT_SLOTS = 4
STAGE_SLOTS = 2
UNIT = 8
LN_EXP = "natural_log_exp_and_others"


STAGES = [("ffn", 0), ("mix_e", 0), ("ffn", 1), ("ffn", 2), ("mix_o", 0), ("ffn", 3)]


def loop(engine, first, last, body):
    if last - first == 1:
        body(first)
    elif last > first:
        with engine.Fori(first, last) as t:
            body(t)


def build_step(nc, i, o):
    TP = i["x_prompt"].shape[1]
    TS = i["x_sample"].shape[0]
    TOK = TP + TS
    HALF = TOK // 2
    DM = i["x_prompt"].shape[2]
    FF = i["ffn_w_gate"].shape[3]
    KD, KF = DM // P, FF // P
    NB = TP // P
    LAYERS = i["ln_ffn"].shape[0]
    HB = i["gdn_a_log"].shape[1]
    HA = i["state_gla"].shape[2]
    DKA = i["state_gla"].shape[3]
    DV = i["state_gla"].shape[4]
    RANK = i["gla_w_gate"].shape[1]
    HC = i["sb_bias"].shape[1]
    HDC = i["cache_sb_k"].shape[4]
    PAGES = i["page_table"].shape[1]
    POOL = i["cache_sb_k"].shape[1]
    CW = i["gdn_conv_w"].shape[1]
    KR = i["state_rg_h"].shape[2] // P
    HP = HA // 2
    QKV = 3 * HB
    TAIL = CW - 1 + TS
    assert TOK % 4 == 0 and DM % P == 0 and FF % P == 0 and TP % P == 0 and KF % 2 == 0 and KD % 4 == 0

    E_TILES = QKV + 2 * HP + 2 * HA + HB
    O_TILES = 5 * KR
    PARTS = -(-KF // UNIT)
    PHASES = {"ffn": [("in", 2 * KF), ("down", PARTS * KD)],
              "mix_e": [("mix_e", 1 + E_TILES), ("out_e", KD)],
              "mix_o": [("mix_o", O_TILES), ("out_o", KD)]}
    FIRST, UNITS = {}, 0
    for stage_name, f in STAGES:
        for name, n in PHASES[stage_name]:
            FIRST[name + str(f)] = UNITS
            UNITS += n
    LAST_NORM = len(STAGES)

    ROWS_A = [("ln_ffn", LAYERS * 2 * KD), ("ln_mix_e", KD), ("ln_mix_o", KD), ("ln_final", KD),
              ("gla_b_gate", HP), ("gla_onorm", 1), ("gdn_onorm", 1), ("gdn_conv_w", CW * QKV)]
    ROWS_B = [("rg_conv_w", CW * KR), ("rg_conv_b", KR), ("rg_b_a", KR), ("rg_b_x", KR), ("rg_lambda", KR)]
    PRM, cols = {}, 0
    for name, n in ROWS_A + ROWS_B:
        PRM[name] = cols
        cols += n
    NA = sum(n for _, n in ROWS_A)
    NPRM = cols
    NORM_PRM = [PRM["ln_ffn"] + KD * f if name == "ffn" else PRM["ln_" + name] for name, f in STAGES]
    NORM_PRM.append(PRM["ln_final"])

    E_STORES = 7
    O_STORES = 9
    KC = HC // 2
    WC = HC * HDC
    O_PARTS = HA + HB if ("mix_e", 0) in STAGES else 0
    assert NB == 4 and TP == 512 and HDC * 2 == P and KC == KR
    SCORE = [(0, TP), (TP, TP - P), (2 * TP, TP - 2 * P), (2 * TP - P, P)]
    SCORES = 2 * TP + 2 * P

    def rows(ap):
        names = " ".join("abcd"[:len(ap.shape)])
        flat = ap.rearrange(f"{names} -> ({names})") if len(ap.shape) > 1 else ap
        return flat.rearrange("(r p) -> r p", p=P)

    ctx = ExitStack()
    with ctx:
        def sb(name, shape, dt=F32, stack=ctx):
            return stack.enter_context(nc.sbuf_tensor(name, shape, dt))

        def sem(name):
            return ctx.enter_context(nc.semaphore(name))

        ident = sb("ident", [P, P])
        ones = sb("ones", [P, P])
        prm = sb("prm", [P, NPRM])
        xT = sb("xT", [P, KD, TOK])
        ssum = sb("ssum", [P, TOK])
        rstd = sb("rstd", [P, TOK])
        tmp = sb("tmp", [P, 4, TOK])
        stage = sb("stage", [P, STAGE_SLOTS, UNIT * P])
        whi = sb("whi", [P, SPLIT_SLOTS, UNIT * P], F32R)
        wlo = sb("wlo", [P, SPLIT_SLOTS, UNIT * P], F32R)
        histG = sb("histG", [P, QKV, TS, CW - 1])
        histR = sb("histR", [P, KR, TS, CW - 1])
        h0T = sb("h0T", [P, KR, TS])
        PS = ctx.enter_context(nc.psum_tensor("PS", [P, 8, 512], F32))

        def pair(n):
            return PS[:, 2 * n:2 * n + 2, 0:HALF]

        def two(ap):
            return ap.rearrange("p (a b) -> p a b", a=2)

        def banks(n, m):
            return PS[:, n:n + m, :].rearrange("p a b -> p (a b)")

        def col(name, n=0):
            return prm[:, PRM[name] + n:PRM[name] + n + 1]

        def tile(buf, m):
            return buf[:, bass.ds(m, 1), :].rearrange("p a b -> p (a b)")

        shared = ExitStack()
        hh = sb("hh", [P, KD, TOK], F32R, shared)
        hl = sb("hl", [P, KD, TOK], F32R, shared)
        st = ExitStack()
        act_h = sb("act_h", [P, KF, TOK], F32R, st)
        act_l = sb("act_l", [P, KF, TOK], F32R, st)
        st.close()
        st = ExitStack()
        xrow = sb("xrow", [P, NB, DM], F32, st)
        xsrow = sb("xsrow", [TS, DM], F32, st)
        prow_a = sb("prow_a", [NA, P], F32, st)
        prow_b = sb("prow_b", [NPRM - NA, P], F32, st)
        hrow_g = sb("hrow_g", [TS * (CW - 1), QKV * P], F32, st)
        hrow_r = sb("hrow_r", [TS * (CW - 1), KR * P], F32, st)
        hrow_0 = sb("hrow_0", [TS, KR * P], F32, st)
        st.close()
        st = ExitStack()
        yrow = sb("yrow", [P, NB, DM], F32, st)
        ysrow = sb("ysrow", [TS, DM], F32, st)
        st.close()
        BQ, BK, BV = 0, HB, 2 * HB
        AQ, AK, AV, AR, BZ = QKV, QKV + HP, QKV + 2 * HP, QKV + 2 * HP + HA, QKV + 2 * HP + 2 * HA
        st = ExitStack()
        oE = sb("oE", [P, E_TILES, TOK], F32R, st)
        st.close()
        st = ExitStack()
        prE = sb("prE", [P, E_TILES, TOK], F32, st)
        stA_s = sb("stA_s", [P, TS, HP, DV], F32, st)
        stB_s = sb("stB_s", [P, TS, HB, DV], F32, st)
        small = sb("small", [96, TOK], F32, st)
        wgate = sb("wgate", [RANK, HP * P], F32, st)
        gdnp = sb("gdnp", [36, 4], F32, st)
        masks = sb("masks", [P, 7, P], F32, st)
        keep = sb("keep", [P, P], F32, st)
        strict = sb("strict", [P, P], F32, st)
        colGB = sb("colGB", [P, NB, 96], F32, st)
        stA = sb("stA", [P, HP, DV], F32, st)
        stB = sb("stB", [P, HB, DV], F32, st)
        tailE = sb("tailE", [P, QKV, TAIL], F32, st)
        dq = sb("dq", [P, HP, 4, P], F32, st)
        raw_at = ExitStack()
        rawE = sb("rawE", [P, 2, CW - 1 + TOK], F32, raw_at)
        raw_at.close()
        gG = sb("gG", [P, HP, TOK], F32, st)
        st.close()
        OX, OY, OQ, OK, OV = 0, KR, 2 * KR, 2 * KR + KC, 2 * KR + 2 * KC
        st = ExitStack()
        oO = sb("oO", [P, O_TILES, TOK], F32R, st)
        st.close()
        st = ExitStack()
        prO = sb("prO", [P, O_TILES, TOK], F32, st)
        tailO = sb("tailO", [P, KR, TAIL], F32, st)
        wrg = sb("wrg", [P, 2, KR, P], F32, st)
        cc = sb("cc", [P, 4, KR], F32, st)
        after = sb("after", [P, P], F32, st)
        before = sb("before", [P, P], F32, st)
        sbb = sb("sbb", [P, 2, HC], F32, st)
        ptab = sb("ptab", [1, TS * PAGES], I32, st)
        rg_at = ExitStack()
        rawO = sb("rawO", [P, 2, CW - 1 + TOK], F32, rg_at)
        rgR = sb("rgR", [P, KR, TOK], F32, rg_at)
        rgI = sb("rgI", [P, KR, TOK], F32, rg_at)
        rgA = sb("rgA", [P, KR, TOK], F32, rg_at)
        rgT = sb("rgT", [P, KR, TOK], F32, rg_at)
        rg_at.close()
        vtok = sb("vtok", [P, NB, WC], F32, st)
        ktok = sb("ktok", [P, NB, WC], F32, st)
        rowS = sb("rowS", [TS, 3, WC], F32, st)
        rowX = sb("rowX", [TAIL, 2, KR * P], F32, st)
        pages = sb("pages", [P, 4, PAGES, WC], F32, st)
        kq = sb("kq", [P, WC], F32, st)
        smS = sb("smS", [P, 3, PAGES, TS, HC], F32, st)
        st.close()
        shared.close()
        st = ExitStack()
        skL = sb("skL", [P, 2, SCORES], F32, st)
        skX = sb("skX", [P, 2, SCORES], F32, st)
        skY = sb("skY", [P, 2, SCORES], F32, st)
        skR = sb("skR", [P, TP - P + TP - 2 * P], F32, st)
        st.close()
        st = ExitStack()
        dif = sb("dif", [P, HB, P], F32, st)
        EG = sb("EG", [P, HB, P], F32, st)
        QKr = sb("QKr", [P, HB, P], F32, st)
        Lt = sb("Lt", [P, HB, P], F32, st)
        DT = sb("DT", [P, HB, P], F32, st)
        Dm = sb("Dm", [P, HB, P], F32, st)
        T1 = sb("T1", [P, HB, P], F32, st)
        qgB = sb("qgB", [P, HB, P], F32, st)
        kbg = sb("kbg", [P, HB, P], F32, st)
        kdB = sb("kdB", [P, HB, P], F32, st)
        vbB = sb("vbB", [P, HB, P], F32, st)
        nWT = sb("nWT", [P, HB, P], F32, st)
        colS = sb("colS", [P, 4, HB], F32, st)
        eA = sb("eA", [P, HP, P], F32, st)
        qgA = sb("qgA", [P, HP, P], F32, st)
        kdA = sb("kdA", [P, HP, P], F32, st)
        st.close()
        st = ExitStack()
        dkA = sb("dkA", [P, HP, P], F32, st)
        kdtA = sb("kdtA", [P, HP, P], F32, st)
        vtA = sb("vtA", [P, HA, P], F32, st)
        attT = sb("attT", [P, 2, HP, P], F32, st)
        st.close()
        st = ExitStack()
        egS = sb("egS", [P, HB, TS], F32, st)
        beS = sb("beS", [P, HB, TS], F32, st)
        vnS = sb("vnS", [P, HB, TS], F32, st)
        eaS = sb("eaS", [P, HP, TS], F32, st)
        vnR = sb("vnR", [HB * TS, DV], F32, st)
        vaR = sb("vaR", [TS, HA, DV], F32, st)
        kvS = sb("kvS", [P, 4, DV], F32, st)
        st.close()

        x_loaded, p_loaded, s_loaded = sem("x_loaded"), sem("p_loaded"), sem("s_loaded")
        consts = sem("consts")
        setup_t, prm_ready, hist_ready = sem("setup_t"), sem("prm_ready"), sem("hist_ready")
        w_loaded = [sem(f"w_loaded{n}") for n in range(STAGE_SLOTS)]
        hi_ready, lo_ready, unit_done = sem("hi_ready"), sem("lo_ready"), sem("unit_done")
        x_ready, sq_ready, ssum_zero, ssum_added = sem("x_ready"), sem("sq_ready"), sem("ssum_zero"), sem("ssum_added")
        norm_sum, ln_ready, rstd_ready = sem("norm_sum"), sem("ln_ready"), sem("rstd_ready")
        h_hi, h_lo = sem("h_hi"), sem("h_lo")
        gate_read, gate_ready, up_read, prod_ready, act_hi, act_lo = (
            sem(n) for n in "gate_read gate_ready up_read prod_ready act_hi act_lo".split())
        y_ready, y_t, y_row, stored = sem("y_ready"), sem("y_t"), sem("y_row"), sem("stored")

        e_free, e_loaded, e_consts = sem("e_free"), sem("e_loaded"), sem("e_consts")
        small_part = sem("small_part")
        pe_read, conv_step, silu_e = sem("pr_read_e"), sem("conv_step_e"), sem("silu_e")
        dve_chain, act_chain = sem("dve_chain"), sem("act_chain")
        gla_z, gla_sp, gla_r, gdn_sp, gates = (sem(n) for n in ("gla_z", "gla_sp", "gla_r", "gdn_sp", "gates"))
        l2_sq, l2_sum, l2_rn, l2_done = sem("l2_sq"), sem("l2_sum"), sem("l2_rn"), sem("l2_done")
        tail_t, tail_row, tail_stored, e_stored = sem("tail_t"), sem("tail_row"), sem("tail_stored"), sem("e_stored")
        col_t, col_ready = sem("col_t"), sem("col_ready")
        (ga_exp, ga_dif, ga_fac, ga_fac2, ga_att, ga_attc, ga_mask, ga_vt, ga_vtc, ga_kdt, ga_kdtc, ga_o, ga_oc,
         ga_s, ga_sc) = (sem("ga_" + n) for n in
            "exp dif fac fac2 att attc mask vt vtc kdt kdtc o oc s sc".split())
        (gb_bc, gb_eg, gb_dif, gb_rel, gb_kq, gb_qkr, gb_dt0, gb_kv, gb_ks, gb_vb, gb_d0, gb_d0c, gb_t1, gb_t1c,
         gb_dd, gb_ddc, gb_wt, gb_wtc, gb_vn, gb_vnc, gb_o, gb_oc, gb_s, gb_sc, gb_qg, gb_c1, gb_c2) = (
            sem("gb_" + n) for n in ("bc eg dif rel kq qkr dt0 kv ks vb d0 d0c t1 t1c dd ddc wt wtc vn vnc o oc "
                                     "s sc qg c1 c2").split())
        (sa_bc, sa_eg, sa_ks, sa_vn, sa_r, sa_rc, sa_b, sa_kv, sa_st, sa_o, sa_oc) = (
            sem("sa_" + n) for n in "bc eg ks vn r rc b kv st o oc".split())
        on_sq, on_sum, on_rn, on_y, o_hi, o_lo = (sem(n) for n in ("on_sq", "on_sum", "on_rn", "on_y", "o_hi", "o_lo"))

        o_consts, o_loaded, o_stored = sem("o_consts"), sem("o_loaded"), sem("o_stored")
        po_read, conv_step_o, xo_ready = sem("pr_read_o"), sem("conv_step_o"), sem("xo_ready")
        rg_c1, rg_c2, rg_z, rg_sig, rg_u, rg_a, rg_m, rg_mult, rg_gelu, rg_od = (
            sem("rg_" + n) for n in "c1 c2 z sig u a m mult gelu od".split())
        kv_t, row_t = sem("kv_t"), sem("row_t")
        v_rows = sem("v_rows")
        k_rows = sem("k_rows")
        sk_z, sk_read, sk_ln, sk_sp, sk_acc, sk_add, sk_w, sk_mask, sk_o, sk_oc = (
            sem("sk_" + n) for n in "z read ln sp acc add w mask o oc".split())
        page_loaded = [sem(f"page_loaded{n}") for n in range(4)]
        sm_q, sm_kq, sm_z, sm_ln, sm_sp, sm_acc, sm_w, sm_pv, sm_oc = (
            sem("sm_" + n) for n in "q kq z ln sp acc w pv oc".split())

        block = ctx.enter_context(nc.Block())

        def loads(b, per, t, q):
            return 16 * ((b + q) // STAGE_SLOTS + 1 + per // STAGE_SLOTS * t)

        @block.sync
        def _(sp):
            def unit_free(u):
                sp.wait_ge(hi_ready, u - STAGE_SLOTS + 1)
                sp.wait_ge(lo_ready, u - STAGE_SLOTS + 1)

            def load(s, src, tiles=UNIT):
                slot = s % STAGE_SLOTS
                dst = stage[:, slot, 0:tiles * P].rearrange("p (k n) -> p k n", n=P)
                sp.dma_start(dst, src).then_inc(w_loaded[slot], 16)

            def tiled(w):
                return w.rearrange("(k p) n -> p k n", p=P)

            def ffn_in(f):
                b = FIRST[f"in{f}"]
                wg, wu = tiled(i["ffn_w_gate"][f // 2, f % 2]), tiled(i["ffn_w_up"][f // 2, f % 2])

                def body(t):
                    for q in range(4):
                        if not (f == 0 and isinstance(t, int) and t == 0 and q < STAGE_SLOTS):
                            unit_free(b + 4 * t + q)
                        load(b + q, (wu if q % 2 else wg)[:, :, bass.ds((2 * t + q // 2) * P, P)])

                if f == 0:
                    body(0)
                loop(sp, 1 if f == 0 else 0, KF // 2, body)

            def ffn_down(f):
                b = FIRST[f"down{f}"]
                wd = tiled(i["ffn_w_down"][f // 2, f % 2])

                def body(t):
                    for q in range(4 * PARTS):
                        unit_free(b + 4 * PARTS * t + q)
                        k = q % PARTS * UNIT
                        n = min(UNIT, KF - k)
                        load(b + q, wd[:, k:k + n, bass.ds((4 * t + q // PARTS) * P, P)], n)
                loop(sp, 0, KD // 4, body)

            def tiles4(b, w, column, first, last):
                def body(t):
                    for q in range(4):
                        unit_free(b + 4 * t + q)
                        load(b + q, w[:, :, bass.ds((4 * (t - first) + q) * P + column, P)])
                loop(sp, first, last, body)

            def mix_e():
                b, w = FIRST["mix_e0"], tiled(i["w_in_e"][0])
                qk, v = HA * DKA, HA * DV
                la = 2 * qk + 2 * v
                qkv = la + RANK
                ab = qkv + (QKV + HB) * P
                unit_free(b)
                slot = b % STAGE_SLOTS
                dst = stage[:, slot, :].rearrange("p (k n) -> p k n", n=P)
                sp.dma_start(dst[:, :, 0:RANK], w[:, :, la:la + RANK]).then_inc(small_part, 16)
                sp.dma_start(dst[:, :, 32:32 + HB], w[:, :, ab:ab + HB]).then_inc(small_part, 16)
                sp.wait_ge(small_part, 32)
                sp.dma_start(dst[:, :, 64:64 + HB], w[:, :, ab + HB:ab + 2 * HB]).then_inc(w_loaded[slot], 16)
                tiles4(b + 1, w, qkv, 0, 3)
                tiles4(b + 1, w, 0, 3, 6)
                tiles4(b + 1, w, qkv + QKV * P, 6, 7)

            for name, f in STAGES:
                if name == "ffn":
                    ffn_in(f)
                    ffn_down(f)
                elif name == "mix_e":
                    mix_e()
                    tiles4(FIRST["out_e0"], tiled(i["w_out_e"][0]), 0, 0, KD // 4)
                elif name == "mix_o":
                    b, w = FIRST["mix_o0"], tiled(i["w_in_o"][0])
                    tiles4(b, w, 3 * WC, 0, 2 * KR // 4)
                    tiles4(b, w, 0, 2 * KR // 4, O_TILES // 4)
                    tiles4(FIRST["out_o0"], tiled(i["w_out_o"][0]), 0, 0, KD // 4)

        @block.gpsimd
        def _(pool):
            stores = 0

            def store(dst, src):
                nonlocal stores
                stores += 1
                pool.dma_start(dst, src).then_inc(stored, 16)

            pool.memset(ones[:], 1.0).then_inc(consts, 1)
            pool.memset(ident[:], 1.0).then_inc(consts, 1)
            pool.wait_ge(consts, 2)
            pool.affine_select(out=ident[:], in_=ident[:], compare_op=ALU.is_equal, fill=0.0, base=0,
                               pattern=[[-1, P]], channel_multiplier=1).then_inc(consts, 1)

            def mix_e():
                def select(m, op, base, pattern, mult):
                    pool.wait_ge(e_consts, select.n)
                    pool.affine_select(out=m, in_=m, compare_op=op, fill=0.0, base=base, pattern=pattern,
                                       channel_multiplier=mult).then_inc(e_consts, 1)
                    select.n += 1

                pool.wait_ge(unit_done, FIRST["mix_e0"])
                for par in range(2):
                    src = i["state_gla"][0].rearrange("b (h q) k v -> q k (b h) v", q=2)[par]
                    pool.dma_start(stA_s[par * DKA:(par + 1) * DKA, :, :, :].rearrange("p b h v -> p (b h) v"), src)\
                        .then_inc(e_loaded, 16)
                pool.dma_start(stB_s[:].rearrange("p b h v -> p (b h) v"),
                               i["state_gdn"][0].rearrange("b h k v -> k (b h) v")).then_inc(e_loaded, 16)
                pool.dma_start(wgate[:], i["gla_w_gate"][0]).then_inc(e_loaded, 16)
                pool.dma_start(gdnp[32:32 + HB, 0:1], i["gdn_dt_bias"].rearrange("a h -> h a")).then_inc(e_loaded, 16)
                pool.dma_start(gdnp[32:32 + HB, 1:2], i["gdn_a_log"].rearrange("a h -> h a")).then_inc(e_loaded, 16)
                pool.memset(masks[:], 0.0).then_inc(e_consts, 1)
                pool.memset(keep[:], 1.0).then_inc(e_consts, 1)
                pool.memset(strict[:], 1.0).then_inc(e_consts, 1)
                pool.memset(stA[:], 0.0).then_inc(e_consts, 1)
                pool.memset(stB[:], 0.0).then_inc(e_consts, 1)
                pool.wait_ge(e_consts, 5)
                for l in range(7):
                    half = masks[:, l, :].rearrange("p (n a b) -> p n a b", a=2, b=1 << l)
                    pool.memset(half[:, :, 1 if l == 0 else 0, :], 1.0).then_inc(e_consts, 1)
                select.n = 12
                select(masks[:, 0, :].rearrange("p (n a) -> p n a", a=2)[:, :, 1], ALU.is_equal, 0, [[-2, P // 2]], 1)
                for l in range(1, 7):
                    b = 1 << l
                    half = masks[:, l, :].rearrange("p (n a b) -> p n a b", a=2, b=b)[:, :, 0, :]
                    select(half, ALU.is_ge, -b, [[-2 * b, P // (2 * b)], [0, b]], 1)
                    select(half, ALU.is_ge, 2 * b - 1, [[2 * b, P // (2 * b)], [0, b]], -1)
                select(keep[:], ALU.is_ge, 0, [[1, P]], -1)
                select(strict[:], ALU.is_gt, 0, [[1, P]], -1)
                for c in range(NB):
                    pool.wait_ge(ga_attc, c + 1)
                    a = attT[:].rearrange("p a b t -> p (a b) t")
                    pool.affine_select(out=a, in_=a, compare_op=ALU.is_ge, fill=0.0, base=0,
                                       pattern=[[0, HA], [1, P]], channel_multiplier=-1).then_inc(ga_mask, 1)

                def save(dst, src):
                    pool.dma_start(dst, src).then_inc(e_stored, 16)

                pool.wait_ge(tail_row, 3)
                tail = tmp[0:TAIL, :, :].rearrange("p a b -> p (a b)")[:, 0:QKV * P]
                pool.dma_start(o["gcv_p"][0, 0], tail[0:CW - 1, :]).then_inc(tail_stored, 16)
                pool.dma_start(o["gcv_s"][0, :, CW - 2, :], tail[CW - 1:TAIL, :]).then_inc(tail_stored, 16)
                save(o["gcv_s"][0, :, 0:CW - 2, :], i["state_gdn_conv"][0, :, 1:CW - 1, :])
                pool.wait_ge(ga_sc, NB)
                for par in range(2):
                    save(o["gla_p"][0, 0].rearrange("(h q) k v -> q k h v", q=2)[par], stA[par * DKA:(par + 1) * DKA, :, :])
                pool.wait_ge(gb_sc, NB)
                save(o["gdn_p"][0, 0].rearrange("h k v -> k h v"), stB[:])
                pool.wait_ge(sa_st, HP * TS + HB * TS)
                for par in range(2):
                    save(o["gla_s"][0].rearrange("b (h q) k v -> q k (b h) v", q=2)[par],
                         stA_s[par * DKA:(par + 1) * DKA, :, :, :].rearrange("p b h v -> p (b h) v"))
                save(o["gdn_s"][0].rearrange("b h k v -> k (b h) v"), stB_s[:].rearrange("p b h v -> p (b h) v"))

            def mix_o():
                pool.wait_ge(unit_done, FIRST["mix_o0"])
                pool.memset(wrg[:], 0.0).then_inc(o_consts, 1)
                pool.memset(after[:], 1.0).then_inc(o_consts, 1)
                pool.memset(before[:], 1.0).then_inc(o_consts, 1)
                pool.dma_start(sbb[:, 0, :], i["sb_bias"][0:1, :].to_broadcast([P, HC])).then_inc(o_loaded, 16)
                pool.dma_start(ptab[:], i["page_table"].rearrange("(x b) p -> x (b p)", x=1)).then_inc(o_loaded, 16)
                pool.wait_ge(o_consts, 3)
                for n, w in enumerate(("rg_w_a", "rg_w_x")):
                    for q in range(2):
                        src = i[w][0].rearrange("(m q) a b -> q a m b", q=2)[q]
                        half = slice(q * (P // 2), (q + 1) * (P // 2))
                        pool.dma_start(wrg[half, n, :, half], src).then_inc(o_loaded, 16)
                pool.affine_select(out=after[:], in_=after[:], compare_op=ALU.is_gt, fill=0.0, base=0,
                                   pattern=[[-1, P]], channel_multiplier=1).then_inc(o_consts, 1)
                pool.affine_select(out=before[:], in_=before[:], compare_op=ALU.is_gt, fill=0.0, base=0,
                                   pattern=[[1, P]], channel_multiplier=-1).then_inc(o_consts, 1)

                def load_pages(g):
                    cache = i["cache_sb_v" if g >= TS else "cache_sb_k"]
                    for p in range(PAGES):
                        at = g % TS * PAGES + p
                        page = nc.values_load(ptab[0:1, at:at + 1], engines=[mybir.EngineType.Pool], min_val=0,
                                              max_val=POOL - 1,
                                              skip_runtime_bounds_check_because="the table names pages of the pool")
                        pool.dma_start(pages[:, g % 4, p, :],
                                       cache[0, bass.ds(page, 1)].rearrange("a t h d -> t (a h d)"))\
                            .then_inc(page_loaded[g % 4], 16)

                def save(dst, src):
                    pool.dma_start(dst, src).then_inc(o_stored, 16)

                pool.wait_ge(o_loaded, 96)
                pool.wait_ge(rg_od, KR)
                for g in range(4):
                    load_pages(g)
                save(o["rgc_s"][0, :, 0:CW - 2, :], i["state_rg_conv"][0, :, 1:CW - 1, :])
                pool.wait_ge(v_rows, NB)
                save(o["sbv_p"][0, 0].rearrange("(c p) h d -> p c (h d)", p=P), vtok[:])
                pool.wait_ge(k_rows, NB)
                save(o["sbk_p"][0, 0].rearrange("(c p) h d -> p c (h d)", p=P), ktok[:])
                pool.wait_ge(v_rows, NB + 3)
                save(o["sbk_s"][0, :, 0].rearrange("b h d -> b (h d)"), rowS[:, 1, :])
                save(o["sbv_s"][0, :, 0].rearrange("b h d -> b (h d)"), rowS[:, 2, :])
                pool.wait_ge(k_rows, NB + 2)
                save(o["rgh_p"][0], rowX[0:1, 0, :])
                save(o["rgh_s"][0], rowX[1:1 + TS, 0, :])
                save(o["rgc_p"][0, 0], rowX[0:CW - 1, 1, :])
                save(o["rgc_s"][0, :, CW - 2, :], rowX[CW - 1:TAIL, 1, :])
                for g in range(4, 2 * TS):
                    if g < TS + 4:
                        pool.wait_ge(sm_kq, g - 3)
                    else:
                        pool.wait_ge(sm_pv, g - 3 - TS)
                    load_pages(g)

            for name, f in STAGES:
                if name == "mix_e":
                    mix_e()
                elif name == "mix_o":
                    mix_o()
            pool.wait_ge(y_row, KD + 2)
            for b in range(NB):
                store(o["y_prompt"][0, b * P:(b + 1) * P, :], yrow[:, b, :])
            store(o["y_sample"][:, 0, :], ysrow[:])
            pool.wait_ge(stored, 16 * stores)
            if ("mix_e", 0) in STAGES:
                pool.wait_ge(e_stored, 16 * E_STORES)
                pool.wait_ge(tail_stored, 32)
            if ("mix_o", 0) in STAGES:
                pool.wait_ge(o_stored, 16 * O_STORES)

        @block.scalar
        def _(act):
            def split(b, per, t, q):
                s = b + q
                act.wait_ge(w_loaded[s % STAGE_SLOTS], loads(b, per, t, q))
                if not isinstance(t, int) or s + per * t >= SPLIT_SLOTS:
                    act.wait_ge(unit_done, s + per * t - SPLIT_SLOTS + 1)
                act.activation(whi[:, s % SPLIT_SLOTS, :], stage[:, s % STAGE_SLOTS, :], ACT.Copy)\
                   .then_inc(hi_ready, 1)

            def split_ahead(b, per, t, q):
                if not isinstance(t, int) or b + per * t + q + LOOKAHEAD < UNITS:
                    split(b, per, t, q + LOOKAHEAD)

            def square(k, m, slot):
                act.wait_ge(x_ready, KD * k + m + 1)
                if not isinstance(m, int) or m >= 2 or k:
                    act.wait_ge(ssum_added, KD * k + m - 1)
                act.activation(tmp[:, slot, :], tile(xT, m), ACT.Square).then_inc(sq_ready, 1)
                if k < LAST_NORM:
                    act.activation(tile(hh, m), tile(xT, m), ACT.Copy, scale=prm[:, bass.ds(m + NORM_PRM[k], 1)])\
                       .then_inc(h_hi, 1)

            def norm(k):
                act.preload_act_table(ACT.Ln)
                act.wait_ge(norm_sum, k + 1)
                act.activation(two(rstd[:]), pair(3), ACT.Ln, scale=1.0 / DM, bias=EPS)\
                   .then_inc(ln_ready, 1)
                act.wait_ge(ln_ready, k + 1)
                act.activation(rstd[:], rstd[:], ACT.Exp, scale=-0.5).then_inc(rstd_ready, 1)
                if k < LAST_NORM and STAGES[k][0] != "mix_o":
                    act.preload_act_table(ACT.Silu)

            def ffn_in(s, f):
                b = FIRST[f"in{f}"]
                before_it = STAGES[s - 1][0] if s else None
                if before_it == "mix_e":
                    act.wait_ge(e_stored, 16 * E_STORES)
                elif before_it == "mix_o":
                    act.wait_ge(o_stored, 16 * O_STORES)

                def body(t):
                    for a in range(2):
                        n = KF * f + 2 * t + a
                        split_ahead(b, 4, t, 2 * a)
                        act.wait_ge(gate_read, n + 1)
                        act.activation(tmp[:, a, :], tmp[:, a, :], ACT.Silu).then_inc(gate_ready, 1)
                        split_ahead(b, 4, t, 2 * a + 1)
                        act.wait_ge(prod_ready, n + 1)
                        act.activation(act_h[:, bass.ds(2 * t + a, 1), :].rearrange("p a b -> p (a b)"),
                                       tmp[:, 2 + a, :], ACT.Copy).then_inc(act_hi, 1)
                body(0)
                loop(act, 1, KF // 2, body)

            def ffn_down(s, f):
                b = FIRST[f"down{f}"]

                def body(t):
                    for a in range(4):
                        for c in range(PARTS):
                            split_ahead(b, 4 * PARTS, t, PARTS * a + c)
                        square(s + 1, 4 * t + a, a % 2)
                if s + 1 == LAST_NORM:
                    for t in range(KD // 4):
                        body(t)
                else:
                    loop(act, 0, KD // 4, body)

            chain = [0]

            def link(ins):
                chain[0] += 1
                ins.then_inc(act_chain, 1)
                act.wait_ge(act_chain, chain[0])

            def out_proj(s, name):
                b = FIRST[name]

                def body(t):
                    for a in range(4):
                        split_ahead(b, 4, t, a)
                        square(s + 1, 4 * t + a, a % 2)
                loop(act, 0, KD // 4, body)

            def project_e():
                b = FIRST["mix_e0"]
                split_ahead(b, 4, 0, 0)

                def silu(n, slot):
                    act.wait_ge(conv_step, 8 * (n + 1))
                    act.activation(prE[:, bass.ds(n, 1), :].rearrange("p a b -> p (a b)"), tmp[:, slot, :], ACT.Silu)\
                       .then_inc(silu_e, 1)

                def body(t):
                    for q in range(4):
                        n = 4 * t + q
                        first = isinstance(t, int) and t == 0
                        split_ahead(b + 1, 4, t, q)
                        if not first or q:
                            silu(n - 1, (q + 1) % 2)
                body(0)
                loop(act, 1, QKV // 4, body)
                silu(QKV - 1, 1)
                for n in range(QKV, E_TILES):
                    split_ahead(b + 1, 4, 0, n)
                    if n >= AR:
                        act.wait_ge(pe_read, n + 2)
                        act.activation(prE[:, n, :], prE[:, n, :], ACT.Silu)

            def softplus_abs(dst, src, bias):
                link(act.activation(dst, src, ACT.Abs, bias=bias))
                link(act.activation(dst, dst, ACT.Exp, scale=-1.0))
                return act.activation(dst, dst, ACT.Ln, bias=1.0)

            def gates_e():
                act.wait_ge(pe_read, 1)
                act.activation(small[64:64 + HB, :], small[64:64 + HB, :], ACT.Sigmoid).then_inc(gates, 1)
                act.preload_act_table_set(LN_EXP)
                act.wait_ge(e_loaded, 96)
                r = slice(32, 32 + HB)
                softplus_abs(rstd[r, :], small[r, :], gdnp[r, 0:1]).then_inc(gdn_sp, 1)
                act.activation(gdnp[r, 2:3], gdnp[r, 1:2], ACT.Exp).then_inc(gdn_sp, 1)
                act.wait_ge(gla_z, 1)
                for h in range(HP):
                    softplus_abs(two(tmp[:, h, :]), pair(h), col("gla_b_gate", h)).then_inc(gla_sp, 1)

            def unit_norm(n, src, sq, total, rn, scale, bias):
                if n >= 2:
                    act.wait_ge(total, n - 1)
                act.activation(tmp[:, n % 2, :], src, ACT.Square).then_inc(sq, 1)

            def unit_rn(n, total, done, rn, scale):
                act.wait_ge(total, n + 1)
                if n >= 2:
                    act.wait_ge(done, n - 1)
                link(act.activation(two(tmp[:, 2 + n % 2, :]), pair(n % 2), ACT.Ln, scale=scale, bias=EPS))
                act.activation(tmp[:, 2 + n % 2, :], tmp[:, 2 + n % 2, :], ACT.Exp, scale=-0.5).then_inc(rn, 1)

            def l2_e():
                act.wait_ge(silu_e, QKV)
                act.wait_ge(gla_r, 2 * HP)
                for n in range(2 * HB + 1):
                    if n < 2 * HB:
                        unit_norm(n, prE[:, n, :], l2_sq, l2_sum, l2_rn, 1.0, EPS)
                    if n:
                        unit_rn(n - 1, l2_sum, l2_done, l2_rn, 1.0)

            def gla(c):
                t = slice(c * P, (c + 1) * P)
                if c:
                    act.wait_ge(ga_sc, c)
                act.activation(eA[:], gG[:, :, t], ACT.Exp, scale=1.0 / GLA_TAU).then_inc(ga_exp, 1)
                act.wait_ge(ga_dif, c + 1)
                act.activation(dq[:], dq[:], ACT.Exp, scale=1.0 / GLA_TAU)
                act.activation(dkA[:], dkA[:], ACT.Exp, scale=-1.0 / GLA_TAU)
                act.activation(kdA[:], kdA[:], ACT.Exp, scale=-1.0 / GLA_TAU).then_inc(ga_fac, 1)
                act.wait_ge(ga_vt, c + 1)
                act.activation(vtA[:].rearrange("p a b -> p (a b)"), banks(2, 1), ACT.Copy).then_inc(ga_vtc, 1)
                act.wait_ge(ga_att, c + 1)
                act.activation(attT[:].rearrange("p a b t -> p a (b t)"), PS[:, 0:2, 0:HP * P], ACT.Copy)\
                   .then_inc(ga_attc, 1)
                act.wait_ge(ga_kdt, c + 1)
                act.activation(kdtA[:].rearrange("p a b -> p (a b)"), banks(3, 1)[:, 0:HP * P], ACT.Copy)\
                   .then_inc(ga_kdtc, 1)
                act.wait_ge(ga_o, c + 1)
                act.activation(prE[:, AV:AV + HA, t].rearrange("p (h q) t -> p q h t", q=2),
                               PS[:, 4:6, 0:HP * P].rearrange("p q (h t) -> p q h t", h=HP), ACT.Copy)\
                   .then_inc(ga_oc, 1)

            def gdn(c):
                t = slice(c * P, (c + 1) * P)
                act.wait_ge(gb_bc, c + 1)
                if c:
                    act.wait_ge(gb_sc, c)
                act.activation(EG[:].rearrange("p a b -> p (a b)"), banks(0, 1), ACT.Exp).then_inc(gb_eg, 1)
                act.activation(colS[:, 0, :], colGB[:, c, 32:32 + HB], ACT.Exp)
                act.wait_ge(gb_dif, c + 1)
                act.activation(colS[:, 3, :], colS[:, 2, :], ACT.Exp).then_inc(gb_c1, 1)
                act.activation(dif[:], dif[:], ACT.Exp).then_inc(gb_rel, 1)
                act.wait_ge(gb_kv, c + 1)
                act.wait_ge(gb_c2, c + 1)
                act.wait_ge(gb_c1, c + 1)
                for h in range(HB):
                    kt = banks(4, 1)[:, h * P:(h + 1) * P]
                    act.activation(kbg[:, h, :], kt, ACT.Copy, scale=colS[:, 1, h:h + 1])
                    last = act.activation(kdB[:, h, :], kt, ACT.Copy, scale=colS[:, 3, h:h + 1])
                last.then_inc(gb_ks, 1)
                act.wait_ge(gb_d0, c + 1)
                act.activation(Dm[:].rearrange("p a b -> p (a b)"), banks(3, 1), ACT.Copy).then_inc(gb_d0c, 1)
                act.wait_ge(gb_wt, c + 1)
                act.activation(nWT[:].rearrange("p a b -> p (a b)"), banks(3, 1), ACT.Copy, scale=-1.0)\
                   .then_inc(gb_wtc, 1)
                act.wait_ge(gb_vn, c + 1)
                act.activation(T1[:].rearrange("p a b -> p (a b)"), banks(7, 1), ACT.Copy).then_inc(gb_vnc, 1)
                act.wait_ge(gb_o, c + 1)
                act.activation(prE[:, BV:BV + HB, t], banks(4, 1).rearrange("p (h t) -> p h t", h=HB), ACT.Copy)\
                   .then_inc(gb_oc, 1)

            def samples_e():
                s = slice(TP, TOK)
                act.wait_ge(sa_bc, 1)
                act.activation(egS[:], banks(6, 1).rearrange("p (h t) -> p h t", h=HB)[:, :, P - TS:P], ACT.Exp)
                act.activation(eaS[:], gG[:, :, s], ACT.Exp, scale=1.0 / GLA_TAU).then_inc(sa_eg, 1)
                act.wait_ge(sa_r, 1)
                act.activation(vaR[:].rearrange("p a b -> p (a b)"), banks(1, 1)[0:TS, :], ACT.Copy).then_inc(sa_rc, 1)
                act.wait_ge(sa_r, 2)
                act.activation(vnR[:], banks(5, 1)[0:HB * TS, 0:DV], ACT.Copy).then_inc(sa_rc, 1)
                n = 0
                for b in range(TS):
                    act.wait_ge(sa_b, b // 2 + 1)
                    for h in range(HP):
                        if n >= 4:
                            act.wait_ge(sa_st, n - 3)
                        act.activation(kvS[:, n % 4, :], banks(2 + b // 2 % 2, 1)[:, (b % 2 * HP + h) * P:(b % 2 * HP + h + 1) * P],
                                       ACT.Copy, scale=prE[:, AK + h, TP + b:TP + b + 1]).then_inc(sa_kv, 1)
                        n += 1
                for r in range(HB * TS):
                    h, b = r // TS, r % TS
                    act.wait_ge(sa_b, TS // 2 + r // 4 + 1)
                    act.wait_ge(sa_st, n - 3)
                    act.activation(kvS[:, n % 4, :], banks(2 + r // 4 % 2, 1)[:, r % 4 * P:(r % 4 + 1) * P],
                                   ACT.Copy, scale=prE[:, BK + h, TP + b:TP + b + 1]).then_inc(sa_kv, 1)
                    n += 1
                act.wait_ge(sa_o, 1)
                ga = PS[:, 6:8, 0:HP * TS].rearrange("p a (h b) -> p a h b", h=HP)
                for par in range(2):
                    act.activation(prE[:, AV + par:AV + HA:2, s], ga[:, par], ACT.Copy).then_inc(sa_oc, 1)
                act.wait_ge(sa_o, 2)
                act.activation(prE[:, BV:BV + HB, s], banks(4, 1)[:, 0:HB * TS].rearrange("p (h b) -> p h b", h=HB),
                               ACT.Copy).then_inc(sa_oc, 1)

            def out_norm_e():
                act.wait_ge(tail_stored, 32)
                act.wait_ge(sa_oc, 3)
                act.wait_ge(ga_oc, NB)
                act.wait_ge(gb_oc, NB)
                for n in range(HA + HB + 2):
                    if n < HA + HB:
                        unit_norm(n, prE[:, AV + n if n < HA else BV + n - HA, :], on_sq, on_sum, on_rn, 1.0 / DV, EPS)
                    if 1 <= n <= HA + HB:
                        unit_rn(n - 1, on_sum, on_y, on_rn, 1.0 / DV)
                    if n >= 2:
                        m = n - 2
                        act.wait_ge(on_y, m + 1)
                        act.activation(oE[:, AR + m, :], prE[:, AV + m if m < HA else BV + m - HA, :], ACT.Copy)\
                           .then_inc(o_hi, 1)

            def project_o():
                b = FIRST["mix_o0"]
                for n in range(O_TILES):
                    split_ahead(b, 4, 0, n)
                    if 1 <= n <= KR:
                        act.wait_ge(conv_step_o, 8 * n)
                        act.activation(prO[:, OX + n - 1, :], tmp[:, (n - 1) % 2, :], ACT.Identity,
                                       bias=col("rg_conv_b", n - 1)).then_inc(xo_ready, 1)
                    if n == KR + 1:
                        softplus_abs(cc[:, 2, :], prm[:, PRM["rg_lambda"]:PRM["rg_lambda"] + KR], 0.0)\
                            .then_inc(rg_c1, 1)
                    if n >= 2 * KR and (n - 2 * KR) % 3 == 0:
                        rg_gates((n - 2 * KR) // 3)
                    if n >= 2 * KR and (n - 2 * KR) % 3 == 1:
                        rg_mult_root((n - 2 * KR) // 3)

            def rg_gates(m):
                act.wait_ge(rg_z, m + 1)
                act.activation(two(rgR[:, m, :]), pair(2), ACT.Sigmoid, bias=col("rg_b_a", m)).then_inc(rg_sig, 1)
                act.activation(two(rgI[:, m, :]), pair(3), ACT.Sigmoid, bias=col("rg_b_x", m)).then_inc(rg_sig, 1)
                act.wait_ge(rg_u, m + 1)
                act.activation(tmp[:, 2 + m % 2, :], tmp[:, 2 + m % 2, :], ACT.Tanh, scale=(2 / 3.141592653589793) ** 0.5)\
                   .then_inc(rg_a, 1)
                act.wait_ge(rg_sig, 2 * m + 1)
                act.wait_ge(rg_c2, 2)
                act.activation(rgT[:, m, :], rgR[:, m, :], ACT.Tanh, scale=cc[:, 1, m:m + 1]).then_inc(rg_a, 1)
                act.activation(rgA[:, m, :], rgR[:, m, :], ACT.Exp, scale=cc[:, 0, m:m + 1]).then_inc(rg_a, 1)

            def rg_mult_root(m):
                act.preload_act_table_set(LN_EXP)
                act.wait_ge(rg_m, m + 1)
                link(act.activation(rgR[:, m, :], rgR[:, m, :], ACT.Ln, bias=1e-37))
                act.activation(rgR[:, m, :], rgR[:, m, :], ACT.Exp, scale=0.5).then_inc(rg_mult, 1)

            def rows_o():
                act.wait_ge(rg_od, KR)
                for n in range(NB):
                    act.wait_ge(kv_t, NB + n + 1)
                    act.activation(ktok[:, n, :], banks(4 + n, 1), ACT.Copy).then_inc(k_rows, 1)
                for n, rows in enumerate((1 + TS, TAIL)):
                    act.wait_ge(row_t, 4 + n)
                    act.activation(rowX[0:rows, n, :], banks(3 + n, 1)[0:rows, :], ACT.Copy).then_inc(k_rows, 1)

            def stick():
                z = banks(0, 3)[:, 0:SCORES]
                act.wait_ge(rg_c2, 2)
                for h in range(HC + 2):
                    if h < HC:
                        act.wait_ge(sk_z, h + 1)
                        if h >= 2:
                            act.wait_ge(sk_o, h - 1)
                        act.activation(skL[:, h % 2, :], z, ACT.Abs, bias=sbb[:, 0, h:h + 1])
                        act.activation(skX[:, h % 2, :], z, ACT.Relu, bias=sbb[:, 0, h:h + 1])
                        act.activation(skY[:, h % 2, :], z, ACT.Relu, scale=-1.0, bias=sbb[:, 1, h:h + 1])\
                           .then_inc(sk_read, 1)
                        act.wait_ge(sk_read, h + 1)
                        link(act.activation(skL[:, h % 2, :], skL[:, h % 2, :], ACT.Exp, scale=-1.0))
                        act.activation(skL[:, h % 2, :], skL[:, h % 2, :], ACT.Ln, bias=1.0).then_inc(sk_ln, 1)
                    if 1 <= h <= HC:
                        act.wait_ge(sk_add, h)
                        a = (h - 1) % 2
                        act.activation(skY[:, a, :], skY[:, a, :], ACT.Exp, scale=-1.0).then_inc(sk_w, 1)
                    if h >= 2:
                        n = h - 2
                        r = slice(n % 2 * HDC, (n % 2 + 1) * HDC)
                        act.wait_ge(sk_o, n + 1)
                        act.activation(prO[r, OQ + n // 2, 0:TP], banks(6 + n % 2, 1)[r, :], ACT.Copy).then_inc(sk_oc, 1)

            def samples_o():
                def flat(n):
                    return smS[:, n].rearrange("p a b h -> p (a b h)")
                act.wait_ge(sm_z, 1)
                softplus_abs(flat(1), flat(0), 0.0).then_inc(sm_ln, 1)
                act.wait_ge(sm_z, 2)
                act.activation(flat(2), flat(2), ACT.Exp).then_inc(sm_w, 1)
                act.wait_ge(sm_pv, TS)
                for q in range(2):
                    r = slice(q * HDC, (q + 1) * HDC)
                    src = banks(2, 1)[r, 0:KC * TS * 2].rearrange("p (m b q) -> p m b q", m=KC, q=2)
                    act.activation(prO[r, OQ:OQ + KC, TP:TOK], src[:, :, :, q], ACT.Copy).then_inc(sm_oc, 1)
                act.wait_ge(sm_oc, 2)
                act.wait_ge(sk_oc, HC)
                act.wait_ge(rg_od, KR)
                for m in range(KC + KR):
                    act.activation(oO[:, OK + m if m < KC else OX + m - KC, :],
                                   prO[:, OQ + m if m < KC else OY + m - KC, :], ACT.Copy).then_inc(o_hi, 1)

            for b in range(NB):
                act.dma_start(xrow[:, b, :], i["x_prompt"][0, b * P:(b + 1) * P, :]).then_inc(x_loaded, 16)
            act.dma_start(xsrow[:], i["x_sample"][:, 0, :]).then_inc(x_loaded, 16)
            for dst, group, first in ((prow_a, ROWS_A, 0), (prow_b, ROWS_B, NA)):
                for name, n in group:
                    r = PRM[name] - first
                    act.dma_start(dst[r:r + n, :], rows(i[name])).then_inc(p_loaded, 16)
            act.dma_start(hrow_g[:], i["state_gdn_conv"][0].rearrange("b w n -> (b w) n")).then_inc(s_loaded, 16)
            act.dma_start(hrow_r[:], i["state_rg_conv"][0].rearrange("b w n -> (b w) n")).then_inc(s_loaded, 16)
            act.dma_start(hrow_0[:], i["state_rg_h"][0]).then_inc(s_loaded, 16)
            for u in range(LOOKAHEAD):
                split(u, 4, 0, 0)
            act.wait_ge(prm_ready, 1)
            for m in range(KD):
                square(0, m, m % 2)
            for s, (name, f) in enumerate(STAGES):
                norm(s)
                if name == "ffn":
                    ffn_in(s, f)
                    ffn_down(s, f)
                elif name == "mix_e":
                    project_e()
                    gates_e()
                    l2_e()
                    for c in range(NB):
                        gla(c)
                    for c in range(NB):
                        gdn(c)
                    samples_e()
                    out_norm_e()
                    out_proj(s, "out_e0")
                elif name == "mix_o":
                    project_o()
                    rows_o()
                    stick()
                    samples_o()
                    out_proj(s, "out_o0")
            norm(LAST_NORM)

        @block.vector
        def _(dve):
            def split(b, per, t, q):
                s = b + q
                slot = s % SPLIT_SLOTS
                dve.wait_ge(hi_ready, s + per * t + 1)
                if not isinstance(t, int) or s + per * t >= SPLIT_SLOTS:
                    dve.wait_ge(unit_done, s + per * t - SPLIT_SLOTS + 1)
                dve.tensor_tensor(wlo[:, slot, :], stage[:, s % STAGE_SLOTS, :], whi[:, slot, :].bitcast(F32),
                                  ALU.subtract).then_inc(lo_ready, 1)

            def split_ahead(b, per, t, q):
                if not isinstance(t, int) or b + per * t + q + LOOKAHEAD < UNITS:
                    split(b, per, t, q + LOOKAHEAD)

            def zero_sum(k):
                if k:
                    dve.wait_ge(norm_sum, k)
                dve.memset(ssum[:], 0.0).then_inc(ssum_zero, 1)

            def add_square(k, m, slot):
                dve.wait_ge(sq_ready, KD * k + m + 1)
                dve.wait_ge(ssum_zero, k + 1)
                if not isinstance(m, int) or m or k:
                    dve.wait_ge(ssum_added, KD * k + m)
                dve.tensor_tensor(ssum[:], ssum[:], tmp[:, slot, :], ALU.add).then_inc(ssum_added, 1)
                if k < LAST_NORM:
                    dve.wait_ge(h_hi, KD * k + m + 1)
                    dve.scalar_tensor_tensor(out=tile(hl, m), in0=tile(xT, m), scalar=prm[:, bass.ds(m + NORM_PRM[k], 1)],
                                             in1=tile(hh, m).bitcast(F32), op0=ALU.mult, op1=ALU.subtract)\
                       .then_inc(h_lo, 1)

            def last_norm():
                g = NORM_PRM[LAST_NORM]
                dve.wait_ge(rstd_ready, LAST_NORM + 1)
                for m in range(KD):
                    if m >= 4:
                        dve.wait_ge(y_t, m - 3)
                    dve.scalar_tensor_tensor(out=tmp[:, m % 4, :], in0=xT[:, m, :], scalar=prm[:, g + m:g + m + 1],
                                             in1=rstd[:], op0=ALU.mult, op1=ALU.mult).then_inc(y_ready, 1)
                    if m >= 3:
                        y_rows(m - 3)
                for m in range(KD - 3, KD):
                    y_rows(m)

            def take(dst, psum, scale=1.0):
                return dve.scalar_tensor_tensor(out=dst, in0=psum, scalar=scale, in1=two(rstd[:]), op0=ALU.mult,
                                                op1=ALU.mult)

            def y_rows(m):
                dve.wait_ge(y_t, m + 1)
                dve.tensor_copy(yrow[:, :, m * P:(m + 1) * P], banks(m % 4, 1).rearrange("p (b n) -> p b n", b=NB))\
                   .then_inc(y_row, 1)
                if m == KD - 1:
                    for a in range(2):
                        dve.tensor_copy(ysrow[:, a * 512:(a + 1) * 512], banks(4 + a, 1)[0:TS, :]).then_inc(y_row, 1)

            def ffn_in(s, f):
                b = FIRST[f"in{f}"]

                def body(t):
                    for a in range(2):
                        n = KF * f + 2 * t + a
                        first = isinstance(t, int) and t == 0
                        split_ahead(b, 4, t, 2 * a)
                        dve.wait_ge(unit_done, b + 4 * t + 2 * a + 1)
                        if first:
                            dve.wait_ge(rstd_ready, s + 1)
                            dve.wait_ge(ssum_added, KD * (s + 1))
                        else:
                            dve.wait_ge(prod_ready, n - 1)
                        take(two(tmp[:, a, :]), pair(2 * a)).then_inc(gate_read, 1)
                        split_ahead(b, 4, t, 2 * a + 1)
                        dve.wait_ge(unit_done, b + 4 * t + 2 * a + 2)
                        if not first or n >= 2:
                            dve.wait_ge(act_lo, n - 1)
                        take(two(tmp[:, 2 + a, :]), pair(2 * a + 1)).then_inc(up_read, 1)
                        dve.wait_ge(up_read, n + 1)
                        dve.wait_ge(gate_ready, n + 1)
                        dve.tensor_tensor(tmp[:, 2 + a, :], tmp[:, a, :], tmp[:, 2 + a, :], ALU.mult)\
                           .then_inc(prod_ready, 1)
                        dve.wait_ge(act_hi, n + 1)
                        dve.tensor_tensor(tile(act_l, 2 * t + a), tmp[:, 2 + a, :],
                                          tile(act_h, 2 * t + a).bitcast(F32), ALU.subtract).then_inc(act_lo, 1)
                    if first:
                        zero_sum(s + 1)
                body(0)
                loop(dve, 1, KF // 2, body)

            def update(s, m, done, psum, scale):
                dve.wait_ge(unit_done, done)
                x = xT[:, bass.ds(m, 1), :].rearrange("p a (b c) -> p (a b) c", b=2)
                dve.scalar_tensor_tensor(out=x, in0=psum, scalar=scale, in1=x, op0=ALU.mult, op1=ALU.add)\
                   .then_inc(x_ready, 1)

            def ffn_down(s, f):
                b = FIRST[f"down{f}"]

                def body(t):
                    for a in range(4):
                        for c in range(PARTS):
                            split_ahead(b, 4 * PARTS, t, PARTS * a + c)
                        update(s, 4 * t + a, b + 4 * PARTS * t + PARTS * (a + 1), pair(a), 0.5)
                        add_square(s + 1, 4 * t + a, a % 2)
                if s + 1 == LAST_NORM:
                    for t in range(KD // 4):
                        body(t)
                else:
                    loop(dve, 0, KD // 4, body)

            chain = [0]

            def link(ins):
                chain[0] += 1
                ins.then_inc(dve_chain, 1)
                dve.wait_ge(dve_chain, chain[0])

            def out_proj(s, name):
                b = FIRST[name]

                def body(t):
                    for a in range(4):
                        split_ahead(b, 4, t, a)
                        update(s, 4 * t + a, b + 4 * t + a + 1, pair(a), 1.0)
                        add_square(s + 1, 4 * t + a, a % 2)
                loop(dve, 0, KD // 4, body)

            def conv(n, slot, raw, hist, wcol, tail, done, step, per, step_n, cstep):
                def w(k):
                    return prm[:, bass.ds(wcol(k, n), 1)]
                y = tmp[:, slot, :]
                dve.wait_ge(done, step)
                dve.tensor_scalar(y, raw[:, slot, CW - 1:CW - 1 + TOK], w(CW - 1), None, ALU.mult).then_inc(cstep, 1)
                for k in range(CW - 1):
                    dve.wait_ge(cstep, step_n + (1 if k == 0 else 2 * k))
                    dve.scalar_tensor_tensor(out=y[:, 0:TP], in0=raw[:, slot, k:k + TP], scalar=w(k), in1=y[:, 0:TP],
                                             op0=ALU.mult, op1=ALU.add).then_inc(cstep, 1)
                    if k:
                        dve.wait_ge(cstep, step_n + 2 * k + 1)
                    past = hist[:, bass.ds(n, 1), :, k].rearrange("p a b -> p (a b)")
                    dve.scalar_tensor_tensor(out=y[:, TP:TOK], in0=past, scalar=w(k), in1=y[:, TP:TOK],
                                             op0=ALU.mult, op1=ALU.add).then_inc(cstep, 1)
                dve.tensor_copy(tail[:, bass.ds(n, 1), :].rearrange("p a b -> p (a b)"),
                                raw[:, slot, TP:TP + TAIL]).then_inc(cstep, 1)

            def project_e(s):
                b = FIRST["mix_e0"]
                split_ahead(b, 4, 0, 0)
                dve.memset(rawE[:, :, 0:CW - 1], 0.0).then_inc(e_free, 1)
                dve.wait_ge(e_free, 1)
                dve.wait_ge(unit_done, b + 1)
                dve.wait_ge(rstd_ready, s + 1)
                dve.scalar_tensor_tensor(out=two(small[:]), in0=pair(2)[0:96], scalar=1.0, in1=two(rstd[0:96, :]),
                                         op0=ALU.mult, op1=ALU.mult).then_inc(pe_read, 1)

                def body(t):
                    for q in range(4):
                        n = 4 * t + q
                        split_ahead(b + 1, 4, t, q)
                        dve.wait_ge(unit_done, b + 2 + 4 * t + q)
                        if isinstance(t, int) and t == 0 and q < 2:
                            dve.wait_ge(ssum_added, KD * (s + 1))
                        else:
                            dve.wait_ge(conv_step, 8 * (n - 1))
                            dve.wait_ge(silu_e, n - 1)
                        take(two(rawE[:, q % 2, CW - 1:CW - 1 + TOK]), pair(q)).then_inc(pe_read, 1)
                        conv(n, q % 2, rawE, histG, lambda k, n: PRM["gdn_conv_w"] + k * QKV + n, tailE,
                             pe_read, n + 2, None, 8 * n, conv_step)
                body(0)
                zero_sum(s + 1)
                loop(dve, 1, QKV // 4, body)
                for n in range(QKV, E_TILES):
                    split_ahead(b + 1, 4, 0, n)
                    dve.wait_ge(unit_done, b + 2 + n)
                    take(two(prE[:, n, :]), pair(n % 4), DKA ** -0.5 if n < AK else 1.0).then_inc(pe_read, 1)

            def gates_e():
                dve.wait_ge(e_loaded, 96)
                r = slice(32, 32 + HB)
                dve.wait_ge(pe_read, 1)
                dve.wait_ge(gdn_sp, 2)
                link(dve.tensor_scalar(small[r, :], small[r, :], gdnp[r, 0:1], 0.0, ALU.add, ALU.max))
                link(dve.tensor_tensor(rstd[r, :], rstd[r, :], small[r, :], ALU.add))
                link(dve.tensor_scalar(rstd[r, :], rstd[r, :], gdnp[r, 2:3], -1.0, ALU.mult, ALU.mult))
                for c in range(NB):
                    t = slice(c * P, (c + 1) * P)
                    dve.tensor_tensor_scan(small[r, t], ones[r, :], rstd[r, t], 0.0, ALU.mult, ALU.add)
                dve.tensor_copy(small[r, TP:TOK], rstd[r, TP:TOK]).then_inc(gates, 1)
                dve.wait_ge(silu_e, QKV)
                for h in range(HP):
                    dve.wait_ge(gla_sp, h + 1)
                    link(dve.tensor_scalar(two(tmp[:, 2 + h, :]), pair(h), col("gla_b_gate", h), 0.0, ALU.add, ALU.min))
                    dve.tensor_tensor(tmp[:, 2 + h, :], tmp[:, 2 + h, :], tmp[:, h, :], ALU.subtract).then_inc(gla_r, 1)
                    dve.wait_ge(gla_r, 2 * h + 1)
                    for c in range(NB):
                        t = slice(c * P, (c + 1) * P)
                        dve.tensor_tensor_scan(gG[:, h, t], ones[:], tmp[:, 2 + h, t], 0.0, ALU.mult, ALU.add)
                    dve.tensor_copy(gG[:, h, TP:TOK], tmp[:, 2 + h, TP:TOK]).then_inc(gla_r, 1)

            def l2_e():
                for n in range(2 * HB):
                    dve.wait_ge(l2_rn, n + 1)
                    dve.scalar_tensor_tensor(out=prE[:, n, :], in0=prE[:, n, :], scalar=P ** -0.5 if n < HB else 1.0,
                                             in1=tmp[:, 2 + n % 2, :], op0=ALU.mult, op1=ALU.mult).then_inc(l2_done, 1)
                dve.wait_ge(col_t, 1)
                dve.tensor_copy(colGB[:], banks(7, 1)[:, 0:NB * 96].rearrange("p (c r) -> p c r", c=NB))\
                   .then_inc(col_ready, 1)
                dve.wait_ge(tail_t, 1)
                dve.wait_ge(l2_done, 2 * HB)
                for n in range(3):
                    dve.tensor_copy(tmp[0:TAIL, :, :].rearrange("p a b -> p (a b)")[:, n * 512:(n + 1) * 512],
                                    banks(4 + n, 1)[0:TAIL, :]).then_inc(tail_row, 1)

            def gla(c):
                t = slice(c * P, (c + 1) * P)
                lim = CLAMP * GLA_TAU
                if c:
                    dve.wait_ge(ga_fac2, 4 * c)
                    dve.wait_ge(ga_att, c)
                    dve.wait_ge(ga_kdt, c)
                for h in range(HP):
                    for j in range(4):
                        mid = gG[:, h, c * P + 32 * j + 15:c * P + 32 * j + 16]
                        dve.tensor_scalar(dq[:, h, j, :], gG[:, h, t], mid, lim, ALU.subtract, ALU.min)
                        dve.tensor_scalar(dkA[:, h, 32 * j:32 * j + 32], gG[:, h, c * P + 32 * j:c * P + 32 * j + 32],
                                          mid, -lim, ALU.subtract, ALU.max)
                    end = gG[:, h, c * P + P - 1:c * P + P]
                    last = dve.tensor_scalar(kdA[:, h, :], gG[:, h, t], end, None, ALU.subtract)
                last.then_inc(ga_dif, 1)
                dve.wait_ge(ga_fac, c + 1)
                dve.wait_ge(ga_exp, c + 1)
                if c:
                    dve.wait_ge(ga_o, c)
                for h in range(HP):
                    q = prE[:, AQ + h:AQ + h + 1, t]
                    k = prE[:, AK + h, t]
                    dve.tensor_tensor(dq[:, h], dq[:, h], q.to_broadcast([P, 4, P]), ALU.mult)
                    dve.tensor_tensor(dkA[:, h, :], dkA[:, h, :], k, ALU.mult).then_inc(ga_fac2, 1)
                    dve.tensor_tensor(kdA[:, h, :], kdA[:, h, :], k, ALU.mult)
                    dve.tensor_tensor(qgA[:, h, :], eA[:, h, :], prE[:, AQ + h, t], ALU.mult).then_inc(ga_fac2, 1)
                dve.wait_ge(ga_s, c + 1)
                for h in range(HP):
                    dve.scalar_tensor_tensor(out=stA[:, h, :], in0=stA[:, h, :], scalar=eA[:, h, P - 1:P],
                                             in1=banks(6, 1)[:, h * DV:(h + 1) * DV], op0=ALU.mult, op1=ALU.add)\
                       .then_inc(ga_sc, 1) if h == HP - 1 else \
                        dve.scalar_tensor_tensor(out=stA[:, h, :], in0=stA[:, h, :], scalar=eA[:, h, P - 1:P],
                                                 in1=banks(6, 1)[:, h * DV:(h + 1) * DV], op0=ALU.mult, op1=ALU.add)

            def over(m):
                return m.rearrange("p (a t) -> p a t", a=1)

            def gdn(c):
                t = slice(c * P, (c + 1) * P)
                G = banks(0, 1).rearrange("p (h t) -> p h t", h=HB)
                bank = lambda n: banks(n, 1).rearrange("p (h t) -> p h t", h=HB)
                beta = colGB[:, c, 64:64 + HB]
                dve.wait_ge(gb_eg, c + 1)
                for h in range(HB):
                    dve.tensor_scalar(dif[:, h, :], G[:, h, :], colGB[:, c, 32 + h:33 + h], 0.0, ALU.subtract, ALU.min)
                dve.tensor_tensor(colS[:, 2, :], G[:, :, P - 1], colGB[:, c, 32:32 + HB], ALU.subtract).then_inc(gb_dif, 1)
                dve.tensor_tensor(Lt[:], bank(1), over(strict[:]).to_broadcast([P, HB, P]), ALU.mult)
                dve.wait_ge(gb_c1, c + 1)
                dve.tensor_tensor(colS[:, 1, :], colS[:, 0, :], beta, ALU.mult).then_inc(gb_c2, 1)
                dve.wait_ge(gb_rel, c + 1)
                link(dve.tensor_tensor(dif[:], dif[:], over(keep[:]).to_broadcast([P, HB, P]), ALU.mult))
                dve.wait_ge(gb_kq, c + 1)
                link(dve.tensor_tensor(Dm[:], bank(2), dif[:], ALU.mult))
                link(dve.tensor_tensor(Lt[:], Lt[:], Dm[:], ALU.mult))
                link(dve.tensor_tensor(DT[:], Lt[:], over(masks[:, 0, :]).to_broadcast([P, HB, P]), ALU.mult))
                dve.tensor_tensor(DT[:], over(ident[:]).to_broadcast([P, HB, P]), DT[:], ALU.subtract).then_inc(gb_dt0, 1)
                dve.tensor_tensor(QKr[:], bank(3), dif[:], ALU.mult).then_inc(gb_qkr, 1)
                dve.wait_ge(gb_kv, c + 1)
                for h in range(HB):
                    last = dve.tensor_scalar(vbB[:, h, :], bank(5)[:, h, :], beta[:, h:h + 1], None, ALU.mult)
                last.then_inc(gb_vb, 1)
                dve.tensor_tensor(qgB[:], EG[:], prE[:, BQ:BQ + HB, t], ALU.mult).then_inc(gb_qg, 1)
                n2 = HB // 2
                for l in range(1, 7):
                    e = 12 * c + 2 * (l - 1)
                    mask = over(masks[:, l, :]).to_broadcast([P, n2, P])
                    for a in range(2):
                        part = banks(4 * a, 1)[:, 0:n2 * P].rearrange("p (h t) -> p h t", h=n2)
                        dve.wait_ge(gb_t1, e + a + 1)
                        dve.tensor_tensor(T1[:, n2 * a:n2 * (a + 1), :], part, mask, ALU.mult).then_inc(gb_t1c, 1)
                    for a in range(2):
                        hs = slice(n2 * a, n2 * (a + 1))
                        dve.wait_ge(gb_dd, e + a + 1)
                        if l < 6:
                            part = banks(4 * a + 1, 1)[:, 0:n2 * P].rearrange("p (h t) -> p h t", h=n2)
                            dve.tensor_tensor(Dm[:, hs, :], Dm[:, hs, :], part, ALU.subtract)
                        part = banks(4 * a + 2, 1)[:, 0:n2 * P].rearrange("p (h t) -> p h t", h=n2)
                        dve.tensor_tensor(DT[:, hs, :], DT[:, hs, :], part, ALU.subtract).then_inc(gb_ddc, 1)
                dve.wait_ge(gb_s, c + 1)
                for h in range(HB):
                    last = dve.scalar_tensor_tensor(out=stB[:, h, :], in0=stB[:, h, :], scalar=EG[:, h, P - 1:P],
                                                    in1=bank(5)[:, h, :], op0=ALU.mult, op1=ALU.add)
                last.then_inc(gb_sc, 1)

            def samples_e():
                s = slice(TP, TOK)
                dve.wait_ge(sa_bc, 1)
                dve.tensor_copy(beS[:], banks(7, 1).rearrange("p (h t) -> p h t", h=HB)[:, :, P - TS:P])
                dve.wait_ge(sa_ks, 1)
                dve.wait_ge(sa_eg, 1)
                link(dve.tensor_tensor(vnS[:], banks(0, 1)[:, 0:HB * TS].rearrange("p (h b) -> p h b", h=HB), egS[:],
                                       ALU.mult))
                link(dve.tensor_tensor(vnS[:], prE[:, BV:BV + HB, s], vnS[:], ALU.subtract))
                dve.tensor_tensor(vnS[:], vnS[:], beS[:], ALU.mult).then_inc(sa_vn, 1)
                n = 0
                for b in range(TS):
                    for h in range(HP):
                        dve.wait_ge(sa_kv, n + 1)
                        dve.scalar_tensor_tensor(out=stA_s[:, b, h, :], in0=stA_s[:, b, h, :], scalar=eaS[:, h, b:b + 1],
                                                 in1=kvS[:, n % 4, :], op0=ALU.mult, op1=ALU.add).then_inc(sa_st, 1)
                        n += 1
                for r in range(HB * TS):
                    h, b = r // TS, r % TS
                    dve.wait_ge(sa_kv, n + 1)
                    dve.scalar_tensor_tensor(out=stB_s[:, b, h, :], in0=stB_s[:, b, h, :], scalar=egS[:, h, b:b + 1],
                                             in1=kvS[:, n % 4, :], op0=ALU.mult, op1=ALU.add).then_inc(sa_st, 1)
                    n += 1

            def out_norm_e():
                for n in range(HA + HB + 1):
                    if n < HA + HB:
                        y = prE[:, AV + n if n < HA else BV + n - HA, :]
                        g = prE[:, AR + n if n < HA else BZ + n - HA, :]
                        dve.wait_ge(on_rn, n + 1)
                        link(dve.scalar_tensor_tensor(out=y, in0=y, scalar=col("gla_onorm" if n < HA else "gdn_onorm"),
                                                      in1=tmp[:, 2 + n % 2, :], op0=ALU.mult, op1=ALU.mult))
                        dve.tensor_tensor(y, y, g, ALU.mult).then_inc(on_y, 1)
                    if n:
                        m = n - 1
                        dve.wait_ge(o_hi, m + 1)
                        at = AV + m if m < HA else BV + m - HA
                        dve.tensor_tensor(oE[:, at, :], prE[:, at, :], oE[:, AR + m, :].bitcast(F32), ALU.subtract)\
                           .then_inc(o_lo, 1)

            def project_o(s):
                b = FIRST["mix_o0"]
                for n in range(O_TILES):
                    split_ahead(b, 4, 0, n)
                    if n == 0:
                        dve.memset(rawO[:, :, 0:CW - 1], 0.0).then_inc(e_free, 1)
                        dve.wait_ge(e_free, 2 if O_PARTS else 1)
                    if n == 2:
                        zero_sum(s + 1)
                    dve.wait_ge(unit_done, b + n + 1)
                    if n == 0:
                        dve.wait_ge(rstd_ready, s + 1)
                        dve.wait_ge(ssum_added, KD * (s + 1))
                    if n >= KR:
                        take(two(prO[:, n, :]), pair(n % 4 if n < 2 * KR else n % 2),
                             HDC ** -0.5 if OQ <= n < OK else 1.0).then_inc(po_read, 1)
                    else:
                        if n >= 2:
                            dve.wait_ge(conv_step_o, 8 * (n - 1))
                            dve.wait_ge(xo_ready, n - 1)
                        take(two(rawO[:, n % 2, CW - 1:CW - 1 + TOK]), pair(n % 4)).then_inc(po_read, 1)
                        conv(n, n % 2, rawO, histR, lambda k, n: PRM["rg_conv_w"] + k * KR + n, tailO,
                             po_read, n + 1, None, 8 * n, conv_step_o)
                    if n == KR + 1:
                        dve.wait_ge(o_loaded, 96)
                        dve.tensor_scalar(sbb[:, 1, :], sbb[:, 0, :], -1.0, None, ALU.mult).then_inc(rg_c2, 1)
                        lam = prm[:, PRM["rg_lambda"]:PRM["rg_lambda"] + KR]
                        link(dve.tensor_scalar(cc[:, 3, :], lam, -1.0, 0.0, ALU.mult, ALU.max))
                        dve.wait_ge(rg_c1, 1)
                        link(dve.tensor_tensor(cc[:, 3, :], cc[:, 3, :], cc[:, 2, :], ALU.add))
                        dve.tensor_scalar(cc[:, 0, :], cc[:, 3, :], -RG_C, None, ALU.mult)
                        dve.tensor_scalar(cc[:, 1, :], cc[:, 3, :], RG_C, None, ALU.mult).then_inc(rg_c2, 1)
                    if n >= 2 * KR:
                        (rg_gelu_arg, rg_mult_square, rg_scan)[(n - 2 * KR) % 3]((n - 2 * KR) // 3)

            def rg_gelu_arg(m):
                u, y = tmp[:, 2 + m % 2, :], prO[:, OY + m, :]
                dve.wait_ge(po_read, KR + m + 1)
                if m >= 2:
                    dve.wait_ge(rg_gelu, m - 1)
                link(dve.tensor_tensor(u, y, y, ALU.mult))
                link(dve.tensor_scalar(u, u, 0.044715, 1.0, ALU.mult, ALU.add))
                dve.tensor_tensor(u, u, y, ALU.mult).then_inc(rg_u, 1)

            def rg_mult_square(m):
                dve.wait_ge(rg_a, 3 * m + 3)
                link(dve.tensor_tensor(rgR[:, m, :], rgA[:, m, :], rgA[:, m, :], ALU.mult))
                dve.scalar_tensor_tensor(out=rgR[:, m, :], in0=rgR[:, m, :], scalar=1.0, in1=rgT[:, m, :],
                                         op0=ALU.add, op1=ALU.mult).then_inc(rg_m, 1)
                y = prO[:, OY + m, :]
                dve.scalar_tensor_tensor(out=y, in0=tmp[:, 2 + m % 2, :], scalar=1.0, in1=y,
                                         op0=ALU.add, op1=ALU.mult).then_inc(rg_gelu, 1)
                link(dve.tensor_tensor(rgI[:, m, :], rgI[:, m, :], prO[:, OX + m, :], ALU.mult))

            def rg_scan(m):
                x, b, a = prO[:, OX + m, :], rgR[:, m, :], rgA[:, m, :]
                dve.wait_ge(rg_mult, m + 1)
                link(dve.tensor_tensor(b, b, rgI[:, m, :], ALU.mult))
                dve.memset(a[:, 0:1], 0.0)
                link(dve.tensor_copy(b[:, 0:1], rgI[:, m, 0:1]))
                dve.tensor_tensor_scan(x[:, 0:TP], a[:, 0:TP], b[:, 0:TP], 0.0, ALU.mult, ALU.add)
                link(dve.tensor_tensor(x[:, TP:TOK], a[:, TP:TOK], h0T[:, m, :], ALU.mult))
                link(dve.tensor_tensor(x[:, TP:TOK], x[:, TP:TOK], b[:, TP:TOK], ALU.add))
                y = prO[:, OY + m, :]
                dve.scalar_tensor_tensor(out=y, in0=x, scalar=0.5, in1=y, op0=ALU.mult, op1=ALU.mult)\
                   .then_inc(rg_od, 1)

            def rows_o():
                for n in range(NB):
                    dve.wait_ge(kv_t, n + 1)
                    dve.tensor_copy(vtok[:, n, :], banks(n, 1)).then_inc(v_rows, 1)
                for n in range(3):
                    dve.wait_ge(row_t, n + 1)
                    dve.tensor_copy(rowS[:, n, :], banks(n, 1)[0:TS, :]).then_inc(v_rows, 1)

            def stick():
                def mask(buf, a):
                    for at, _ in SCORE:
                        last = dve.tensor_tensor(buf[:, a, at:at + P], buf[:, a, at:at + P], before[:], ALU.mult)
                    return last

                dve.wait_ge(o_consts, 5)
                for h in range(HC + 2):
                    if 2 <= h:
                        dve.wait_ge(sk_w, h - 1)
                        mask(skY, h % 2).then_inc(sk_mask, 1)
                    if h < HC:
                        a = h % 2
                        dve.wait_ge(sk_ln, h + 1)
                        dve.tensor_tensor(skY[:, a, :], skY[:, a, :], skL[:, a, :], ALU.add)
                        link(dve.tensor_tensor(skX[:, a, :], skX[:, a, :], skL[:, a, :], ALU.add))
                        link(mask(skX, a))
                        if h:
                            dve.wait_ge(sk_acc, h)
                        x1, x2, x3 = (skX[:, a, at:at + w] for at, w in SCORE[1:])
                        w1 = TP - P
                        dve.tensor_copy(skR[:, w1:w1 + P], x2[:, 0:P])
                        dve.tensor_copy(skR[:, 0:P], x1[:, 0:P])
                        link(dve.tensor_tensor(skR[:, w1 + P:], x2[:, P:], x3, ALU.add))
                        dve.tensor_tensor(skR[:, P:w1], x1[:, P:], skR[:, w1:], ALU.add).then_inc(sk_sp, 1)
                    if 1 <= h <= HC:
                        a = (h - 1) % 2
                        dve.wait_ge(sk_acc, h)
                        dve.tensor_tensor(skY[:, a, :], skY[:, a, :], banks(3, 3)[:, 0:SCORES], ALU.add)\
                           .then_inc(sk_add, 1)

            def samples_o():
                z, sp, w = (smS[:, n] for n in range(3))
                for b in range(TS):
                    dve.wait_ge(sm_q, b + 1)
                    dve.wait_ge(page_loaded[b % 4], 16 * PAGES * (b // 4 + 1))
                    for p in range(PAGES):
                        link(dve.tensor_tensor(kq[:], pages[:, b % 4, p, :], banks(b % 2, 1), ALU.mult))
                        last = dve.tensor_reduce(z[:, p, b, :], kq[:].rearrange("p (h d) -> p h d", h=HC), AX.X, ALU.add)
                        if p < PAGES - 1:
                            link(last)
                    last.then_inc(sm_kq, 1)
                    dve.wait_ge(sm_kq, b + 1)
                def flat(x):
                    return x.rearrange("p a b h -> p (a b) h")
                bias = sbb[:, 0:1, :].to_broadcast([P, PAGES * TS, HC])
                dve.tensor_tensor(flat(z), flat(z), bias, ALU.add).then_inc(sm_z, 1)
                dve.wait_ge(sm_z, 1)
                dve.tensor_scalar(w, z, 0.0, None, ALU.min)
                dve.wait_ge(sm_ln, 1)
                link(dve.tensor_scalar(z, z, 0.0, None, ALU.max))
                dve.tensor_tensor(w, w, sp, ALU.subtract)
                dve.tensor_tensor(z, z, sp, ALU.add).then_inc(sm_sp, 1)
                dve.wait_ge(sm_acc, 1)
                acc = banks(3, 1)[:, 0:PAGES * TS * HC]
                dve.tensor_tensor(w.rearrange("p a b h -> p (a b h)"), w.rearrange("p a b h -> p (a b h)"), acc,
                                  ALU.subtract).then_inc(sm_z, 1)
                for m in range(KC + KR):
                    dve.wait_ge(o_hi, O_PARTS + m + 1)
                    at, high = (OQ + m, OK + m) if m < KC else (OY + m - KC, OX + m - KC)
                    dve.tensor_tensor(oO[:, at, :], prO[:, at, :], oO[:, high, :].bitcast(F32), ALU.subtract)\
                       .then_inc(o_lo, 1)

            zero_sum(0)
            dve.wait_ge(setup_t, 1)
            dve.tensor_copy(prm[:], banks(5, 1)[:, 0:NPRM]).then_inc(prm_ready, 1)
            dve.wait_ge(setup_t, 2)
            dve.tensor_copy(xT[:, :, TP:TOK], banks(4, 1)[:, 0:KD * TS].rearrange("p (m s) -> p m s", m=KD))\
               .then_inc(prm_ready, 1)
            dve.wait_ge(prm_ready, 2)
            for m in range(KD):
                dve.wait_ge(setup_t, 3 + m)
                dve.tensor_copy(xT[:, m, 0:TP], banks(m % 4, 1)).then_inc(x_ready, 1)
                split(m, 4, 0, 0) if m < LOOKAHEAD else None
                if m:
                    add_square(0, m - 1, (m - 1) % 2)
            add_square(0, KD - 1, (KD - 1) % 2)
            dve.wait_ge(setup_t, 3 + KD)
            hist = banks(6, 1)
            n = TS * (CW - 1)
            dve.tensor_copy(histG[:].rearrange("p a b c -> p (a b c)"), hist[:, 0:QKV * n]).then_inc(hist_ready, 1)
            dve.tensor_copy(histR[:].rearrange("p a b c -> p (a b c)"), hist[:, QKV * n:(QKV + KR) * n])\
               .then_inc(hist_ready, 1)
            dve.tensor_copy(h0T[:].rearrange("p a b -> p (a b)"),
                            hist[:, (QKV + KR) * n:(QKV + KR) * n + KR * TS]).then_inc(hist_ready, 1)
            for s, (name, f) in enumerate(STAGES):
                if name == "ffn":
                    ffn_in(s, f)
                    ffn_down(s, f)
                elif name == "mix_e":
                    project_e(s)
                    gates_e()
                    l2_e()
                    for c in range(NB):
                        gla(c)
                    for c in range(NB):
                        gdn(c)
                    samples_e()
                    out_norm_e()
                    out_proj(s, "out_e0")
                elif name == "mix_o":
                    project_o(s)
                    rows_o()
                    stick()
                    samples_o()
                    out_proj(s, "out_o0")
            last_norm()

        @block.tensor
        def _(pe):
            def unit(s, number, rhs_hi, rhs_lo, tiles, psum, start, stop, ready=None):
                slot = s % SPLIT_SLOTS
                pe.wait_ge(lo_ready, number + 1)
                for k in range(tiles):
                    if ready is not None:
                        ready(k)
                    hi, lo = (w[:, slot, k * P:(k + 1) * P] for w in (whi, wlo))
                    for w, x in ((hi, rhs_hi), (hi, rhs_lo), (lo, rhs_hi)):
                        for half in range(2):
                            last = w is lo and k == tiles - 1
                            mm = pe.matmul(psum[:, half, :], w, x(k)[:, half * HALF:(half + 1) * HALF],
                                           start=start and k == 0 and w is hi and x is rhs_hi, stop=stop and last)
                mm.then_inc(unit_done, 1)

            def h_hi_tile(k):
                return hh[:, k, :]

            def h_lo_tile(k):
                return hl[:, k, :]

            def norm(k):
                pe.wait_ge(ssum_added, KD * (k + 1))
                for half in range(2):
                    mm = pe.matmul(pair(3)[:, half, :], ones[:], ssum[:, half * HALF:(half + 1) * HALF],
                                   start=True, stop=True)
                mm.then_inc(norm_sum, 1)

            def ffn_in(s, f):
                b = FIRST[f"in{f}"]

                def body(t):
                    peeled = isinstance(t, int) and t == 0
                    for a in range(2):
                        n = KF * f + 2 * t + a
                        for up in range(2):
                            q = 2 * a + up
                            if not peeled:
                                pe.wait_ge(up_read if up else gate_read, n - 1)
                            if peeled and q == 3:
                                pe.wait_ge(ln_ready, s + 1)
                            unit(b + q, b + 4 * t + q, h_hi_tile, h_lo_tile, KD, pair(q), True, True,
                                 (lambda k: pe.wait_ge(h_lo, KD * s + k + 1)) if peeled and q == 0 else None)
                            if peeled and q == 0:
                                norm(s)
                body(0)
                loop(pe, 1, KF // 2, body)

            def ffn_down(s, f):
                b = FIRST[f"down{f}"]

                def body(t):
                    for a in range(4):
                        pe.wait_ge(x_ready, KD * (s + 1) + 4 * t + a - 3)
                        pe.wait_ge(up_read, KF * (f + 1) - 1 + a // 2)
                        for c in range(PARTS):
                            k0 = UNIT * c
                            n = min(UNIT, KF - k0)
                            pe.wait_ge(act_lo, KF * f + k0 + n)
                            q = PARTS * a + c
                            unit(b + q, b + 4 * PARTS * t + q, lambda k: act_h[:, k0 + k, :],
                                 lambda k: act_l[:, k0 + k, :], n, pair(a), c == 0, c == PARTS - 1)
                loop(pe, 0, KD // 4, body)

            def project(s, b, tiles, read, extra):
                def body(t):
                    peeled = isinstance(t, int) and t == 0
                    for q in range(4):
                        if not peeled:
                            pe.wait_ge(read, 4 * t + q - 3 + extra)
                        elif q == 2:
                            pe.wait_ge(read, extra)
                        elif q == 3:
                            pe.wait_ge(ln_ready, s + 1)
                        unit(b + q, b + 4 * t + q, h_hi_tile, h_lo_tile, KD, pair(q), True, True,
                             (lambda k: pe.wait_ge(h_lo, KD * s + k + 1)) if peeled and q == 0 else None)
                        if peeled and q == 0:
                            norm(s)
                body(0)
                loop(pe, 1, tiles // 4, body)

            def out_proj(s, name, parts, hi, lo):
                b = FIRST[name]
                pe.wait_ge(o_lo, parts)

                def body(t):
                    for a in range(4):
                        pe.wait_ge(x_ready, KD * (s + 1) + 4 * t + a - 3)
                        unit(b + a, b + 4 * t + a, hi, lo, KD, pair(a), True, True)
                loop(pe, 0, KD // 4, body)

            def project_e(s):
                b = FIRST["mix_e0"]
                unit(b, b, h_hi_tile, h_lo_tile, KD, pair(2), True, True, lambda k: pe.wait_ge(h_lo, KD * s + k + 1))
                project(s, b + 1, E_TILES, pe_read, 1)

            def mm1(out, w, x):
                return pe.matmul(out, w, x, start=True, stop=True)

            def gates_e():
                pe.wait_ge(e_loaded, 96)
                pe.wait_ge(pe_read, E_TILES + 1)
                for h in range(HP):
                    for half in range(2):
                        mm = mm1(pair(h)[:, half, :], wgate[:, h * P:(h + 1) * P],
                                 small[0:RANK, half * HALF:(half + 1) * HALF])
                mm.then_inc(gla_z, 1)

            def unit_sum(n, sq, total, rn):
                pe.wait_ge(sq, n + 1)
                if n >= 2:
                    pe.wait_ge(rn, n - 1)
                for half in range(2):
                    mm = mm1(pair(n % 2)[:, half, :], ones[:], tmp[:, n % 2, half * HALF:(half + 1) * HALF])
                mm.then_inc(total, 1)

            def l2_e():
                for n in range(2 * HB):
                    unit_sum(n, l2_sq, l2_sum, l2_rn)
                pe.wait_ge(gates, 2)
                for c in range(NB):
                    mm = turn(banks(7, 1)[:, c * 96:(c + 1) * 96], small[:, c * P:(c + 1) * P], 96)
                mm.then_inc(col_t, 1)
                pe.wait_ge(conv_step, 8 * QKV)
                pe.wait_ge(l2_rn, 2 * HB)
                for n in range(QKV):
                    mm = turn(banks(4 + n // 4, 1)[0:TAIL, n % 4 * P:(n % 4 + 1) * P], tailE[:, n, :], P)
                mm.then_inc(tail_t, 1)
                pe.wait_ge(tail_row, 3)
                pe.wait_ge(col_ready, 1)
                pe.wait_ge(gla_r, 2 * HP)

            def gla(c):
                t = slice(c * P, (c + 1) * P)
                if c:
                    pe.wait_ge(ga_vtc, c)
                    pe.wait_ge(ga_sc, c)
                for h in range(HA):
                    mm = turn(banks(2, 1)[:, h * P:(h + 1) * P], prE[:, AV + h, t], P)
                mm.then_inc(ga_vt, 1)
                pe.wait_ge(ga_fac2, 2 * HP * (c + 1))
                for h in range(HP):
                    for q in range(2):
                        r = slice(q * DKA, (q + 1) * DKA)
                        for j in range(4):
                            mm = mm1(PS[32 * j:32 * j + 32, q, h * P:(h + 1) * P], dkA[r, h, 32 * j:32 * j + 32],
                                     dq[r, h, j, :])
                mm.then_inc(ga_att, 1)
                for h in range(HP):
                    mm = turn(banks(3, 1)[:, h * P:(h + 1) * P], kdA[:, h, :], P)
                mm.then_inc(ga_kdt, 1)
                pe.wait_ge(ga_vtc, c + 1)
                pe.wait_ge(ga_mask, c + 1)
                if c:
                    pe.wait_ge(ga_oc, c)
                for n in range(HA):
                    h, q = n // 2, n % 2
                    r = slice(q * DKA, (q + 1) * DKA)
                    out = banks(4 + q, 1)[:, h * P:(h + 1) * P]
                    pe.matmul(out, vtA[:, n, :], attT[:, q, h, :], start=True, stop=False)
                    mm = pe.matmul(out, stA[r, h, :], qgA[r, h, :], start=False, stop=True)
                mm.then_inc(ga_o, 1)
                pe.wait_ge(ga_kdtc, c + 1)
                for n in range(HA):
                    h, q = n // 2, n % 2
                    mm = mm1(banks(6, 1)[q * DKA:(q + 1) * DKA, h * DV:(h + 1) * DV], kdtA[:, h, q * DKA:(q + 1) * DKA],
                             vtA[:, n, :])
                mm.then_inc(ga_s, 1)

            def row_of(r, width=P):
                def of(rows):
                    return ident[0:rows, r:r + 1].to_broadcast([rows, width])
                return of

            def gdn(c):
                t = slice(c * P, (c + 1) * P)
                n2 = HB // 2
                bank = lambda n, h: banks(n, 1)[:, h * P:(h + 1) * P]
                if c == 0:
                    pe.wait_ge(ga_oc, NB)
                    pe.wait_ge(ga_sc, NB)
                else:
                    pe.wait_ge(gb_oc, c)
                    pe.wait_ge(gb_sc, c)
                for h in range(HB):
                    mm1(bank(0, h), row_of(32 + h)(96), small[:, t])
                    mm = mm1(bank(1, h), row_of(64 + h)(96), small[:, t])
                mm.then_inc(gb_bc, 1)
                pe.wait_ge(l2_done, 2 * HB)
                for h in range(HB):
                    mm1(bank(2, h), prE[:, BK + h, t], prE[:, BK + h, t])
                    mm = mm1(bank(3, h), prE[:, BK + h, t], prE[:, BQ + h, t])
                mm.then_inc(gb_kq, 1)
                for h in range(HB):
                    turn(bank(4, h), prE[:, BK + h, t], P)
                    mm = turn(bank(5, h), prE[:, BV + h, t], P)
                mm.then_inc(gb_kv, 1)
                pe.wait_ge(gb_dt0, c + 1)
                pe.wait_ge(gb_qkr, c + 1)
                for h in range(HB):
                    mm = turn(bank(3, h), DT[:, h, :], P)
                mm.then_inc(gb_d0, 1)
                pe.wait_ge(gb_d0c, c + 1)
                pe.wait_ge(gb_ks, c + 1)
                pe.wait_ge(gb_vb, c + 1)
                for l in range(1, 7):
                    e = 12 * c + 2 * (l - 1)
                    for a in range(2):
                        if l > 1:
                            pe.wait_ge(gb_ddc, e + a - 1)
                        for j in range(n2):
                            h = n2 * a + j
                            mm = mm1(bank(4 * a, j), Lt[:, h, :], Dm[:, h, :])
                        mm.then_inc(gb_t1, 1)
                    for a in range(2):
                        pe.wait_ge(gb_t1c, e + a + 1)
                        for j in range(n2):
                            h = n2 * a + j
                            if l < 6:
                                mm1(bank(4 * a + 1, j), DT[:, h, :], T1[:, h, :])
                            mm = mm1(bank(4 * a + 2, j), T1[:, h, :], DT[:, h, :])
                        mm.then_inc(gb_dd, 1)
                pe.wait_ge(gb_ddc, 12 * (c + 1))
                for h in range(HB):
                    mm = mm1(bank(3, h), kbg[:, h, :], DT[:, h, :])
                mm.then_inc(gb_wt, 1)
                pe.wait_ge(gb_wtc, c + 1)
                for h in range(HB):
                    pe.matmul(bank(7, h), DT[:, h, :], vbB[:, h, :], start=True, stop=False)
                    mm = pe.matmul(bank(7, h), nWT[:, h, :], stB[:, h, :], start=False, stop=True)
                mm.then_inc(gb_vn, 1)
                pe.wait_ge(gb_vnc, c + 1)
                pe.wait_ge(gb_qg, c + 1)
                for h in range(HB):
                    pe.matmul(bank(4, h), T1[:, h, :], QKr[:, h, :], start=True, stop=False)
                    mm = pe.matmul(bank(4, h), stB[:, h, :], qgB[:, h, :], start=False, stop=True)
                mm.then_inc(gb_o, 1)
                for h in range(HB):
                    mm = mm1(bank(5, h), kdB[:, h, :], T1[:, h, :])
                mm.then_inc(gb_s, 1)

            def samples_e():
                pe.wait_ge(gb_oc, NB)
                pe.wait_ge(gb_sc, NB)
                for h in range(HB):
                    mm1(banks(6, 1)[:, h * P:(h + 1) * P], row_of(32 + h)(96), small[:, TOK - P:TOK])
                    mm = mm1(banks(7, 1)[:, h * P:(h + 1) * P], row_of(64 + h)(96), small[:, TOK - P:TOK])
                mm.then_inc(sa_bc, 1)
                for r in range(HB * TS):
                    h, b = r // TS, r % TS
                    mm = mm1(banks(0, 1)[:, r:r + 1], stB_s[:, b, h, :], prE[:, BK + h, TP + b:TP + b + 1])
                mm.then_inc(sa_ks, 1)
                for h in range(HA):
                    mm = turn(banks(1, 1)[0:TS, h * P:(h + 1) * P], prE[:, AV + h, TP:TOK], P)
                mm.then_inc(sa_r, 1)
                pe.wait_ge(sa_vn, 1)
                turn(banks(5, 1)[0:HB * TS, 0:DV], vnS[:].rearrange("p h b -> p (h b)"), P).then_inc(sa_r, 1)
                pe.wait_ge(sa_rc, 2)
                v = vaR[:].rearrange("p (h q) v -> p q h v", q=2)
                for b in range(TS):
                    if b >= 4:
                        pe.wait_ge(sa_kv, (b // 2 - 1) * 2 * HP)
                    for q in range(2):
                        at = b % 2 * HP * P
                        mm = mm1(banks(2 + b // 2 % 2, 1)[q * DKA:(q + 1) * DKA, at:at + HP * P],
                                 ident[0:TS, b:b + 1].to_broadcast([TS, DKA]), v[:, q])
                    if b % 2:
                        mm.then_inc(sa_b, 1)
                for r in range(HB * TS):
                    if r % 4 == 0:
                        g = r // 4
                        pe.wait_ge(sa_kv, HP * TS if g < 2 else HP * TS + 4 * (g - 1))
                    mm = mm1(banks(2 + r // 4 % 2, 1)[:, r % 4 * P:(r % 4 + 1) * P],
                             row_of(r)(HB * TS), vnR[:])
                    if r % 4 == 3:
                        mm.then_inc(sa_b, 1)
                pe.wait_ge(sa_st, HP * TS)
                for q in range(2):
                    for h in range(HP):
                        for b in range(TS):
                            r = slice(q * DKA, (q + 1) * DKA)
                            mm = mm1(PS[:, 6 + q, h * TS + b:h * TS + b + 1], stA_s[r, b, h, :],
                                     prE[r, AQ + h, TP + b:TP + b + 1])
                mm.then_inc(sa_o, 1)
                pe.wait_ge(sa_st, HP * TS + HB * TS)
                for r in range(HB * TS):
                    h, b = r // TS, r % TS
                    mm = mm1(banks(4, 1)[:, r:r + 1], stB_s[:, b, h, :], prE[:, BQ + h, TP + b:TP + b + 1])
                mm.then_inc(sa_o, 1)

            def out_norm_e():
                pe.wait_ge(sa_kv, HP * TS + HB * TS)
                pe.wait_ge(sa_vn, 1)
                for n in range(HA + HB):
                    unit_sum(n, on_sq, on_sum, on_rn)

            def project_o(s):
                b = FIRST["mix_o0"]
                for n in range(O_TILES):
                    early = n < 2 * KR
                    if n >= 2 * KR and (n - 2 * KR) % 3 == 0:
                        m = (n - 2 * KR) // 3
                        pe.wait_ge(o_loaded, 96)
                        pe.wait_ge(xo_ready, m + 1)
                        pe.wait_ge(po_read, 2 * KR)
                        if m:
                            pe.wait_ge(rg_sig, 2 * m)
                        for a in range(2):
                            for half in range(2):
                                mm = mm1(pair(2 + a)[:, half, :], wrg[:, a, m, :],
                                         prO[:, OX + m, half * HALF:(half + 1) * HALF])
                        mm.then_inc(rg_z, 1)
                    if n == 1:
                        norm(s)
                    if n == 3:
                        pe.wait_ge(ln_ready, s + 1)
                    if early and n >= 4:
                        pe.wait_ge(po_read, n - 3)
                    elif not early:
                        pe.wait_ge(po_read, n - 1)
                    unit(b + n, b + n, h_hi_tile, h_lo_tile, KD, pair(n % 4 if early else n % 2), True, True,
                         (lambda k: pe.wait_ge(h_lo, KD * s + k + 1)) if n == 0 else None)

            def rows_o():
                pe.wait_ge(po_read, O_TILES)
                pe.wait_ge(rg_sig, 2 * KR)
                for tiles, at in ((OV, 0), (OK, 4)):
                    for c in range(NB):
                        for m in range(KC):
                            mm = turn(banks(at + c, 1)[:, m * P:(m + 1) * P], prO[:, tiles + m, c * P:(c + 1) * P], P)
                        mm.then_inc(kv_t, 1)
                for n, tiles in enumerate((OQ, OK, OV)):
                    pe.wait_ge(v_rows, n + 1)
                    for m in range(KC):
                        mm = turn(banks(n, 1)[0:TS, m * P:(m + 1) * P], prO[:, tiles + m, TP:TOK], P)
                    mm.then_inc(row_t, 1)
                pe.wait_ge(v_rows, NB)
                pe.wait_ge(rg_od, KR)
                for m in range(KR):
                    mm = turn(banks(3, 1)[0:1 + TS, m * P:(m + 1) * P], prO[:, OX + m, TP - 1:TOK], P)
                mm.then_inc(row_t, 1)
                pe.wait_ge(k_rows, 1)
                for m in range(KR):
                    mm = turn(banks(4, 1)[0:TAIL, m * P:(m + 1) * P], tailO[:, m, :], P)
                mm.then_inc(row_t, 1)

            def stick():
                pe.wait_ge(v_rows, NB + 3)
                for h in range(HC + 2):
                    if h < HC:
                        r = slice(h % 2 * HDC, (h % 2 + 1) * HDC)
                        if h:
                            pe.wait_ge(sk_read, h)
                        for n, (at, w) in enumerate(SCORE):
                            mm = mm1(banks(0, 3)[:, at:at + w], prO[r, OK + h // 2, n * P:(n + 1) * P],
                                     prO[r, OQ + h // 2, n * P:TP])
                        mm.then_inc(sk_z, 1)
                    if 1 <= h <= HC:
                        a = (h - 1) % 2
                        if h == 1:
                            pe.wait_ge(k_rows, NB + 2)
                            pe.wait_ge(k_rows, NB)
                        else:
                            pe.wait_ge(sk_add, h - 1)
                        pe.wait_ge(sk_sp, h)
                        later = [skR[:, 0:TP - P], skR[:, TP - P:], skX[:, a, SCORE[3][0]:SCORE[3][0] + P]]
                        for n, (at, w) in enumerate(SCORE):
                            acc = banks(3, 3)[:, at:at + w]
                            mm = pe.matmul(acc, after[:], skX[:, a, at:at + w], start=True, stop=n == NB - 1)
                            if n < NB - 1:
                                mm = pe.matmul(acc[:, P:], ones[:], later[n], start=False, stop=True)
                        mm.then_inc(sk_acc, 1)
                    if h >= 2:
                        n = h - 2
                        r = slice(n % 2 * HDC, (n % 2 + 1) * HDC)
                        if n >= 2:
                            pe.wait_ge(sk_oc, n - 1)
                        pe.wait_ge(sk_mask, n + 1)
                        for c, (at, w) in enumerate(SCORE):
                            mm = pe.matmul(banks(6 + n % 2, 1)[r, c * P:TP], vtok[:, c, n * HDC:(n + 1) * HDC],
                                           skY[:, n % 2, at:at + w], start=c == 0, stop=c == NB - 1)
                        mm.then_inc(sk_o, 1)

            def samples_o():
                for b in range(TS):
                    if b >= 2:
                        pe.wait_ge(sm_kq, b - 1)
                    mm1(banks(b % 2, 1), row_of(b)(TS), rowS[:, 0, :]).then_inc(sm_q, 1)
                pe.wait_ge(sm_sp, 1)
                pe.wait_ge(sk_add, HC)
                n = TS * HC
                x = [smS[:, 0, p].rearrange("p b h -> p (b h)") for p in range(PAGES)]
                for p in range(PAGES):
                    acc = banks(3, 1)[:, p * n:(p + 1) * n]
                    mm = pe.matmul(acc, after[:], x[p], start=True, stop=p == PAGES - 1)
                    for later in range(p + 1, PAGES):
                        mm = pe.matmul(acc, ones[:], x[later], start=False, stop=later == PAGES - 1)
                mm.then_inc(sm_acc, 1)
                pe.wait_ge(sm_w, 1)
                for b in range(TS):
                    pe.wait_ge(page_loaded[b % 4], 16 * PAGES * ((b + TS) // 4 + 1))
                    for m in range(KC):
                        for p in range(PAGES):
                            at = (m * TS + b) * 2
                            mm = pe.matmul(banks(2, 1)[:, at:at + 2], pages[:, b % 4, p, m * P:(m + 1) * P],
                                           smS[:, 2, p, b, 2 * m:2 * m + 2], start=p == 0, stop=p == PAGES - 1)
                    mm.then_inc(sm_pv, 1)

            def turn(dst, src, n):
                return pe.transpose(dst, src, ident[0:n, 0:n])

            pe.wait_ge(consts, 3)
            pe.wait_ge(p_loaded, 16 * (len(ROWS_A) + len(ROWS_B)))
            turn(banks(5, 1)[:, 0:NA], prow_a[:], NA)
            turn(banks(5, 1)[:, NA:NPRM], prow_b[:], NPRM - NA).then_inc(setup_t, 1)
            pe.wait_ge(x_loaded, 16 * (NB + 1))
            for m in range(KD):
                mm = turn(banks(4, 1)[:, m * TS:(m + 1) * TS], xsrow[:, m * P:(m + 1) * P], TS)
            mm.then_inc(setup_t, 1)
            for m in range(KD):
                if m >= 4:
                    pe.wait_ge(x_ready, m - 3)
                for b in range(NB):
                    mm = turn(banks(m % 4, 1)[:, b * P:(b + 1) * P], xrow[:, b, m * P:(m + 1) * P], P)
                mm.then_inc(setup_t, 1)
            pe.wait_ge(s_loaded, 48)
            n = TS * (CW - 1)
            for m in range(QKV):
                turn(banks(6, 1)[:, m * n:(m + 1) * n], hrow_g[:, m * P:(m + 1) * P], n)
            for m in range(KR):
                turn(banks(6, 1)[:, (QKV + m) * n:(QKV + m + 1) * n], hrow_r[:, m * P:(m + 1) * P], n)
                at = (QKV + KR) * n + m * TS
                mm = turn(banks(6, 1)[:, at:at + TS], hrow_0[:, m * P:(m + 1) * P], TS)
            mm.then_inc(setup_t, 1)
            pe.wait_ge(hist_ready, 3)
            for s, (name, f) in enumerate(STAGES):
                if name == "ffn":
                    ffn_in(s, f)
                    ffn_down(s, f)
                elif name == "mix_e":
                    project_e(s)
                    gates_e()
                    l2_e()
                    for c in range(NB):
                        gla(c)
                    for c in range(NB):
                        gdn(c)
                    samples_e()
                    out_norm_e()
                    out_proj(s, "out_e0", HA + HB, lambda m: oE[:, AR + m, :],
                             lambda m: oE[:, AV + m if m < HA else BV + m - HA, :])
                elif name == "mix_o":
                    project_o(s)
                    rows_o()
                    stick()
                    samples_o()
                    out_proj(s, "out_o0", O_PARTS + KC + KR, lambda m: oO[:, OK + m if m < KC else OX + m - KC, :],
                             lambda m: oO[:, OQ + m if m < KC else OY + m - KC, :])
            norm(LAST_NORM)
            for m in range(KD):
                pe.wait_ge(y_ready, m + 1)
                if m >= 4:
                    pe.wait_ge(y_row, m - 3)
                y = tmp[:, m % 4, :]
                turn(banks(4 + m // 4, 1)[0:TS, (m % 4) * P:(m % 4 + 1) * P], y[:, TP:TOK], P)
                for b in range(NB):
                    mm = turn(banks(m % 4, 1)[:, b * P:(b + 1) * P], y[:, b * P:(b + 1) * P], P)
                mm.then_inc(y_t, 1)


_OUTS = ["y_prompt", "y_sample", "gla_p", "gla_s", "gdn_p", "gdn_s", "gcv_p", "gcv_s",
         "sbk_p", "sbk_s", "sbv_p", "sbv_s", "rgh_p", "rgh_s", "rgc_p", "rgc_s"]


def _shapes(a):
    bp, tp, dm = a["x_prompt"]
    bs = a["x_sample"][0]
    gla, gdn, conv = a["state_gla"][2:], a["state_gdn"][2:], a["state_gdn_conv"][2:]
    kv, h, rc = a["cache_sb_k"][3:], a["state_rg_h"][2:], a["state_rg_conv"][2:]
    ne, no = a["state_gla"][0], a["state_rg_h"][0]
    return [(bp, tp, dm), tuple(a["x_sample"]), (ne, bp) + gla, (ne, bs) + gla, (ne, bp) + gdn, (ne, bs) + gdn,
            (ne, bp) + conv, (ne, bs) + conv, (no, bp, tp) + kv, (no, bs, 1) + kv, (no, bp, tp) + kv,
            (no, bs, 1) + kv, (no, bp) + h, (no, bs) + h, (no, bp) + rc, (no, bs) + rc]


def kernel(**inputs):
    import numpy as _np
    import concourse.bacc as _bacc
    from concourse import mybir as _mybir
    from concourse.bass_utils import run_bass_kernel_spmd as _run

    nc = _bacc.Bacc("TRN2", target_bir_lowering=False, num_devices=1)
    arrays, ins, outs = {}, {}, {}
    for name, value in inputs.items():
        a = _np.ascontiguousarray(value)
        arrays[f"in_{name}"] = a
        ins[name] = nc.dram_tensor(f"in_{name}", a.shape, _mybir.dt.from_np(a.dtype), kind="ExternalInput").ap()
    shapes = _shapes({k: tuple(a.shape) for k, a in inputs.items()})
    for name, shape in zip(_OUTS, shapes):
        outs[name] = nc.dram_tensor(f"out_{name}", shape, F32, kind="ExternalOutput").ap()
    build_step(nc, ins, outs)
    r = _run(nc, [arrays], core_ids=[0])
    return tuple(r.results[0][f"out_{name}"] for name in _OUTS)
```

```python
from contextlib import ExitStack

import concourse.bass as bass
from concourse import mybir

F32 = mybir.dt.float32
F32R = mybir.dt.float32r
I32 = mybir.dt.int32
ACT = mybir.ActivationFunctionType
ALU = mybir.AluOpType
AX = mybir.AxisListType

P = 128
EPS = 1e-6
GLA_TAU = 16.0
RG_C = 8.0
CLAMP = 80.0
LOOKAHEAD = 3
SPLIT_SLOTS = 4
STAGE_SLOTS = 2
UNIT = 8
LN_EXP = "natural_log_exp_and_others"


STAGES = [("ffn", 0), ("mix_e", 0), ("ffn", 1), ("ffn", 2), ("mix_o", 0), ("ffn", 3)]


def loop(engine, first, last, body):
    if last - first == 1:
        body(first)
    elif last > first:
        with engine.Fori(first, last) as t:
            body(t)


def build_step(nc, i, o):
    TP = i["x_prompt"].shape[1]
    TS = i["x_sample"].shape[0]
    TOK = TP + TS
    HALF = TOK // 2
    DM = i["x_prompt"].shape[2]
    FF = i["ffn_w_gate"].shape[3]
    KD, KF = DM // P, FF // P
    NB = TP // P
    LAYERS = i["ln_ffn"].shape[0]
    HB = i["gdn_a_log"].shape[1]
    HA = i["state_gla"].shape[2]
    DKA = i["state_gla"].shape[3]
    DV = i["state_gla"].shape[4]
    RANK = i["gla_w_gate"].shape[1]
    HC = i["sb_bias"].shape[1]
    HDC = i["cache_sb_k"].shape[4]
    PAGES = i["page_table"].shape[1]
    POOL = i["cache_sb_k"].shape[1]
    CW = i["gdn_conv_w"].shape[1]
    KR = i["state_rg_h"].shape[2] // P
    HP = HA // 2
    QKV = 3 * HB
    TAIL = CW - 1 + TS
    assert TOK % 4 == 0 and DM % P == 0 and FF % P == 0 and TP % P == 0 and KF % 2 == 0 and KD % 4 == 0

    E_TILES = QKV + 2 * HP + 2 * HA + HB
    O_TILES = 5 * KR
    PARTS = -(-KF // UNIT)
    PHASES = {"ffn": [("in", 2 * KF), ("down", PARTS * KD)],
              "mix_e": [("mix_e", 1 + E_TILES), ("out_e", KD)],
              "mix_o": [("mix_o", O_TILES), ("out_o", KD)]}
    FIRST, UNITS = {}, 0
    for stage_name, f in STAGES:
        for name, n in PHASES[stage_name]:
            FIRST[name + str(f)] = UNITS
            UNITS += n
    LAST_NORM = len(STAGES)

    ROWS_A = [("ln_ffn", LAYERS * 2 * KD), ("ln_mix_e", KD), ("ln_mix_o", KD), ("ln_final", KD),
              ("gla_b_gate", HP), ("gla_onorm", 1), ("gdn_onorm", 1), ("gdn_conv_w", CW * QKV)]
    ROWS_B = [("rg_conv_w", CW * KR), ("rg_conv_b", KR), ("rg_b_a", KR), ("rg_b_x", KR), ("rg_lambda", KR)]
    PRM, cols = {}, 0
    for name, n in ROWS_A + ROWS_B:
        PRM[name] = cols
        cols += n
    NA = sum(n for _, n in ROWS_A)
    NPRM = cols
    NORM_PRM = [PRM["ln_ffn"] + KD * f if name == "ffn" else PRM["ln_" + name] for name, f in STAGES]
    NORM_PRM.append(PRM["ln_final"])

    E_STORES = 7
    O_STORES = 9
    KC = HC // 2
    WC = HC * HDC
    O_PARTS = HA + HB if ("mix_e", 0) in STAGES else 0
    assert NB == 4 and TP == 512 and HDC * 2 == P and KC == KR and TS == HC
    SCORE = [(0, TP), (TP, TP - P), (2 * TP, TP - 2 * P), (2 * TP - P, P)]
    SCORES = 2 * TP + 2 * P

    def rows(ap):
        names = " ".join("abcd"[:len(ap.shape)])
        flat = ap.rearrange(f"{names} -> ({names})") if len(ap.shape) > 1 else ap
        return flat.rearrange("(r p) -> r p", p=P)

    ctx = ExitStack()
    with ctx:
        def sb(name, shape, dt=F32, stack=ctx):
            return stack.enter_context(nc.sbuf_tensor(name, shape, dt))

        def sem(name):
            return ctx.enter_context(nc.semaphore(name))

        ident = sb("ident", [P, P])
        ones = sb("ones", [P, P])
        prm = sb("prm", [P, NPRM])
        xT = sb("xT", [P, KD, TOK])
        ssum = sb("ssum", [P, TOK])
        rstd = sb("rstd", [P, TOK])
        tmp = sb("tmp", [P, 4, TOK])
        stage = sb("stage", [P, STAGE_SLOTS, UNIT * P])
        whi = sb("whi", [P, SPLIT_SLOTS, UNIT * P], F32R)
        wlo = sb("wlo", [P, SPLIT_SLOTS, UNIT * P], F32R)
        histG = sb("histG", [P, QKV, TS, CW - 1])
        histR = sb("histR", [P, KR, TS, CW - 1])
        h0T = sb("h0T", [P, KR, TS])
        PS = ctx.enter_context(nc.psum_tensor("PS", [P, 8, 512], F32))

        def pair(n):
            return PS[:, 2 * n:2 * n + 2, 0:HALF]

        def two(ap):
            return ap.rearrange("p (a b) -> p a b", a=2)

        def banks(n, m):
            return PS[:, n:n + m, :].rearrange("p a b -> p (a b)")

        def col(name, n=0):
            return prm[:, PRM[name] + n:PRM[name] + n + 1]

        def tile(buf, m):
            return buf[:, bass.ds(m, 1), :].rearrange("p a b -> p (a b)")

        shared = ExitStack()
        hh = sb("hh", [P, KD, TOK], F32R, shared)
        hl = sb("hl", [P, KD, TOK], F32R, shared)
        st = ExitStack()
        act_h = sb("act_h", [P, KF, TOK], F32R, st)
        act_l = sb("act_l", [P, KF, TOK], F32R, st)
        st.close()
        st = ExitStack()
        xrow = sb("xrow", [P, NB, DM], F32, st)
        xsrow = sb("xsrow", [TS, DM], F32, st)
        prow_a = sb("prow_a", [NA, P], F32, st)
        prow_b = sb("prow_b", [NPRM - NA, P], F32, st)
        hrow_g = sb("hrow_g", [TS * (CW - 1), QKV * P], F32, st)
        hrow_r = sb("hrow_r", [TS * (CW - 1), KR * P], F32, st)
        hrow_0 = sb("hrow_0", [TS, KR * P], F32, st)
        st.close()
        st = ExitStack()
        yrow = sb("yrow", [P, NB, DM], F32, st)
        ysrow = sb("ysrow", [TS, DM], F32, st)
        st.close()
        BQ, BK, BV = 0, HB, 2 * HB
        AQ, AK, AV, AR, BZ = QKV, QKV + HP, QKV + 2 * HP, QKV + 2 * HP + HA, QKV + 2 * HP + 2 * HA
        st = ExitStack()
        oE = sb("oE", [P, E_TILES, TOK], F32R, st)
        st.close()
        st = ExitStack()
        prE = sb("prE", [P, E_TILES, TOK], F32, st)
        gla_at = ExitStack()
        eA = sb("eA", [P, HP, P], F32, gla_at)
        qgA = sb("qgA", [P, HP, P], F32, gla_at)
        kdA = sb("kdA", [P, HP, P], F32, gla_at)
        dkA = sb("dkA", [P, HP, P], F32, gla_at)
        vtA = sb("vtA", [P, HA, P], F32, gla_at)
        attT = sb("attT", [P, 2, HP, P], F32, gla_at)
        gla_at.close()
        stA_s = sb("stA_s", [P, TS, HP, DV], F32, st)
        kdtA = sb("kdtA", [P, HP, P], F32, st)
        egA = sb("egA", [P, HP, TS], F32, st)
        stB_s = sb("stB_s", [P, TS, HB, DV], F32, st)
        small = sb("small", [96, TOK], F32, st)
        wgate = sb("wgate", [RANK, HP * P], F32, st)
        gdnp = sb("gdnp", [36, 4], F32, st)
        masks = sb("masks", [P, 7, P], F32, st)
        keep = sb("keep", [P, P], F32, st)
        strict = sb("strict", [P, P], F32, st)
        colGB = sb("colGB", [P, NB, 96], F32, st)
        stA = sb("stA", [P, HP, DV], F32, st)
        stB = sb("stB", [P, HB, DV], F32, st)
        tailE = sb("tailE", [P, QKV, TAIL], F32, st)
        kqd_at = ExitStack()
        kqd = sb("kqd", [P, HB * TS, 2 * HB * TS], F32, kqd_at)
        kqd_at.close()
        dq = sb("dq", [P, HP, 4, P], F32, st)
        raw_at = ExitStack()
        rawE = sb("rawE", [P, 2, CW - 1 + TOK], F32, raw_at)
        raw_at.close()
        gG = sb("gG", [P, HP, TOK], F32, st)
        st.close()
        GATES_AT, L2_AT, GLA_AT = QKV, QKV + 2, AV + 2
        assert L2_AT + HB <= GLA_AT and E_TILES == GLA_AT + 2 * NB + 2
        LEVELS = 6
        STEPS_A, STEPS = TS, LEVELS * NB
        assert HP == 2 and HB * TS == 2 * (STEPS - STEPS_A)

        def cut(l):
            if l < 2 * HP:
                return prE[:, AQ + l, 0:TP].rearrange("p (h t) -> p h t", h=HB)
            return dq[:, l - 2 * HP].rearrange("p h t -> p (h t)").rearrange("p (h t) -> p h t", h=HB)

        def tile_pair(n):
            return 3 if n >= GLA_AT + 2 else 2 + n % 2 if n >= QKV else n % 4

        OX, OY, OQ, OK, OV = 0, KR, 2 * KR, 2 * KR + KC, 2 * KR + 2 * KC
        st = ExitStack()
        oO = sb("oO", [P, O_TILES, TOK], F32R, st)
        st.close()
        st = ExitStack()
        prO = sb("prO", [P, O_TILES, TOK], F32, st)
        tailO = sb("tailO", [P, KR, TAIL], F32, st)
        wrg = sb("wrg", [P, 2, KR, P], F32, st)
        cc = sb("cc", [P, 4, KR], F32, st)
        after = sb("after", [P, P], F32, st)
        before = sb("before", [P, P], F32, st)
        sbb = sb("sbb", [P, 2, HC], F32, st)
        ptab = sb("ptab", [1, TS * PAGES], I32, st)
        rg_at = ExitStack()
        rawO = sb("rawO", [P, 2, CW - 1 + TOK], F32, rg_at)
        rgR = sb("rgR", [P, KR, TOK], F32, rg_at)
        rgI = sb("rgI", [P, KR, TOK], F32, rg_at)
        rgA = sb("rgA", [P, KR, TOK], F32, rg_at)
        rgT = sb("rgT", [P, KR, TOK], F32, rg_at)
        rg_at.close()
        vtok = sb("vtok", [P, NB, WC], F32, st)
        ktok = sb("ktok", [P, NB, WC], F32, st)
        rowS = sb("rowS", [TS, 3, WC], F32, st)
        rowX = sb("rowX", [TAIL, 2, KR * P], F32, st)
        pages = sb("pages", [P, 4, PAGES, WC], F32, st)
        kq = sb("kq", [P, WC], F32, st)
        smS = sb("smS", [P, 3, PAGES, TS, HC], F32, st)
        smW = sb("smW", [P, PAGES, TS, TS, HC], F32, st)
        smO = sb("smO", [TS * HC, WC], F32, st)
        own = sb("own", [TS * HC, HC], F32, st)
        of_sample = sb("of_sample", [TS * HC, TS], F32, st)
        st.close()
        shared.close()
        st = ExitStack()
        skL = sb("skL", [P, SCORES], F32, st)
        skX = sb("skX", [P, 2, SCORES], F32, st)
        skY = sb("skY", [P, 3, SCORES], F32, st)
        skR = sb("skR", [P, TP - P + TP - 2 * P], F32, st)
        st.close()
        st = ExitStack()
        sample_at = st
        dif = sb("dif", [P, HB, P], F32, st)
        EG = sb("EG", [P, HB, P], F32, st)
        QKr = sb("QKr", [P, HB, P], F32, st)
        Lt = sb("Lt", [P, HB, P], F32, st)
        DT = sb("DT", [P, HB, P], F32, st)
        Dm = sb("Dm", [P, HB, P], F32, st)
        T1 = sb("T1", [P, HB, P], F32, st)
        qgB = sb("qgB", [P, HB, P], F32, st)
        kdB = sb("kdB", [P, HB, P], F32, st)
        vbB = sb("vbB", [P, HB, P], F32, st)
        colS = sb("colS", [P, 4, HB], F32, st)
        egS = sb("egS", [P, HB, TS], F32, sample_at)
        beS = sb("beS", [P, HB, TS], F32, sample_at)
        vnS = sb("vnS", [P, HB, TS], F32, sample_at)
        qkS = sb("qkS", [P, HB, TS], F32, sample_at)
        eaS = sb("eaS", [P, HP, TS], F32, sample_at)
        qkA = sb("qkA", [P, HP, TS], F32, sample_at)
        vnR = sb("vnR", [HB * TS, DV], F32, sample_at)
        vaR = sb("vaR", [TS, HA, DV], F32, sample_at)
        kvS = sb("kvS", [P, 4, DV], F32, sample_at)
        kqR = sb("kqR", [2 * HB * TS, DV], F32, sample_at)
        qaR = sb("qaR", [HA * TS, DV], F32, sample_at)
        qdA = sb("qdA", [P, HP * TS, HA * TS], F32, sample_at)
        sample_at.close()

        x_loaded, p_loaded, s_loaded = sem("x_loaded"), sem("p_loaded"), sem("s_loaded")
        consts = sem("consts")
        setup_t, prm_ready = sem("setup_t"), sem("prm_ready")
        w_loaded = [sem(f"w_loaded{n}") for n in range(STAGE_SLOTS)]
        hi_ready, lo_ready, unit_done = sem("hi_ready"), sem("lo_ready"), sem("unit_done")
        x_ready, sq_ready, ssum_zero, ssum_added = sem("x_ready"), sem("sq_ready"), sem("ssum_zero"), sem("ssum_added")
        norm_sum, ln_ready, rstd_ready = sem("norm_sum"), sem("ln_ready"), sem("rstd_ready")
        h_hi, h_lo = sem("h_hi"), sem("h_lo")
        gate_read, gate_ready, up_read, prod_ready, act_hi, act_lo = (
            sem(n) for n in "gate_read gate_ready up_read prod_ready act_hi act_lo".split())
        y_ready, y_t, y_row, stored = sem("y_ready"), sem("y_t"), sem("y_row"), sem("stored")

        e_free, e_loaded, e_consts = sem("e_free"), sem("e_loaded"), sem("e_consts")
        small_part = sem("small_part")
        pe_read, conv_step, silu_e = sem("pr_read_e"), sem("conv_step_e"), sem("silu_e")
        dve_chain, act_chain = sem("dve_chain"), sem("act_chain")
        gla_z, gla_sp, gla_r, gdn_sp, gates = (sem(n) for n in ("gla_z", "gla_sp", "gla_r", "gdn_sp", "gates"))
        hn_sq, hn_sum, hn_rn, hn_done = sem("hn_sq"), sem("hn_sum"), sem("hn_rn"), sem("hn_done")
        tail_row, tail_stored, e_stored = sem("tail_row"), sem("tail_stored"), sem("e_stored")
        col_t, col_ready = sem("col_t"), sem("col_ready")
        (ga_exp, ga_dif, ga_fac, ga_fac2, ga_att, ga_attc, ga_mask, ga_vt, ga_vtc, ga_kdt, ga_kdtc, ga_o, ga_oc,
         ga_s, ga_sc) = (sem("ga_" + n) for n in
            "exp dif fac fac2 att attc mask vt vtc kdt kdtc o oc s sc".split())
        (gb_bc, gb_eg, gb_dif, gb_rel, gb_kq, gb_qkr, gb_dt0, gb_lm, gb_dm, gb_kv, gb_ks, gb_vb, gb_d0, gb_d0c, gb_t1, gb_t1c,
         gb_dd, gb_ddc, gb_wt, gb_vn, gb_vnc, gb_o, gb_oc, gb_s, gb_sc, gb_qg, gb_c1) = (
            sem("gb_" + n) for n in ("bc eg dif rel kq qkr dt0 lm dm kv ks vb d0 d0c t1 t1c dd ddc wt vn vnc o oc "
                                     "s sc qg c1").split())
        (sa_bc, sa_eg, sa_zero, sa_diag, sa_ks, sa_ksc, sa_kst, sa_qk, sa_vn, sa_r, sa_rc, sa_b, sa_kv, sa_st, sa_o) = (
            sem("sa_" + n) for n in "bc eg zero diag ks ksc kst qk vn r rc b kv st o".split())
        o_hi, o_lo = sem("o_hi"), sem("o_lo")

        o_consts, o_loaded, o_stored = sem("o_consts"), sem("o_loaded"), sem("o_stored")
        po_read, conv_step_o, xo_ready = sem("pr_read_o"), sem("conv_step_o"), sem("xo_ready")
        rg_c1, rg_c2, rg_z, rg_sig, rg_u, rg_a, rg_m, rg_mult, rg_gelu, rg_od = (
            sem("rg_" + n) for n in "c1 c2 z sig u a m mult gelu od".split())
        kv_t, row_t = sem("kv_t"), sem("row_t")
        v_rows = sem("v_rows")
        k_rows = sem("k_rows")
        sk_z, sk_read, sk_ln, sk_added, sk_sp, sk_acc, sk_add, sk_w, sk_mask, sk_o, sk_oc = (
            sem("sk_" + n) for n in "z read ln added sp acc add w mask o oc".split())
        page_loaded = [sem(f"page_loaded{n}") for n in range(4)]
        sm_q, sm_kq, sm_ln, sm_w, sm_pv, sm_oc = (sem("sm_" + n) for n in "q kq ln w pv oc".split())
        sm_step = sem("sm_step")
        sm_sum = sem("sm_sum")

        block = ctx.enter_context(nc.Block())

        def loads(b, per, t, q):
            return 16 * ((b + q) // STAGE_SLOTS + 1 + per // STAGE_SLOTS * t)

        @block.sync
        def _(sp):
            def unit_free(u):
                sp.wait_ge(hi_ready, u - STAGE_SLOTS + 1)
                sp.wait_ge(lo_ready, u - STAGE_SLOTS + 1)

            def load(s, src, tiles=UNIT):
                slot = s % STAGE_SLOTS
                dst = stage[:, slot, 0:tiles * P].rearrange("p (k n) -> p k n", n=P)
                sp.dma_start(dst, src).then_inc(w_loaded[slot], 16)

            def tiled(w):
                return w.rearrange("(k p) n -> p k n", p=P)

            def ffn_in(f):
                b = FIRST[f"in{f}"]
                wg, wu = tiled(i["ffn_w_gate"][f // 2, f % 2]), tiled(i["ffn_w_up"][f // 2, f % 2])

                def body(t):
                    for q in range(4):
                        if not (f == 0 and isinstance(t, int) and t == 0 and q < STAGE_SLOTS):
                            unit_free(b + 4 * t + q)
                        load(b + q, (wu if q % 2 else wg)[:, :, bass.ds((2 * t + q // 2) * P, P)])

                if f == 0:
                    body(0)
                loop(sp, 1 if f == 0 else 0, KF // 2, body)

            def ffn_down(f):
                b = FIRST[f"down{f}"]
                wd = tiled(i["ffn_w_down"][f // 2, f % 2])

                def body(t):
                    for q in range(4 * PARTS):
                        unit_free(b + 4 * PARTS * t + q)
                        k = q % PARTS * UNIT
                        n = min(UNIT, KF - k)
                        load(b + q, wd[:, k:k + n, bass.ds((4 * t + q // PARTS) * P, P)], n)
                loop(sp, 0, KD // 4, body)

            def tiles4(b, w, column, first, last):
                def body(t):
                    for q in range(4):
                        unit_free(b + 4 * t + q)
                        load(b + q, w[:, :, bass.ds((4 * (t - first) + q) * P + column, P)])
                loop(sp, first, last, body)

            def mix_e():
                b, w = FIRST["mix_e0"], tiled(i["w_in_e"][0])
                qk, v = HA * DKA, HA * DV
                la = 2 * qk + 2 * v
                qkv = la + RANK
                ab = qkv + (QKV + HB) * P
                unit_free(b)
                slot = b % STAGE_SLOTS
                dst = stage[:, slot, :].rearrange("p (k n) -> p k n", n=P)
                sp.dma_start(dst[:, :, 0:RANK], w[:, :, la:la + RANK]).then_inc(small_part, 16)
                sp.dma_start(dst[:, :, 32:32 + HB], w[:, :, ab:ab + HB]).then_inc(small_part, 16)
                sp.wait_ge(small_part, 32)
                sp.dma_start(dst[:, :, 64:64 + HB], w[:, :, ab + HB:ab + 2 * HB]).then_inc(w_loaded[slot], 16)
                tiles4(b + 1, w, qkv, 0, 3)
                tiles4(b + 1, w, 0, 3, 6)
                tiles4(b + 1, w, qkv + QKV * P, 6, 7)

            for name, f in STAGES:
                if name == "ffn":
                    ffn_in(f)
                    ffn_down(f)
                elif name == "mix_e":
                    mix_e()
                    tiles4(FIRST["out_e0"], tiled(i["w_out_e"][0]), 0, 0, KD // 4)
                elif name == "mix_o":
                    b, w = FIRST["mix_o0"], tiled(i["w_in_o"][0])
                    tiles4(b, w, 3 * WC, 0, 2 * KR // 4)
                    tiles4(b, w, 0, 2 * KR // 4, O_TILES // 4)
                    tiles4(FIRST["out_o0"], tiled(i["w_out_o"][0]), 0, 0, KD // 4)

        @block.gpsimd
        def _(pool):
            stores = 0

            def store(dst, src):
                nonlocal stores
                stores += 1
                pool.dma_start(dst, src).then_inc(stored, 16)

            pool.memset(ones[:], 1.0).then_inc(consts, 1)
            pool.memset(ident[:], 1.0).then_inc(consts, 1)
            pool.wait_ge(consts, 2)
            pool.affine_select(out=ident[:], in_=ident[:], compare_op=ALU.is_equal, fill=0.0, base=0,
                               pattern=[[-1, P]], channel_multiplier=1).then_inc(consts, 1)

            def mix_e():
                def select(m, op, base, pattern, mult):
                    pool.wait_ge(e_consts, select.n)
                    pool.affine_select(out=m, in_=m, compare_op=op, fill=0.0, base=base, pattern=pattern,
                                       channel_multiplier=mult).then_inc(e_consts, 1)
                    select.n += 1

                pool.wait_ge(unit_done, FIRST["mix_e0"])
                pool.dma_start(stB_s[:].rearrange("p b h v -> p (b h) v"),
                               i["state_gdn"][0].rearrange("b h k v -> k (b h) v")).then_inc(e_loaded, 16)
                pool.dma_start(wgate[:], i["gla_w_gate"][0]).then_inc(e_loaded, 16)
                pool.dma_start(gdnp[32:32 + HB, 0:1], i["gdn_dt_bias"].rearrange("a h -> h a")).then_inc(e_loaded, 16)
                pool.dma_start(gdnp[32:32 + HB, 1:2], i["gdn_a_log"].rearrange("a h -> h a")).then_inc(e_loaded, 16)
                pool.memset(masks[:], 0.0).then_inc(e_consts, 1)
                pool.memset(keep[:], 1.0).then_inc(e_consts, 1)
                pool.memset(strict[:], 1.0).then_inc(e_consts, 1)
                pool.memset(stA[:], 0.0).then_inc(e_consts, 1)
                pool.memset(stB[:], 0.0).then_inc(e_consts, 1)
                pool.wait_ge(e_consts, 5)
                for l in range(7):
                    half = masks[:, l, :].rearrange("p (n a b) -> p n a b", a=2, b=1 << l)
                    pool.memset(half[:, :, 1, :], 1.0).then_inc(e_consts, 1)
                select.n = 12
                select(masks[:, 0, :].rearrange("p (n a) -> p n a", a=2)[:, :, 1], ALU.is_equal, 0, [[-2, P // 2]], 1)
                for l in range(1, 7):
                    b = 1 << l
                    half = masks[:, l, :].rearrange("p (n a b) -> p n a b", a=2, b=b)[:, :, 1, :]
                    select(half, ALU.is_ge, 0, [[-2 * b, P // (2 * b)], [0, b]], 1)
                    select(half, ALU.is_ge, b - 1, [[2 * b, P // (2 * b)], [0, b]], -1)
                select(keep[:], ALU.is_ge, 0, [[1, P]], -1)
                select(strict[:], ALU.is_gt, 0, [[1, P]], -1)
                for c in range(NB):
                    pool.wait_ge(ga_attc, c + 1)
                    a = attT[:].rearrange("p a b t -> p (a b) t")
                    pool.affine_select(out=a, in_=a, compare_op=ALU.is_ge, fill=0.0, base=0,
                                       pattern=[[0, HA], [1, P]], channel_multiplier=-1).then_inc(ga_mask, 1)

                pool.wait_ge(sa_eg, 1)
                pool.wait_ge(ga_att, NB)
                pool.memset(kqd[:], 0.0).then_inc(sa_zero, 1)

                def save(dst, src):
                    pool.dma_start(dst, src).then_inc(e_stored, 16)

                pool.wait_ge(ga_sc, NB)
                pool.wait_ge(ga_oc, NB)
                for par in range(2):
                    src = i["state_gla"][0].rearrange("b (h q) k v -> q k (b h) v", q=2)[par]
                    pool.dma_start(stA_s[par * DKA:(par + 1) * DKA, :, :, :].rearrange("p b h v -> p (b h) v"), src)\
                        .then_inc(e_loaded, 16)
                pool.wait_ge(tail_row, 3)
                tail = tmp[0:TAIL, :, :].rearrange("p a b -> p (a b)")[:, 0:QKV * P]
                pool.dma_start(o["gcv_p"][0, 0], tail[0:CW - 1, :]).then_inc(tail_stored, 16)
                pool.dma_start(o["gcv_s"][0, :, CW - 2, :], tail[CW - 1:TAIL, :]).then_inc(tail_stored, 16)
                save(o["gcv_s"][0, :, 0:CW - 2, :], i["state_gdn_conv"][0, :, 1:CW - 1, :])
                pool.wait_ge(ga_sc, NB)
                for par in range(2):
                    save(o["gla_p"][0, 0].rearrange("(h q) k v -> q k h v", q=2)[par], stA[par * DKA:(par + 1) * DKA, :, :])
                for c in range(NB):
                    pool.wait_ge(gb_dt0, c + 1)
                    for l in range(LEVELS):
                        m = masks[:, l + 1:l + 2, :].to_broadcast([P, HB, P])
                        pool.tensor_tensor(cut(l), Lt[:], m, ALU.mult).then_inc(gb_lm, 1)
                pool.wait_ge(gb_sc, NB)
                save(o["gdn_p"][0, 0].rearrange("h k v -> k h v"), stB[:])
                pool.wait_ge(sa_st, HP * TS + HB * TS)
                for par in range(2):
                    save(o["gla_s"][0].rearrange("b (h q) k v -> q k (b h) v", q=2)[par],
                         stA_s[par * DKA:(par + 1) * DKA, :, :, :].rearrange("p b h v -> p (b h) v"))
                save(o["gdn_s"][0].rearrange("b h k v -> k (b h) v"), stB_s[:].rearrange("p b h v -> p (b h) v"))

            def mix_o():
                pool.wait_ge(unit_done, FIRST["mix_o0"])
                pool.memset(wrg[:], 0.0).then_inc(o_consts, 1)
                pool.memset(after[:], 1.0).then_inc(o_consts, 1)
                pool.memset(before[:], 1.0).then_inc(o_consts, 1)
                pool.dma_start(sbb[:, 0, :], i["sb_bias"][0:1, :].to_broadcast([P, HC])).then_inc(o_loaded, 16)
                pool.dma_start(ptab[:], i["page_table"].rearrange("(x b) p -> x (b p)", x=1)).then_inc(o_loaded, 16)
                pool.wait_ge(o_consts, 3)
                for n, w in enumerate(("rg_w_a", "rg_w_x")):
                    for q in range(2):
                        src = i[w][0].rearrange("(m q) a b -> q a m b", q=2)[q]
                        half = slice(q * (P // 2), (q + 1) * (P // 2))
                        pool.dma_start(wrg[half, n, :, half], src).then_inc(o_loaded, 16)
                pool.affine_select(out=after[:], in_=after[:], compare_op=ALU.is_gt, fill=0.0, base=0,
                                   pattern=[[-1, P]], channel_multiplier=1).then_inc(o_consts, 1)
                pool.affine_select(out=before[:], in_=before[:], compare_op=ALU.is_gt, fill=0.0, base=0,
                                   pattern=[[1, P]], channel_multiplier=-1).then_inc(o_consts, 1)

                def load_pages(g):
                    cache = i["cache_sb_v" if g >= TS else "cache_sb_k"]
                    for p in range(PAGES):
                        at = g % TS * PAGES + p
                        page = nc.values_load(ptab[0:1, at:at + 1], engines=[mybir.EngineType.Pool], min_val=0,
                                              max_val=POOL - 1,
                                              skip_runtime_bounds_check_because="the table names pages of the pool")
                        pool.dma_start(pages[:, g % 4, p, :],
                                       cache[0, bass.ds(page, 1)].rearrange("a t h d -> t (a h d)"))\
                            .then_inc(page_loaded[g % 4], 16)

                def save(dst, src):
                    pool.dma_start(dst, src).then_inc(o_stored, 16)

                pool.wait_ge(rg_od, KR)
                pool.memset(smW[:], 0.0).then_inc(o_consts, 1)
                pool.memset(own[:], 0.0).then_inc(o_consts, 1)
                pool.memset(of_sample[:], 1.0).then_inc(o_consts, 1)
                pool.wait_ge(o_consts, 8)
                for b in range(TS):
                    pool.affine_select(out=own[:], in_=own[:], compare_op=ALU.not_equal, fill=1.0, base=-HC * b,
                                       pattern=[[-1, HC]], channel_multiplier=1).then_inc(o_consts, 1)
                    pool.wait_ge(o_consts, 9 + b)
                pool.affine_select(out=of_sample[:], in_=of_sample[:], compare_op=ALU.is_ge, fill=0.0, base=0,
                                   pattern=[[-HC, TS]], channel_multiplier=1).then_inc(o_consts, 1)
                pool.wait_ge(o_consts, 9 + TS)
                pool.affine_select(out=of_sample[:], in_=of_sample[:], compare_op=ALU.is_ge, fill=0.0, base=HC - 1,
                                   pattern=[[HC, TS]], channel_multiplier=-1).then_inc(o_consts, 1)
                pool.wait_ge(o_loaded, 96)
                for g in range(4):
                    load_pages(g)
                save(o["rgc_s"][0, :, 0:CW - 2, :], i["state_rg_conv"][0, :, 1:CW - 1, :])
                pool.wait_ge(v_rows, NB)
                save(o["sbv_p"][0, 0].rearrange("(c p) h d -> p c (h d)", p=P), vtok[:])
                pool.wait_ge(k_rows, NB)
                save(o["sbk_p"][0, 0].rearrange("(c p) h d -> p c (h d)", p=P), ktok[:])
                pool.wait_ge(v_rows, NB + 3)
                save(o["sbk_s"][0, :, 0].rearrange("b h d -> b (h d)"), rowS[:, 1, :])
                save(o["sbv_s"][0, :, 0].rearrange("b h d -> b (h d)"), rowS[:, 2, :])
                pool.wait_ge(k_rows, NB + 2)
                save(o["rgh_p"][0], rowX[0:1, 0, :])
                save(o["rgh_s"][0], rowX[1:1 + TS, 0, :])
                save(o["rgc_p"][0, 0], rowX[0:CW - 1, 1, :])
                save(o["rgc_s"][0, :, CW - 2, :], rowX[CW - 1:TAIL, 1, :])
                for n in range(HC):
                    pool.wait_ge(sm_kq, n + 1)
                    load_pages(n + 4)
                    pool.wait_ge(sk_w, n + 1)
                    for at, _ in SCORE:
                        block_w = skY[:, n % 3, at:at + P]
                        last = pool.tensor_tensor(block_w, block_w, before[:], ALU.mult)
                    last.then_inc(sk_mask, 1)
                for g in range(TS + 4, 2 * TS):
                    pool.wait_ge(sm_pv, g - 3 - TS)
                    load_pages(g)

            for name, f in STAGES:
                if name == "mix_e":
                    mix_e()
                elif name == "mix_o":
                    mix_o()
            for a in range(2):
                pool.wait_ge(y_row, KD // 2 * (a + 1))
                part = slice(a * DM // 2, (a + 1) * DM // 2)
                store(o["y_prompt"][0].rearrange("(b p) n -> p b n", p=P)[:, :, part], yrow[:, :, part])
            pool.wait_ge(y_row, KD + 2)
            store(o["y_sample"][:, 0, :], ysrow[:])
            pool.wait_ge(stored, 16 * stores)
            if ("mix_e", 0) in STAGES:
                pool.wait_ge(e_stored, 16 * E_STORES)
                pool.wait_ge(tail_stored, 32)
            if ("mix_o", 0) in STAGES:
                pool.wait_ge(o_stored, 16 * O_STORES)

        @block.scalar
        def _(act):
            def split(b, per, t, q):
                s = b + q
                act.wait_ge(w_loaded[s % STAGE_SLOTS], loads(b, per, t, q))
                if not isinstance(t, int) or s + per * t >= SPLIT_SLOTS:
                    act.wait_ge(unit_done, s + per * t - SPLIT_SLOTS + 1)
                act.activation(whi[:, s % SPLIT_SLOTS, :], stage[:, s % STAGE_SLOTS, :], ACT.Copy)\
                   .then_inc(hi_ready, 1)

            def split_ahead(b, per, t, q):
                if not isinstance(t, int) or b + per * t + q + LOOKAHEAD < UNITS:
                    split(b, per, t, q + LOOKAHEAD)

            def square(k, m, slot):
                act.wait_ge(x_ready, KD * k + m + 1)
                if not isinstance(m, int) or m >= 2 or k:
                    act.wait_ge(ssum_added, KD * k + m - 1)
                act.activation(tmp[:, slot, :], tile(xT, m), ACT.Square).then_inc(sq_ready, 1)
                if k < LAST_NORM:
                    act.activation(tile(hh, m), tile(xT, m), ACT.Copy, scale=prm[:, bass.ds(m + NORM_PRM[k], 1)])\
                       .then_inc(h_hi, 1)

            def norm(k):
                act.preload_act_table(ACT.Ln)
                act.wait_ge(norm_sum, k + 1)
                act.activation(two(rstd[:]), pair(3), ACT.Ln, scale=1.0 / DM, bias=EPS)\
                   .then_inc(ln_ready, 1)
                act.wait_ge(ln_ready, k + 1)
                act.activation(rstd[:], rstd[:], ACT.Exp, scale=-0.5).then_inc(rstd_ready, 1)
                if k < LAST_NORM and STAGES[k][0] != "mix_o":
                    act.preload_act_table(ACT.Silu)

            def ffn_in(s, f):
                b = FIRST[f"in{f}"]
                before_it = STAGES[s - 1][0] if s else None
                if before_it == "mix_e":
                    act.wait_ge(e_stored, 16 * E_STORES)
                elif before_it == "mix_o":
                    act.wait_ge(o_stored, 16 * O_STORES)

                def body(t):
                    for a in range(2):
                        n = KF * f + 2 * t + a
                        split_ahead(b, 4, t, 2 * a)
                        act.wait_ge(gate_read, n + 1)
                        act.activation(tmp[:, a, :], tmp[:, a, :], ACT.Silu).then_inc(gate_ready, 1)
                        split_ahead(b, 4, t, 2 * a + 1)
                        act.wait_ge(prod_ready, n + 1)
                        act.activation(act_h[:, bass.ds(2 * t + a, 1), :].rearrange("p a b -> p (a b)"),
                                       tmp[:, 2 + a, :], ACT.Copy).then_inc(act_hi, 1)
                body(0)
                loop(act, 1, KF // 2, body)

            def ffn_down(s, f):
                b = FIRST[f"down{f}"]

                def body(t):
                    for a in range(4):
                        for c in range(PARTS):
                            split_ahead(b, 4 * PARTS, t, PARTS * a + c)
                        square(s + 1, 4 * t + a, a % 2)
                if s + 1 == LAST_NORM:
                    for t in range(KD // 4):
                        body(t)
                else:
                    loop(act, 0, KD // 4, body)

            chain = [0]

            def link(ins):
                chain[0] += 1
                ins.then_inc(act_chain, 1)
                act.wait_ge(act_chain, chain[0])

            def out_proj(s, name):
                b = FIRST[name]

                def body(t):
                    for a in range(4):
                        split_ahead(b, 4, t, a)
                        square(s + 1, 4 * t + a, a % 2)
                loop(act, 0, KD // 4, body)

            def project_e():
                b = FIRST["mix_e0"]
                split_ahead(b, 4, 0, 0)

                def silu(n, slot):
                    act.wait_ge(conv_step, 8 * (n + 1))
                    act.activation(prE[:, bass.ds(n, 1), :].rearrange("p a b -> p (a b)"), tmp[:, slot, :], ACT.Silu)\
                       .then_inc(silu_e, 1)

                def body(t):
                    for q in range(4):
                        n = 4 * t + q
                        first = isinstance(t, int) and t == 0
                        split_ahead(b + 1, 4, t, q)
                        if not first or q:
                            silu(n - 1, (q + 1) % 2)
                body(0)
                loop(act, 1, QKV // 4, body)
                silu(QKV - 1, 1)
                for n in range(QKV, E_TILES):
                    split_ahead(b + 1, 4, 0, n)
                    if n == GATES_AT:
                        gdn_gates()
                    if n == GATES_AT + 1:
                        gla_gates()
                    if L2_AT <= n < L2_AT + HB:
                        l2_e(2 * (n - L2_AT))
                    if n >= GLA_AT:
                        c = (n - GLA_AT) // 2
                        (gla_odd if (n - GLA_AT) % 2 else gla_even)(c)

            def softplus_abs(dst, src, bias):
                link(act.activation(dst, src, ACT.Abs, bias=bias))
                link(act.activation(dst, dst, ACT.Exp, scale=-1.0))
                return act.activation(dst, dst, ACT.Ln, bias=1.0)

            def gdn_gates():
                act.wait_ge(pe_read, 1)
                act.wait_ge(silu_e, QKV)
                act.activation(small[64:64 + HB, :], small[64:64 + HB, :], ACT.Sigmoid).then_inc(gates, 1)
                act.preload_act_table_set(LN_EXP)
                act.wait_ge(e_loaded, 64)
                r = slice(32, 32 + HB)
                softplus_abs(tmp[r, 3, :], small[r, :], gdnp[r, 0:1]).then_inc(gdn_sp, 1)
                act.activation(gdnp[r, 2:3], gdnp[r, 1:2], ACT.Exp).then_inc(gdn_sp, 1)

            def gla_gates():
                act.wait_ge(gla_z, 1)
                for h in range(HP):
                    softplus_abs(two(tmp[:, h, :]), pair(h), col("gla_b_gate", h)).then_inc(gla_sp, 1)

            def unit_norm(n, src):
                if n >= 2:
                    act.wait_ge(hn_sum, n - 1)
                act.activation(tmp[:, n % 2, :], src, ACT.Square).then_inc(hn_sq, 1)

            def unit_rn(n, scale):
                act.wait_ge(hn_sum, n + 1)
                if n >= 2:
                    act.wait_ge(hn_done, n - 1)
                link(act.activation(two(tmp[:, 2 + n % 2, :]), pair(n % 2), ACT.Ln, scale=scale, bias=EPS))
                act.activation(tmp[:, 2 + n % 2, :], tmp[:, 2 + n % 2, :], ACT.Exp, scale=-0.5).then_inc(hn_rn, 1)

            def l2_e(n):
                act.wait_ge(gla_r, 2 * HP)
                for m in (n, n + 1):
                    unit_norm(m, prE[:, m, :])
                for m in (n, n + 1):
                    unit_rn(m, 1.0)

            def gla_even(c):
                if c:
                    act.wait_ge(ga_vt, c)
                    act.activation(vtA[:].rearrange("p a b -> p (a b)"), banks(2, 1), ACT.Copy).then_inc(ga_vtc, 1)
                    act.wait_ge(ga_att, c)
                    act.activation(attT[:].rearrange("p a b t -> p a (b t)"), PS[:, 0:2, 0:HP * P], ACT.Copy)\
                       .then_inc(ga_attc, 1)
                    act.wait_ge(ga_kdt, c)
                    act.activation(kdtA[:].rearrange("p a b -> p (a b)"), banks(3, 1)[:, 0:HP * P], ACT.Copy)\
                       .then_inc(ga_kdtc, 1)
                if c < NB:
                    act.wait_ge(ga_dif, c + 1)
                    act.activation(dq[:], dq[:], ACT.Exp, scale=1.0 / GLA_TAU)
                    act.activation(dkA[:], dkA[:], ACT.Exp, scale=-1.0 / GLA_TAU)
                    act.activation(kdA[:], kdA[:], ACT.Exp, scale=-1.0 / GLA_TAU).then_inc(ga_fac, 1)

            def gla_odd(c):
                if c:
                    act.wait_ge(ga_o, c)
                    act.activation(prE[:, AV:AV + HA, (c - 1) * P:c * P].rearrange("p (h q) t -> p q h t", q=2),
                                   PS[:, 4:6, 0:HP * P].rearrange("p q (h t) -> p q h t", h=HP), ACT.Copy)\
                       .then_inc(ga_oc, 1)
                if c == 0:
                    act.activation(egA[:], gG[:, :, TP:TOK], ACT.Exp, scale=1.0 / GLA_TAU).then_inc(sa_eg, 1)
                if c < NB:
                    if c:
                        act.wait_ge(ga_sc, c)
                    act.activation(eA[:], gG[:, :, c * P:(c + 1) * P], ACT.Exp, scale=1.0 / GLA_TAU).then_inc(ga_exp, 1)

            def silu_gates():
                act.wait_ge(pe_read, E_TILES + 1)
                for n in range(AR, E_TILES, 4):
                    act.activation(prE[:, n:n + 4, :], prE[:, n:n + 4, :], ACT.Silu)

            def gdn_decays(c):
                act.wait_ge(gb_dif, c + 1)
                act.activation(dif[:], dif[:], ACT.Exp).then_inc(gb_rel, 1)
                act.activation(colS[:, 0, :], colGB[:, c, 32:32 + HB], ACT.Exp)
                act.activation(colS[:, 3, :], colS[:, 2, :], ACT.Exp).then_inc(gb_c1, 1)

            def gdn(c):
                t = slice(c * P, (c + 1) * P)
                act.wait_ge(gb_d0, c + 1)
                act.activation(Dm[:].rearrange("p a b -> p (a b)"), banks(6, 1), ACT.Copy).then_inc(gb_d0c, 1)
                if c:
                    act.wait_ge(gb_sc, c)
                act.activation(EG[:].rearrange("p a b -> p (a b)"), banks(0, 1), ACT.Exp).then_inc(gb_eg, 1)
                act.wait_ge(gb_kv, c + 1)
                act.wait_ge(gb_c1, c + 1)
                for h in range(HB):
                    kt = banks(4, 1)[:, h * P:(h + 1) * P]
                    last = act.activation(kdB[:, h, :], kt, ACT.Copy, scale=colS[:, 3, h:h + 1])
                last.then_inc(gb_ks, 1)
                for l in range(LEVELS):
                    for a in range(2):
                        act.wait_ge(gb_t1, 2 * (LEVELS * c + l) + a + 1)
                        act.activation(T1[:, HB // 2 * a:HB // 2 * (a + 1), :].rearrange("p h t -> p (h t)"),
                                       banks(4 * a, 1)[:, 0:HB // 2 * P], ACT.Copy).then_inc(gb_t1c, 1)
                    update_products(LEVELS * c + l)
                    if c == 0 and l == 0:
                        silu_gates()
                act.wait_ge(gb_vn, c + 1)
                act.activation(T1[:].rearrange("p a b -> p (a b)"), banks(7, 1), ACT.Copy, scale=-1.0)\
                   .then_inc(gb_vnc, 1)
                if c < NB - 1:
                    gdn_decays(c + 1)
                act.wait_ge(gb_o, c + 1)
                act.activation(prE[:, BV:BV + HB, t], banks(4, 1).rearrange("p (h t) -> p h t", h=HB), ACT.Copy)\
                   .then_inc(gb_oc, 1)

            def samples_e():
                s = slice(TP, TOK)
                act.wait_ge(sa_bc, 1)
                act.activation(egS[:], banks(6, 1).rearrange("p (h t) -> p h t", h=HB)[:, :, P - TS:P], ACT.Exp)\
                   .then_inc(sa_eg, 1)
                act.wait_ge(sa_ks, 1)
                act.activation(kqR[:], banks(0, 1)[0:2 * HB * TS, 0:DV], ACT.Copy).then_inc(sa_ksc, 1)
                act.wait_ge(sa_ks, 2)
                act.activation(qaR[:], banks(1, 1)[0:HA * TS, 0:DV], ACT.Copy).then_inc(sa_ksc, 1)
                act.wait_ge(sa_r, 1)
                act.activation(vaR[:].rearrange("p a b -> p (a b)"), banks(1, 1)[0:TS, :], ACT.Copy).then_inc(sa_rc, 1)
                act.wait_ge(sa_r, 2)
                act.activation(vnR[:], banks(0, 1)[0:HB * TS, 0:DV], ACT.Copy).then_inc(sa_rc, 1)

            def update_products(j):
                act.wait_ge(sa_b, j + 1)
                for e in range(2):
                    n = 2 * j + e
                    if n >= 4:
                        act.wait_ge(sa_st, n - 3)
                    k = AK + e if j < STEPS_A else BK + (n - 2 * STEPS_A) // TS
                    b = TP + (j if j < STEPS_A else (n - 2 * STEPS_A) % TS)
                    act.activation(kvS[:, n % 4, :], banks(7 if j % 2 else 3, 1)[:, e * P:(e + 1) * P], ACT.Copy,
                                   scale=prE[:, k, b:b + 1]).then_inc(sa_kv, 1)

            def out_norm_e():
                act.wait_ge(tail_stored, 32)
                act.preload_act_table_set(LN_EXP)
                act.wait_ge(sa_o, 2)
                act.wait_ge(ga_oc, NB)
                act.wait_ge(gb_oc, NB)
                for n in range(HA + HB + 2):
                    if n < HA + HB:
                        unit_norm(2 * HB + n, prE[:, AV + n if n < HA else BV + n - HA, :])
                    if 1 <= n <= HA + HB:
                        unit_rn(2 * HB + n - 1, 1.0 / DV)
                    if n >= 2:
                        m = n - 2
                        act.wait_ge(hn_done, 2 * HB + m + 1)
                        act.activation(oE[:, AR + m, :], prE[:, AV + m if m < HA else BV + m - HA, :], ACT.Copy)\
                           .then_inc(o_hi, 1)

            def project_o():
                b = FIRST["mix_o0"]
                for n in range(O_TILES):
                    split_ahead(b, 4, 0, n)
                    if 1 <= n <= KR:
                        act.wait_ge(conv_step_o, 8 * n)
                        act.activation(prO[:, OX + n - 1, :], tmp[:, (n - 1) % 2, :], ACT.Identity,
                                       bias=col("rg_conv_b", n - 1)).then_inc(xo_ready, 1)
                    if n == KR + 1:
                        softplus_abs(cc[:, 2, :], prm[:, PRM["rg_lambda"]:PRM["rg_lambda"] + KR], 0.0)\
                            .then_inc(rg_c1, 1)
                    if n >= 2 * KR and (n - 2 * KR) % 3 == 0:
                        rg_gates((n - 2 * KR) // 3)
                    if n >= 2 * KR and (n - 2 * KR) % 3 == 1:
                        rg_mult_root((n - 2 * KR) // 3)

            def rg_gates(m):
                act.wait_ge(rg_z, m + 1)
                act.activation(two(rgR[:, m, :]), pair(2), ACT.Sigmoid, bias=col("rg_b_a", m)).then_inc(rg_sig, 1)
                act.activation(two(rgI[:, m, :]), pair(3), ACT.Sigmoid, bias=col("rg_b_x", m)).then_inc(rg_sig, 1)
                act.wait_ge(rg_u, m + 1)
                act.activation(tmp[:, 2 + m % 2, :], tmp[:, 2 + m % 2, :], ACT.Tanh, scale=(2 / 3.141592653589793) ** 0.5)\
                   .then_inc(rg_a, 1)
                act.wait_ge(rg_sig, 2 * m + 1)
                act.wait_ge(rg_c2, 2)
                act.activation(rgT[:, m, :], rgR[:, m, :], ACT.Tanh, scale=cc[:, 1, m:m + 1]).then_inc(rg_a, 1)
                act.activation(rgA[:, m, :], rgR[:, m, :], ACT.Exp, scale=cc[:, 0, m:m + 1]).then_inc(rg_a, 1)

            def rg_mult_root(m):
                act.preload_act_table_set(LN_EXP)
                act.wait_ge(rg_m, m + 1)
                link(act.activation(rgR[:, m, :], rgR[:, m, :], ACT.Ln, bias=1e-37))
                act.activation(rgR[:, m, :], rgR[:, m, :], ACT.Exp, scale=0.5).then_inc(rg_mult, 1)

            def rows_o():
                act.wait_ge(rg_od, KR)
                for n in range(NB):
                    act.wait_ge(kv_t, NB + n + 1)
                    act.activation(ktok[:, n, :], banks(4 + n, 1), ACT.Copy).then_inc(k_rows, 1)
                for n, rows in enumerate((1 + TS, TAIL)):
                    act.wait_ge(row_t, 4 + n)
                    act.activation(rowX[0:rows, n, :], banks(3 + n, 1)[0:rows, :], ACT.Copy).then_inc(k_rows, 1)

            def stick():
                z = banks(0, 3)[:, 0:SCORES]
                act.preload_act_table_set(LN_EXP)
                act.wait_ge(rg_c2, 2)
                for h in range(HC + 2):
                    if h < HC:
                        act.wait_ge(sk_z, h + 1)
                        if h >= 2:
                            act.wait_ge(sk_acc, h - 1)
                        act.activation(skX[:, h % 2, :], z, ACT.Relu, bias=sbb[:, 0, h:h + 1])
                        if h >= 3:
                            act.wait_ge(sk_o, h - 2)
                        act.activation(skY[:, h % 3, :], z, ACT.Relu, scale=-1.0, bias=sbb[:, 1, h:h + 1])
                        if h:
                            act.wait_ge(sk_added, h)
                        act.activation(skL[:], z, ACT.Abs, bias=sbb[:, 0, h:h + 1]).then_inc(sk_read, 1)
                        act.wait_ge(sk_read, h + 1)
                        link(act.activation(skL[:], skL[:], ACT.Exp, scale=-1.0))
                        act.activation(skL[:], skL[:], ACT.Ln, bias=1.0).then_inc(sk_ln, 1)
                    if 1 <= h <= HC:
                        act.wait_ge(sk_add, h)
                        a = (h - 1) % 3
                        act.activation(skY[:, a, :], skY[:, a, :], ACT.Exp, scale=-1.0).then_inc(sk_w, 1)
                    if h >= 2:
                        n = h - 2
                        r = slice(n % 2 * HDC, (n % 2 + 1) * HDC)
                        act.wait_ge(sk_o, n + 1)
                        act.activation(prO[r, OQ + n // 2, 0:TP], banks(6, 1)[r, :], ACT.Copy).then_inc(sk_oc, 1)

            def samples_o():
                def flat(n):
                    return smS[:, n].rearrange("p a b h -> p (a b h)")
                act.wait_ge(sm_step, 1)
                softplus_abs(flat(1), flat(0), 0.0).then_inc(sm_ln, 1)
                act.wait_ge(sm_step, 3)
                act.wait_ge(o_consts, 10 + TS)
                for p in range(PAGES):
                    blocks = smW[:, p].rearrange("p a b h -> p (a b h)")
                    step = (TS + 1) * HC
                    for b in range(TS):
                        last = act.activation(blocks[:, b * step:b * step + HC], smS[:, 2, p, b, :], ACT.Exp)
                last.then_inc(sm_w, 1)
                act.wait_ge(sm_sum, 2)
                act.activation(prO[:, OQ:OQ + KC, TP:TOK], banks(5, 1)[:, 0:KC * TS].rearrange("p (m b) -> p m b", m=KC),
                               ACT.Copy).then_inc(sm_oc, 1)
                act.wait_ge(sm_oc, 1)
                act.wait_ge(sk_oc, HC)
                act.wait_ge(rg_od, KR)
                for m in range(KC + KR):
                    act.activation(oO[:, OK + m if m < KC else OX + m - KC, :],
                                   prO[:, OQ + m if m < KC else OY + m - KC, :], ACT.Copy).then_inc(o_hi, 1)

            for b in range(NB):
                act.dma_start(xrow[:, b, :], i["x_prompt"][0, b * P:(b + 1) * P, :]).then_inc(x_loaded, 16)
            act.dma_start(xsrow[:], i["x_sample"][:, 0, :]).then_inc(x_loaded, 16)
            for dst, group, first in ((prow_a, ROWS_A, 0), (prow_b, ROWS_B, NA)):
                for name, n in group:
                    r = PRM[name] - first
                    act.dma_start(dst[r:r + n, :], rows(i[name])).then_inc(p_loaded, 16)
            act.dma_start(hrow_g[:], i["state_gdn_conv"][0].rearrange("b w n -> (b w) n")).then_inc(s_loaded, 16)
            act.dma_start(hrow_r[:], i["state_rg_conv"][0].rearrange("b w n -> (b w) n")).then_inc(s_loaded, 16)
            act.dma_start(hrow_0[:], i["state_rg_h"][0]).then_inc(s_loaded, 16)
            for u in range(LOOKAHEAD):
                split(u, 4, 0, 0)
            act.wait_ge(prm_ready, 2)
            for m in range(KD):
                act.wait_ge(setup_t, 3 + m)
                act.activation(xT[:, m, 0:TP], banks(m % 4, 1), ACT.Copy).then_inc(x_ready, 1)
                square(0, m, m % 2)
            for s, (name, f) in enumerate(STAGES):
                norm(s)
                if name == "ffn":
                    ffn_in(s, f)
                    ffn_down(s, f)
                elif name == "mix_e":
                    project_e()
                    samples_e()
                    gdn_decays(0)
                    for c in range(NB):
                        gdn(c)
                    out_norm_e()
                    out_proj(s, "out_e0")
                elif name == "mix_o":
                    project_o()
                    rows_o()
                    stick()
                    samples_o()
                    out_proj(s, "out_o0")
            norm(LAST_NORM)
            for m in range(KD):
                act.wait_ge(y_t, m + 1)
                act.activation(yrow[:, :, m * P:(m + 1) * P], banks(m % 4, 1).rearrange("p (b n) -> p b n", b=NB), ACT.Copy)\
                   .then_inc(y_row, 1)
            for a in range(2):
                act.activation(ysrow[:, a * 512:(a + 1) * 512], banks(4 + a, 1)[0:TS, :], ACT.Copy).then_inc(y_row, 1)

        @block.vector
        def _(dve):
            def split(b, per, t, q):
                s = b + q
                slot = s % SPLIT_SLOTS
                dve.wait_ge(hi_ready, s + per * t + 1)
                if not isinstance(t, int) or s + per * t >= SPLIT_SLOTS:
                    dve.wait_ge(unit_done, s + per * t - SPLIT_SLOTS + 1)
                dve.tensor_tensor(wlo[:, slot, :], stage[:, s % STAGE_SLOTS, :], whi[:, slot, :].bitcast(F32),
                                  ALU.subtract).then_inc(lo_ready, 1)

            def split_ahead(b, per, t, q):
                if not isinstance(t, int) or b + per * t + q + LOOKAHEAD < UNITS:
                    split(b, per, t, q + LOOKAHEAD)

            def zero_sum(k):
                if k:
                    dve.wait_ge(norm_sum, k)
                dve.memset(ssum[:], 0.0).then_inc(ssum_zero, 1)

            def add_square(k, m, slot):
                if k < LAST_NORM:
                    dve.wait_ge(h_hi, KD * k + m + 1)
                    dve.scalar_tensor_tensor(out=tile(hl, m), in0=tile(xT, m), scalar=prm[:, bass.ds(m + NORM_PRM[k], 1)],
                                             in1=tile(hh, m).bitcast(F32), op0=ALU.mult, op1=ALU.subtract)\
                       .then_inc(h_lo, 1)
                dve.wait_ge(sq_ready, KD * k + m + 1)
                dve.wait_ge(ssum_zero, k + 1)
                if not isinstance(m, int) or m or k:
                    dve.wait_ge(ssum_added, KD * k + m)
                dve.tensor_tensor(ssum[:], ssum[:], tmp[:, slot, :], ALU.add).then_inc(ssum_added, 1)

            def last_norm():
                g = NORM_PRM[LAST_NORM]
                dve.wait_ge(rstd_ready, LAST_NORM + 1)
                for m in range(KD):
                    if m >= 4:
                        dve.wait_ge(y_t, m - 3)
                    dve.scalar_tensor_tensor(out=tmp[:, m % 4, :], in0=xT[:, m, :], scalar=prm[:, g + m:g + m + 1],
                                             in1=rstd[:], op0=ALU.mult, op1=ALU.mult).then_inc(y_ready, 1)

            def take(dst, psum, scale=1.0):
                return dve.scalar_tensor_tensor(out=dst, in0=psum, scalar=scale, in1=two(rstd[:]), op0=ALU.mult,
                                                op1=ALU.mult)

            def ffn_in(s, f):
                b = FIRST[f"in{f}"]

                def body(t):
                    for a in range(2):
                        n = KF * f + 2 * t + a
                        first = isinstance(t, int) and t == 0
                        split_ahead(b, 4, t, 2 * a)
                        dve.wait_ge(unit_done, b + 4 * t + 2 * a + 1)
                        if first:
                            dve.wait_ge(rstd_ready, s + 1)
                            dve.wait_ge(ssum_added, KD * (s + 1))
                        else:
                            dve.wait_ge(prod_ready, n - 1)
                        take(two(tmp[:, a, :]), pair(2 * a)).then_inc(gate_read, 1)
                        split_ahead(b, 4, t, 2 * a + 1)
                        dve.wait_ge(unit_done, b + 4 * t + 2 * a + 2)
                        if not first or n >= 2:
                            dve.wait_ge(act_lo, n - 1)
                        take(two(tmp[:, 2 + a, :]), pair(2 * a + 1)).then_inc(up_read, 1)
                        dve.wait_ge(up_read, n + 1)
                        dve.wait_ge(gate_ready, n + 1)
                        dve.tensor_tensor(tmp[:, 2 + a, :], tmp[:, a, :], tmp[:, 2 + a, :], ALU.mult)\
                           .then_inc(prod_ready, 1)
                        dve.wait_ge(act_hi, n + 1)
                        dve.tensor_tensor(tile(act_l, 2 * t + a), tmp[:, 2 + a, :],
                                          tile(act_h, 2 * t + a).bitcast(F32), ALU.subtract).then_inc(act_lo, 1)
                    if first:
                        zero_sum(s + 1)
                body(0)
                loop(dve, 1, KF // 2, body)

            def update(s, m, done, psum, scale):
                dve.wait_ge(unit_done, done)
                x = xT[:, bass.ds(m, 1), :].rearrange("p a (b c) -> p (a b) c", b=2)
                dve.scalar_tensor_tensor(out=x, in0=psum, scalar=scale, in1=x, op0=ALU.mult, op1=ALU.add)\
                   .then_inc(x_ready, 1)

            def ffn_down(s, f):
                b = FIRST[f"down{f}"]

                def body(t):
                    for a in range(4):
                        for c in range(PARTS):
                            split_ahead(b, 4 * PARTS, t, PARTS * a + c)
                        update(s, 4 * t + a, b + 4 * PARTS * t + PARTS * (a + 1), pair(a), 0.5)
                        add_square(s + 1, 4 * t + a, a % 2)
                if s + 1 == LAST_NORM:
                    for t in range(KD // 4):
                        body(t)
                else:
                    loop(dve, 0, KD // 4, body)

            chain = [0]

            def link(ins):
                chain[0] += 1
                ins.then_inc(dve_chain, 1)
                dve.wait_ge(dve_chain, chain[0])

            def out_proj(s, name):
                b = FIRST[name]

                def body(t):
                    for a in range(4):
                        split_ahead(b, 4, t, a)
                        update(s, 4 * t + a, b + 4 * t + a + 1, pair((a + 2) % 4), 1.0)
                        add_square(s + 1, 4 * t + a, a % 2)
                loop(dve, 0, KD // 4, body)

            def conv(n, slot, raw, hist, wcol, tail, done, step, step_n, cstep):
                def w(k):
                    return prm[:, bass.ds(wcol(k, n), 1)]
                y = tmp[:, slot, :]
                dve.wait_ge(done, step)
                dve.tensor_scalar(y, raw[:, slot, CW - 1:CW - 1 + TOK], w(CW - 1), None, ALU.mult).then_inc(cstep, 1)
                for k in range(CW - 1):
                    dve.wait_ge(cstep, step_n + (1 if k == 0 else 2 * k))
                    dve.scalar_tensor_tensor(out=y[:, 0:TP], in0=raw[:, slot, k:k + TP], scalar=w(k), in1=y[:, 0:TP],
                                             op0=ALU.mult, op1=ALU.add).then_inc(cstep, 1)
                    if k:
                        dve.wait_ge(cstep, step_n + 2 * k + 1)
                    past = hist[:, bass.ds(n, 1), :, k].rearrange("p a b -> p (a b)")
                    dve.scalar_tensor_tensor(out=y[:, TP:TOK], in0=past, scalar=w(k), in1=y[:, TP:TOK],
                                             op0=ALU.mult, op1=ALU.add).then_inc(cstep, 1)
                dve.tensor_copy(tail[:, bass.ds(n, 1), :].rearrange("p a b -> p (a b)"),
                                raw[:, slot, TP:TP + TAIL]).then_inc(cstep, 1)

            def project_e(s):
                b = FIRST["mix_e0"]
                split_ahead(b, 4, 0, 0)
                dve.memset(rawE[:, :, 0:CW - 1], 0.0).then_inc(e_free, 1)
                dve.wait_ge(e_free, 1)
                dve.wait_ge(unit_done, b + 1)
                dve.wait_ge(rstd_ready, s + 1)
                dve.scalar_tensor_tensor(out=two(small[:]), in0=pair(2)[0:96], scalar=1.0, in1=two(rstd[0:96, :]),
                                         op0=ALU.mult, op1=ALU.mult).then_inc(pe_read, 1)

                def body(t):
                    for q in range(4):
                        n = 4 * t + q
                        split_ahead(b + 1, 4, t, q)
                        dve.wait_ge(unit_done, b + 2 + 4 * t + q)
                        if isinstance(t, int) and t == 0 and q < 2:
                            dve.wait_ge(ssum_added, KD * (s + 1))
                        else:
                            dve.wait_ge(conv_step, 8 * (n - 1))
                            dve.wait_ge(silu_e, n - 1)
                        take(two(rawE[:, q % 2, CW - 1:CW - 1 + TOK]), pair(q)).then_inc(pe_read, 1)
                        conv(n, q % 2, rawE, histG, lambda k, n: PRM["gdn_conv_w"] + k * QKV + n, tailE,
                             pe_read, n + 2, 8 * n, conv_step)
                body(0)
                zero_sum(s + 1)
                loop(dve, 1, QKV // 4, body)
                for n in range(QKV, E_TILES):
                    split_ahead(b + 1, 4, 0, n)
                    dve.wait_ge(unit_done, b + 2 + n)
                    take(two(prE[:, n, :]), pair(tile_pair(n)), DKA ** -0.5 if n < AK else 1.0).then_inc(pe_read, 1)
                    if n == GATES_AT:
                        gdn_gates()
                    if n == GATES_AT + 1:
                        gla_gates()
                    if L2_AT <= n < L2_AT + HB:
                        l2_e(2 * (n - L2_AT))
                    if n >= GLA_AT:
                        c = (n - GLA_AT) // 2
                        (gla_odd if (n - GLA_AT) % 2 else gla_even)(c)

            def gdn_gates():
                dve.wait_ge(e_loaded, 64)
                r = slice(32, 32 + HB)
                dve.wait_ge(pe_read, 1)
                dve.wait_ge(gdn_sp, 2)
                link(dve.tensor_scalar(small[r, :], small[r, :], gdnp[r, 0:1], 0.0, ALU.add, ALU.max))
                g = tmp[r, 3, :]
                link(dve.tensor_tensor(g, g, small[r, :], ALU.add))
                link(dve.tensor_scalar(g, g, gdnp[r, 2:3], -1.0, ALU.mult, ALU.mult))
                for c in range(NB):
                    t = slice(c * P, (c + 1) * P)
                    dve.tensor_tensor_scan(small[r, t], ones[r, :], g[:, t], 0.0, ALU.mult, ALU.add)
                dve.tensor_copy(small[r, TP:TOK], g[:, TP:TOK]).then_inc(gates, 1)
                dve.wait_ge(gates, 2)

            def gla_gates():
                dve.wait_ge(silu_e, QKV)
                for h in range(HP):
                    dve.wait_ge(gla_sp, h + 1)
                    link(dve.tensor_scalar(two(tmp[:, 2 + h, :]), pair(h), col("gla_b_gate", h), 0.0, ALU.add, ALU.min))
                    dve.tensor_tensor(tmp[:, 2 + h, :], tmp[:, 2 + h, :], tmp[:, h, :], ALU.subtract).then_inc(gla_r, 1)
                    dve.wait_ge(gla_r, 2 * h + 1)
                    for c in range(NB):
                        t = slice(c * P, (c + 1) * P)
                        dve.tensor_tensor_scan(gG[:, h, t], ones[:], tmp[:, 2 + h, t], 0.0, ALU.mult, ALU.add)
                    dve.tensor_copy(gG[:, h, TP:TOK], tmp[:, 2 + h, TP:TOK]).then_inc(gla_r, 1)

            def l2_e(n):
                for m in (n, n + 1):
                    dve.wait_ge(hn_rn, m + 1)
                    dve.scalar_tensor_tensor(out=prE[:, m, :], in0=prE[:, m, :], scalar=P ** -0.5 if m < HB else 1.0,
                                             in1=tmp[:, 2 + m % 2, :], op0=ALU.mult, op1=ALU.mult).then_inc(hn_done, 1)

            def turned_e():
                dve.wait_ge(col_t, 1)
                dve.tensor_copy(colGB[:], banks(7, 1)[:, 0:NB * 96].rearrange("p (c r) -> p c r", c=NB))\
                   .then_inc(col_ready, 1)
                dve.wait_ge(col_t, 2)
                dve.wait_ge(hn_done, 2 * HB)
                for n in range(3):
                    dve.tensor_copy(tmp[0:TAIL, :, :].rearrange("p a b -> p (a b)")[:, n * 512:(n + 1) * 512],
                                    banks(4 + n, 1)[0:TAIL, :]).then_inc(tail_row, 1)

            def gla_even(c):
                if c == NB:
                    return
                t = slice(c * P, (c + 1) * P)
                lim = CLAMP * GLA_TAU
                if c:
                    dve.wait_ge(ga_fac2, 4 * c)
                    dve.wait_ge(ga_att, c)
                    dve.wait_ge(ga_kdt, c)
                for h in range(HP):
                    for j in range(4):
                        mid = gG[:, h, c * P + 32 * j + 15:c * P + 32 * j + 16]
                        dve.tensor_scalar(dq[:, h, j, :], gG[:, h, t], mid, lim, ALU.subtract, ALU.min)
                        dve.tensor_scalar(dkA[:, h, 32 * j:32 * j + 32], gG[:, h, c * P + 32 * j:c * P + 32 * j + 32],
                                          mid, -lim, ALU.subtract, ALU.max)
                    end = gG[:, h, c * P + P - 1:c * P + P]
                    last = dve.tensor_scalar(kdA[:, h, :], gG[:, h, t], end, None, ALU.subtract)
                last.then_inc(ga_dif, 1)

            def gla_odd(c):
                if c:
                    dve.wait_ge(ga_s, c)
                    for h in range(HP):
                        last = dve.scalar_tensor_tensor(out=stA[:, h, :], in0=stA[:, h, :], scalar=eA[:, h, P - 1:P],
                                                        in1=banks(3, 1)[:, HP * P + h * DV:HP * P + (h + 1) * DV],
                                                        op0=ALU.mult, op1=ALU.add)
                    last.then_inc(ga_sc, 1)
                if c == NB:
                    return
                t = slice(c * P, (c + 1) * P)
                dve.wait_ge(ga_fac, c + 1)
                dve.wait_ge(ga_exp, c + 1)
                if c:
                    dve.wait_ge(ga_o, c)
                for h in range(HP):
                    q = prE[:, AQ + h:AQ + h + 1, t]
                    k = prE[:, AK + h, t]
                    dve.tensor_tensor(dq[:, h], dq[:, h], q.to_broadcast([P, 4, P]), ALU.mult)
                    dve.tensor_tensor(dkA[:, h, :], dkA[:, h, :], k, ALU.mult).then_inc(ga_fac2, 1)
                    dve.tensor_tensor(kdA[:, h, :], kdA[:, h, :], k, ALU.mult)
                    dve.tensor_tensor(qgA[:, h, :], eA[:, h, :], prE[:, AQ + h, t], ALU.mult).then_inc(ga_fac2, 1)

            def over(m):
                return m.rearrange("p (a t) -> p a t", a=1)

            def gdn_decays(c):
                G = banks(0, 1).rearrange("p (h t) -> p h t", h=HB)
                dve.wait_ge(gb_bc, c + 1)
                for h in range(HB):
                    dve.tensor_scalar(dif[:, h, :], G[:, h, :], colGB[:, c, 32 + h:33 + h], 0.0, ALU.subtract, ALU.min)
                dve.tensor_tensor(colS[:, 2, :], G[:, :, P - 1], colGB[:, c, 32:32 + HB], ALU.subtract).then_inc(gb_dif, 1)
                dve.tensor_tensor(Lt[:], banks(1, 1).rearrange("p (h t) -> p h t", h=HB),
                                  over(strict[:]).to_broadcast([P, HB, P]), ALU.mult)
                dve.wait_ge(gb_rel, c + 1)
                link(dve.tensor_tensor(dif[:], dif[:], over(keep[:]).to_broadcast([P, HB, P]), ALU.mult))
                dve.wait_ge(gb_kq, c + 1)
                link(dve.tensor_tensor(Dm[:], banks(2, 1).rearrange("p (h t) -> p h t", h=HB), dif[:], ALU.mult))
                link(dve.tensor_tensor(Lt[:], Lt[:], Dm[:], ALU.mult))
                if c:
                    dve.wait_ge(gb_vn, c)
                link(dve.tensor_tensor(DT[:], Lt[:], over(masks[:, 0, :]).to_broadcast([P, HB, P]), ALU.mult))
                dve.tensor_tensor(DT[:], over(ident[:]).to_broadcast([P, HB, P]), DT[:], ALU.subtract).then_inc(gb_dt0, 1)

            def gdn(c):
                t = slice(c * P, (c + 1) * P)
                bank = lambda n: banks(n, 1).rearrange("p (h t) -> p h t", h=HB)
                beta = colGB[:, c, 64:64 + HB]
                dve.wait_ge(gb_c1, c + 1)
                dve.tensor_tensor(colS[:, 1, :], colS[:, 0, :], beta, ALU.mult)
                if c:
                    dve.wait_ge(gb_o, c)
                dve.tensor_tensor(QKr[:], bank(3), dif[:], ALU.mult).then_inc(gb_qkr, 1)
                dve.wait_ge(gb_kv, c + 1)
                for h in range(HB):
                    last = dve.tensor_scalar(vbB[:, h, :], bank(5)[:, h, :], beta[:, h:h + 1], None, ALU.mult)
                link(last)
                dve.wait_ge(gb_wt, c + 1)
                for h in range(HB):
                    last = dve.scalar_tensor_tensor(out=vbB[:, h, :], in0=bank(7)[:, h, :], scalar=colS[:, 1, h:h + 1],
                                                    in1=vbB[:, h, :], op0=ALU.mult, op1=ALU.subtract)
                last.then_inc(gb_vb, 1)
                dve.wait_ge(gb_eg, c + 1)
                dve.tensor_tensor(qgB[:], EG[:], prE[:, BQ:BQ + HB, t], ALU.mult).then_inc(gb_qg, 1)
                n2 = HB // 2
                for l in range(1, 7):
                    e = 12 * c + 2 * (l - 1)
                    for a in range(2):
                        hs = slice(n2 * a, n2 * (a + 1))
                        dve.wait_ge(gb_dd, e + a + 1)
                        if l < 6:
                            part = banks(4 * a + 1, 1)[:, 0:n2 * P].rearrange("p (h t) -> p h t", h=n2)
                            dve.tensor_tensor(Dm[:, hs, :], Dm[:, hs, :], part, ALU.subtract).then_inc(gb_dm, 1)
                        part = banks(4 * a + 2, 1)[:, 0:n2 * P].rearrange("p (h t) -> p h t", h=n2)
                        dve.tensor_tensor(DT[:, hs, :], DT[:, hs, :], part, ALU.subtract).then_inc(gb_ddc, 1)
                    update_states(LEVELS * c + l - 1)
                if c < NB - 1:
                    gdn_decays(c + 1)
                dve.wait_ge(gb_s, c + 1)
                for h in range(HB):
                    last = dve.scalar_tensor_tensor(out=stB[:, h, :], in0=stB[:, h, :], scalar=EG[:, h, P - 1:P],
                                                    in1=bank(5)[:, h, :], op0=ALU.mult, op1=ALU.add)
                last.then_inc(gb_sc, 1)

            def samples_e():
                s = slice(TP, TOK)
                R = HB * TS
                def heads(ap, n=HB):
                    return ap.rearrange("p (h b) -> p h b", h=n)
                dve.memset(qdA[:], 0.0).then_inc(sa_diag, 1)
                k, q, v = (prE[:, t:t + HB, s] for t in (BK, BQ, BV))
                ka, qa = (prE[:, t:t + HP, s] for t in (AK, AQ))
                dve.tensor_tensor(qkS[:], q, k, ALU.mult)
                dve.tensor_tensor(qkA[:], qa, ka, ALU.mult).then_inc(sa_diag, 1)
                dve.wait_ge(sa_bc, 1)
                dve.tensor_copy(beS[:], banks(7, 1).rearrange("p (h t) -> p h t", h=HB)[:, :, P - TS:P])
                dve.wait_ge(sa_eg, 2)
                link(dve.tensor_tensor(eaS[:], egA[:], qa, ALU.mult))
                diag = qdA[:].rearrange("p r c -> p (r c)")
                R2, W2 = HP * TS, HA * TS
                for par in range(2):
                    r = slice(par * DKA, (par + 1) * DKA)
                    last = dve.tensor_copy(heads(diag[r, par * R2:par * R2 + (R2 - 1) * (W2 + 1) + 1:W2 + 1], HP), eaS[r])
                link(last)
                dve.wait_ge(sa_zero, 1)
                diag = kqd[:].rearrange("p r c -> p (r c)")
                step = 2 * R + 1
                dve.tensor_copy(heads(diag[:, 0:(R - 1) * step + 1:step]), k)
                dve.tensor_copy(heads(diag[:, R:R + (R - 1) * step + 1:step]), q).then_inc(sa_diag, 1)
                dve.wait_ge(sa_kst, 1)
                turned = banks(2, 1)
                link(dve.tensor_tensor(vnS[:], heads(turned[:, 0:R]), egS[:], ALU.mult))
                link(dve.tensor_tensor(vnS[:], v, vnS[:], ALU.subtract))
                dve.tensor_tensor(vnS[:], vnS[:], beS[:], ALU.mult).then_inc(sa_vn, 1)
                dve.wait_ge(sa_vn, 1)
                dve.wait_ge(sa_qk, 1)
                dve.tensor_tensor(qkS[:], heads(banks(3, 1)[:, 0:R]), vnS[:], ALU.mult)
                link(dve.tensor_tensor(v, heads(turned[:, R:2 * R]), egS[:], ALU.mult))
                dve.tensor_tensor(v, v, qkS[:], ALU.add).then_inc(sa_o, 1)
                dve.wait_ge(sa_r, 1)
                for par in range(2):
                    va = prE[:, AV + par:AV + HA:2, s]
                    link(dve.tensor_tensor(va, heads(banks(4 + par, 1)[:, 0:R2], HP), va, ALU.mult))
                    last = dve.tensor_tensor(va, heads(turned[:, 2 * R + par * R2:2 * R + (par + 1) * R2], HP), va, ALU.add)
                last.then_inc(sa_o, 1)

            def update_states(j):
                for e in range(2):
                    n = 2 * j + e
                    dve.wait_ge(sa_kv, n + 1)
                    if j < STEPS_A:
                        state, decay = stA_s[:, j, e, :], egA[:, e, j:j + 1]
                    else:
                        h, b = divmod(n - 2 * STEPS_A, TS)
                        state, decay = stB_s[:, b, h, :], egS[:, h, b:b + 1]
                    dve.scalar_tensor_tensor(out=state, in0=state, scalar=decay, in1=kvS[:, n % 4, :],
                                             op0=ALU.mult, op1=ALU.add).then_inc(sa_st, 1)

            def out_norm_e():
                for n in range(HA + HB + 1):
                    if n < HA + HB:
                        y = prE[:, AV + n if n < HA else BV + n - HA, :]
                        g = prE[:, AR + n if n < HA else BZ + n - HA, :]
                        dve.wait_ge(hn_rn, 2 * HB + n + 1)
                        link(dve.scalar_tensor_tensor(out=y, in0=y, scalar=col("gla_onorm" if n < HA else "gdn_onorm"),
                                                      in1=tmp[:, 2 + n % 2, :], op0=ALU.mult, op1=ALU.mult))
                        dve.tensor_tensor(y, y, g, ALU.mult).then_inc(hn_done, 1)
                    if n:
                        m = n - 1
                        dve.wait_ge(o_hi, m + 1)
                        at = AV + m if m < HA else BV + m - HA
                        dve.tensor_tensor(oE[:, at, :], prE[:, at, :], oE[:, AR + m, :].bitcast(F32), ALU.subtract)\
                           .then_inc(o_lo, 1)

            def project_o(s):
                b = FIRST["mix_o0"]
                for n in range(O_TILES):
                    split_ahead(b, 4, 0, n)
                    if n == 0:
                        dve.memset(rawO[:, :, 0:CW - 1], 0.0).then_inc(e_free, 1)
                        dve.wait_ge(e_free, 2 if O_PARTS else 1)
                    if n == 2:
                        zero_sum(s + 1)
                    dve.wait_ge(unit_done, b + n + 1)
                    if n == 0:
                        dve.wait_ge(rstd_ready, s + 1)
                        dve.wait_ge(ssum_added, KD * (s + 1))
                    if n >= KR:
                        take(two(prO[:, n, :]), pair(n % 4 if n < 2 * KR else n % 2),
                             HDC ** -0.5 if OQ <= n < OK else 1.0).then_inc(po_read, 1)
                    else:
                        if n >= 2:
                            dve.wait_ge(conv_step_o, 8 * (n - 1))
                            dve.wait_ge(xo_ready, n - 1)
                        take(two(rawO[:, n % 2, CW - 1:CW - 1 + TOK]), pair(n % 4)).then_inc(po_read, 1)
                        conv(n, n % 2, rawO, histR, lambda k, n: PRM["rg_conv_w"] + k * KR + n, tailO,
                             po_read, n + 1, 8 * n, conv_step_o)
                    if n == KR + 1:
                        dve.wait_ge(o_loaded, 96)
                        dve.tensor_scalar(sbb[:, 1, :], sbb[:, 0, :], -1.0, None, ALU.mult).then_inc(rg_c2, 1)
                        lam = prm[:, PRM["rg_lambda"]:PRM["rg_lambda"] + KR]
                        link(dve.tensor_scalar(cc[:, 3, :], lam, -1.0, 0.0, ALU.mult, ALU.max))
                        dve.wait_ge(rg_c1, 1)
                        link(dve.tensor_tensor(cc[:, 3, :], cc[:, 3, :], cc[:, 2, :], ALU.add))
                        dve.tensor_scalar(cc[:, 0, :], cc[:, 3, :], -RG_C, None, ALU.mult)
                        dve.tensor_scalar(cc[:, 1, :], cc[:, 3, :], RG_C, None, ALU.mult).then_inc(rg_c2, 1)
                    if n >= 2 * KR:
                        (rg_gelu_arg, rg_mult_square, rg_scan)[(n - 2 * KR) % 3]((n - 2 * KR) // 3)

            def rg_gelu_arg(m):
                u, y = tmp[:, 2 + m % 2, :], prO[:, OY + m, :]
                dve.wait_ge(po_read, KR + m + 1)
                if m >= 2:
                    dve.wait_ge(rg_gelu, m - 1)
                link(dve.tensor_tensor(u, y, y, ALU.mult))
                link(dve.tensor_scalar(u, u, 0.044715, 1.0, ALU.mult, ALU.add))
                dve.tensor_tensor(u, u, y, ALU.mult).then_inc(rg_u, 1)

            def rg_mult_square(m):
                dve.wait_ge(rg_a, 3 * m + 3)
                link(dve.tensor_tensor(rgR[:, m, :], rgA[:, m, :], rgA[:, m, :], ALU.mult))
                dve.scalar_tensor_tensor(out=rgR[:, m, :], in0=rgR[:, m, :], scalar=1.0, in1=rgT[:, m, :],
                                         op0=ALU.add, op1=ALU.mult).then_inc(rg_m, 1)
                y = prO[:, OY + m, :]
                dve.scalar_tensor_tensor(out=y, in0=tmp[:, 2 + m % 2, :], scalar=1.0, in1=y,
                                         op0=ALU.add, op1=ALU.mult).then_inc(rg_gelu, 1)
                link(dve.tensor_tensor(rgI[:, m, :], rgI[:, m, :], prO[:, OX + m, :], ALU.mult))

            def rg_scan(m):
                x, b, a = prO[:, OX + m, :], rgR[:, m, :], rgA[:, m, :]
                dve.wait_ge(rg_mult, m + 1)
                link(dve.tensor_tensor(b, b, rgI[:, m, :], ALU.mult))
                dve.memset(a[:, 0:1], 0.0)
                link(dve.tensor_copy(b[:, 0:1], rgI[:, m, 0:1]))
                dve.tensor_tensor_scan(x[:, 0:TP], a[:, 0:TP], b[:, 0:TP], 0.0, ALU.mult, ALU.add)
                link(dve.tensor_tensor(x[:, TP:TOK], a[:, TP:TOK], h0T[:, m, :], ALU.mult))
                link(dve.tensor_tensor(x[:, TP:TOK], x[:, TP:TOK], b[:, TP:TOK], ALU.add))
                y = prO[:, OY + m, :]
                dve.scalar_tensor_tensor(out=y, in0=x, scalar=0.5, in1=y, op0=ALU.mult, op1=ALU.mult)\
                   .then_inc(rg_od, 1)

            def rows_o():
                for n in range(NB):
                    dve.wait_ge(kv_t, n + 1)
                    dve.tensor_copy(vtok[:, n, :], banks(n, 1)).then_inc(v_rows, 1)
                for n in range(3):
                    dve.wait_ge(row_t, n + 1)
                    dve.tensor_copy(rowS[:, n, :], banks(n, 1)[0:TS, :]).then_inc(v_rows, 1)

            def stick():
                def mask(buf, a):
                    for at, _ in SCORE:
                        last = dve.tensor_tensor(buf[:, a, at:at + P], buf[:, a, at:at + P], before[:], ALU.mult)
                    return last

                dve.wait_ge(o_consts, 5)
                def add_later(n):
                    dve.wait_ge(sk_acc, n + 1)
                    dve.tensor_tensor(skY[:, n % 3, :], skY[:, n % 3, :], banks(3, 3)[:, 0:SCORES], ALU.add)\
                       .then_inc(sk_add, 1)

                for h in range(HC):
                    a = h % 2
                    if h:
                        add_later(h - 1)
                    dve.wait_ge(sk_ln, h + 1)
                    link(dve.tensor_tensor(skX[:, a, :], skX[:, a, :], skL[:], ALU.add))
                    link(mask(skX, a))
                    x1, x2, x3 = (skX[:, a, at:at + w] for at, w in SCORE[1:])
                    w1 = TP - P
                    dve.tensor_copy(skR[:, w1:w1 + P], x2[:, 0:P])
                    dve.tensor_copy(skR[:, 0:P], x1[:, 0:P])
                    link(dve.tensor_tensor(skR[:, w1 + P:], x2[:, P:], x3, ALU.add))
                    dve.tensor_tensor(skR[:, P:w1], x1[:, P:], skR[:, w1:], ALU.add).then_inc(sk_sp, 1)
                    dve.tensor_tensor(skY[:, h % 3, :], skY[:, h % 3, :], skL[:], ALU.add).then_inc(sk_added, 1)
                    dve.wait_ge(sk_added, h + 1)
                    sample_scores(h)
                add_later(HC - 1)

            def sample_scores(b):
                dve.wait_ge(sm_q, b + 1)
                dve.wait_ge(page_loaded[b % 4], 16 * PAGES * (b // 4 + 1))
                for p in range(PAGES):
                    link(dve.tensor_tensor(kq[:], pages[:, b % 4, p, :], banks(7, 1), ALU.mult))
                    last = dve.tensor_reduce(smS[:, 0, p, b, :], kq[:].rearrange("p (h d) -> p h d", h=HC), AX.X, ALU.add)
                    if p < PAGES - 1:
                        link(last)
                last.then_inc(sm_kq, 1)
                dve.wait_ge(sm_kq, b + 1)

            def samples_o():
                z, sp, w = (smS[:, n] for n in range(3))
                def flat(x):
                    return x.rearrange("p a b h -> p (a b) h")
                bias = sbb[:, 0:1, :].to_broadcast([P, PAGES * TS, HC])
                dve.tensor_tensor(flat(z), flat(z), bias, ALU.add).then_inc(sm_step, 1)
                dve.wait_ge(sm_step, 1)
                dve.tensor_scalar(w, z, 0.0, None, ALU.min)
                dve.wait_ge(sm_ln, 1)
                link(dve.tensor_scalar(z, z, 0.0, None, ALU.max))
                dve.tensor_tensor(w, w, sp, ALU.subtract)
                dve.tensor_tensor(z, z, sp, ALU.add).then_inc(sm_step, 1)
                dve.wait_ge(sm_sum, 1)
                acc = banks(3, 1)[:, 0:PAGES * TS * HC]
                dve.tensor_tensor(w.rearrange("p a b h -> p (a b h)"), w.rearrange("p a b h -> p (a b h)"), acc,
                                  ALU.subtract).then_inc(sm_step, 1)
                dve.wait_ge(sm_pv, TS)
                dve.wait_ge(o_consts, 10 + TS)
                rows = TS * HC
                dve.tensor_tensor(smO[:].rearrange("p (h d) -> p h d", h=HC),
                                  banks(4, 1)[0:rows, :].rearrange("p (h d) -> p h d", h=HC),
                                  own[:].rearrange("p (h a) -> p h a", a=1).to_broadcast([rows, HC, HDC]), ALU.mult)\
                   .then_inc(sm_step, 1)
                for m in range(KC + KR):
                    dve.wait_ge(o_hi, O_PARTS + m + 1)
                    at, high = (OQ + m, OK + m) if m < KC else (OY + m - KC, OX + m - KC)
                    dve.tensor_tensor(oO[:, at, :], prO[:, at, :], oO[:, high, :].bitcast(F32), ALU.subtract)\
                       .then_inc(o_lo, 1)

            zero_sum(0)
            dve.wait_ge(setup_t, 1)
            dve.tensor_copy(prm[:], banks(5, 1)[:, 0:NPRM]).then_inc(prm_ready, 1)
            dve.wait_ge(setup_t, 2)
            dve.tensor_copy(xT[:, :, TP:TOK], banks(4, 1)[:, 0:KD * TS].rearrange("p (m s) -> p m s", m=KD))\
               .then_inc(prm_ready, 1)
            dve.wait_ge(prm_ready, 2)
            for m in range(KD):
                if m < LOOKAHEAD:
                    split(m, 4, 0, 0)
                add_square(0, m, m % 2)
            dve.wait_ge(setup_t, 3 + KD)
            hist = banks(6, 1)
            n = TS * (CW - 1)
            dve.tensor_copy(histG[:].rearrange("p a b c -> p (a b c)"), hist[:, 0:QKV * n]).then_inc(prm_ready, 1)
            dve.tensor_copy(histR[:].rearrange("p a b c -> p (a b c)"), hist[:, QKV * n:(QKV + KR) * n])\
               .then_inc(prm_ready, 1)
            dve.tensor_copy(h0T[:].rearrange("p a b -> p (a b)"),
                            hist[:, (QKV + KR) * n:(QKV + KR) * n + KR * TS]).then_inc(prm_ready, 1)
            for s, (name, f) in enumerate(STAGES):
                if name == "ffn":
                    ffn_in(s, f)
                    ffn_down(s, f)
                elif name == "mix_e":
                    project_e(s)
                    turned_e()
                    samples_e()
                    gdn_decays(0)
                    for c in range(NB):
                        gdn(c)
                    out_norm_e()
                    out_proj(s, "out_e0")
                elif name == "mix_o":
                    project_o(s)
                    rows_o()
                    stick()
                    samples_o()
                    out_proj(s, "out_o0")
            last_norm()

        @block.tensor
        def _(pe):
            def unit(s, number, rhs_hi, rhs_lo, tiles, psum, start, stop, ready=None):
                slot = s % SPLIT_SLOTS
                pe.wait_ge(lo_ready, number + 1)
                for k in range(tiles):
                    if ready is not None:
                        ready(k)
                    hi, lo = (w[:, slot, k * P:(k + 1) * P] for w in (whi, wlo))
                    for w, x in ((hi, rhs_hi), (hi, rhs_lo), (lo, rhs_hi)):
                        for half in range(2):
                            last = w is lo and k == tiles - 1
                            mm = pe.matmul(psum[:, half, :], w, x(k)[:, half * HALF:(half + 1) * HALF],
                                           start=start and k == 0 and w is hi and x is rhs_hi, stop=stop and last)
                mm.then_inc(unit_done, 1)

            def h_hi_tile(k):
                return hh[:, k, :]

            def h_lo_tile(k):
                return hl[:, k, :]

            def norm(k):
                if k == 0:
                    pe.wait_ge(prm_ready, 5)
                pe.wait_ge(ssum_added, KD * (k + 1))
                for half in range(2):
                    mm = pe.matmul(pair(3)[:, half, :], ones[:], ssum[:, half * HALF:(half + 1) * HALF],
                                   start=True, stop=True)
                mm.then_inc(norm_sum, 1)

            def ffn_in(s, f):
                b = FIRST[f"in{f}"]

                def body(t):
                    peeled = isinstance(t, int) and t == 0
                    for a in range(2):
                        n = KF * f + 2 * t + a
                        for up in range(2):
                            q = 2 * a + up
                            if not peeled:
                                pe.wait_ge(up_read if up else gate_read, n - 1)
                            if peeled and q == 3:
                                pe.wait_ge(ln_ready, s + 1)
                            if peeled and q == 0:
                                pe.wait_ge(x_ready, KD * (s + 1) - 1)
                            unit(b + q, b + 4 * t + q, h_hi_tile, h_lo_tile, KD, pair(q), True, True,
                                 (lambda k: pe.wait_ge(h_lo, KD * s + k + 1)) if peeled and q == 0 else None)
                            if peeled and q == 0:
                                norm(s)
                body(0)
                loop(pe, 1, KF // 2, body)

            def ffn_down(s, f):
                b = FIRST[f"down{f}"]

                def body(t):
                    for a in range(4):
                        pe.wait_ge(x_ready, KD * (s + 1) + 4 * t + a - 3)
                        pe.wait_ge(up_read, KF * (f + 1) - 1 + a // 2)
                        for c in range(PARTS):
                            k0 = UNIT * c
                            n = min(UNIT, KF - k0)
                            pe.wait_ge(act_lo, KF * f + k0 + n)
                            q = PARTS * a + c
                            unit(b + q, b + 4 * PARTS * t + q, lambda k: act_h[:, k0 + k, :],
                                 lambda k: act_l[:, k0 + k, :], n, pair(a), c == 0, c == PARTS - 1)
                loop(pe, 0, KD // 4, body)

            def project(s, b, tiles, read, extra):
                def body(t):
                    peeled = isinstance(t, int) and t == 0
                    for q in range(4):
                        if not peeled:
                            pe.wait_ge(read, 4 * t + q - 3 + extra)
                        elif q == 2:
                            pe.wait_ge(read, extra)
                        elif q == 3:
                            pe.wait_ge(ln_ready, s + 1)
                        unit(b + q, b + 4 * t + q, h_hi_tile, h_lo_tile, KD, pair(q), True, True,
                             (lambda k: pe.wait_ge(h_lo, KD * s + k + 1)) if peeled and q == 0 else None)
                        if peeled and q == 0:
                            norm(s)
                body(0)
                loop(pe, 1, tiles // 4, body)

            def out_proj(s, name, parts, hi, lo):
                b = FIRST[name]

                def body(t):
                    for a in range(4):
                        pe.wait_ge(x_ready, KD * (s + 1) + 4 * t + a - 3)
                        unit(b + a, b + 4 * t + a, hi, lo, KD, pair((a + 2) % 4), True, True,
                             (lambda k: pe.wait_ge(o_lo, parts - KD + k + 1)) if isinstance(t, int) and a + t == 0 else None)
                body(0)
                loop(pe, 1, KD // 4, body)

            def project_e(s):
                b = FIRST["mix_e0"]
                unit(b, b, h_hi_tile, h_lo_tile, KD, pair(2), True, True, lambda k: pe.wait_ge(h_lo, KD * s + k + 1))
                project(s, b + 1, QKV, pe_read, 1)
                gates_e()
                for n in range(QKV, E_TILES):
                    pe.wait_ge(pe_read, n + 1 if n >= GLA_AT + 2 else n)
                    unit(b + 1 + n, b + 1 + n, h_hi_tile, h_lo_tile, KD, pair(tile_pair(n)), True, True)
                    if L2_AT <= n < L2_AT + HB:
                        for m in range(2):
                            unit_sum(2 * (n - L2_AT) + m)
                    if n >= GLA_AT + 1:
                        c = (n - GLA_AT - 1) // 2
                        if (n - GLA_AT - 1) % 2 == 0 and c < NB:
                            gla_scores(c)
                        elif (n - GLA_AT - 1) % 2:
                            gla_outputs(c)

            def mm1(out, w, x):
                return pe.matmul(out, w, x, start=True, stop=True)

            def gates_e():
                pe.wait_ge(e_loaded, 64)
                pe.wait_ge(pe_read, QKV + 1)
                for h in range(HP):
                    for half in range(2):
                        mm = mm1(pair(h)[:, half, :], wgate[:, h * P:(h + 1) * P],
                                 small[0:RANK, half * HALF:(half + 1) * HALF])
                mm.then_inc(gla_z, 1)

            def unit_sum(n):
                pe.wait_ge(hn_sq, n + 1)
                if n >= 2:
                    pe.wait_ge(hn_rn, n - 1)
                for half in range(2):
                    mm = mm1(pair(n % 2)[:, half, :], ones[:], tmp[:, n % 2, half * HALF:(half + 1) * HALF])
                mm.then_inc(hn_sum, 1)

            def turned_e():
                pe.wait_ge(gates, 2)
                pe.wait_ge(pe_read, E_TILES + 1)
                for c in range(NB):
                    mm = turn(banks(7, 1)[:, c * 96:(c + 1) * 96], small[:, c * P:(c + 1) * P], 96)
                mm.then_inc(col_t, 1)
                pe.wait_ge(conv_step, 8 * QKV)
                pe.wait_ge(ga_oc, NB)
                for n in range(QKV):
                    mm = turn(banks(4 + n // 4, 1)[0:TAIL, n % 4 * P:(n % 4 + 1) * P], tailE[:, n, :], P)
                mm.then_inc(col_t, 1)
                pe.wait_ge(tail_row, 3)
                pe.wait_ge(col_ready, 1)

            def gla_scores(c):
                t = slice(c * P, (c + 1) * P)
                pe.wait_ge(pe_read, AR + 1)
                pe.wait_ge(hn_rn, 2 * HB)
                if c:
                    pe.wait_ge(ga_vtc, c)
                    pe.wait_ge(ga_sc, c)
                for h in range(HA):
                    mm = turn(banks(2, 1)[:, h * P:(h + 1) * P], prE[:, AV + h, t], P)
                mm.then_inc(ga_vt, 1)
                pe.wait_ge(ga_fac2, 2 * HP * (c + 1))
                for h in range(HP):
                    for q in range(2):
                        r = slice(q * DKA, (q + 1) * DKA)
                        for j in range(4):
                            mm = mm1(PS[32 * j:32 * j + 32, q, h * P:(h + 1) * P], dkA[r, h, 32 * j:32 * j + 32],
                                     dq[r, h, j, :])
                mm.then_inc(ga_att, 1)
                for h in range(HP):
                    mm = turn(banks(3, 1)[:, h * P:(h + 1) * P], kdA[:, h, :], P)
                mm.then_inc(ga_kdt, 1)

            def gla_outputs(c):
                pe.wait_ge(ga_vtc, c + 1)
                pe.wait_ge(ga_mask, c + 1)
                if c:
                    pe.wait_ge(ga_oc, c)
                for n in range(HA):
                    h, q = n // 2, n % 2
                    r = slice(q * DKA, (q + 1) * DKA)
                    out = banks(4 + q, 1)[:, h * P:(h + 1) * P]
                    pe.matmul(out, vtA[:, n, :], attT[:, q, h, :], start=True, stop=False)
                    mm = pe.matmul(out, stA[r, h, :], qgA[r, h, :], start=False, stop=True)
                mm.then_inc(ga_o, 1)
                pe.wait_ge(ga_kdtc, c + 1)
                for n in range(HA):
                    h, q = n // 2, n % 2
                    mm = mm1(banks(3, 1)[q * DKA:(q + 1) * DKA, HP * P + h * DV:HP * P + (h + 1) * DV],
                             kdtA[:, h, q * DKA:(q + 1) * DKA], vtA[:, n, :])
                mm.then_inc(ga_s, 1)

            def row_of(r, width=P):
                def of(rows):
                    return ident[0:rows, r:r + 1].to_broadcast([rows, width])
                return of

            def gdn_starts(c):
                t = slice(c * P, (c + 1) * P)
                bank = lambda n, h: banks(n, 1)[:, h * P:(h + 1) * P]
                for h in range(HB):
                    mm1(bank(0, h), row_of(32 + h)(96), small[:, t])
                    mm = mm1(bank(1, h), row_of(64 + h)(96), small[:, t])
                mm.then_inc(gb_bc, 1)
                for h in range(HB):
                    mm1(bank(2, h), prE[:, BK + h, t], prE[:, BK + h, t])
                    mm = mm1(bank(3, h), prE[:, BK + h, t], prE[:, BQ + h, t])
                mm.then_inc(gb_kq, 1)

            def gdn(c):
                t = slice(c * P, (c + 1) * P)
                n2 = HB // 2
                bank = lambda n, h: banks(n, 1)[:, h * P:(h + 1) * P]
                pe.wait_ge(gb_dt0, c + 1)
                for h in range(HB):
                    mm = turn(bank(6, h), DT[:, h, :], P)
                mm.then_inc(gb_d0, 1)
                if c:
                    pe.wait_ge(gb_oc, c)
                    pe.wait_ge(gb_sc, c)
                for h in range(HB):
                    turn(bank(4, h), prE[:, BK + h, t], P)
                    mm = turn(bank(5, h), prE[:, BV + h, t], P)
                mm.then_inc(gb_kv, 1)
                for h in range(HB):
                    mm = mm1(bank(7, h), prE[:, BK + h, t], stB[:, h, :])
                mm.then_inc(gb_wt, 1)
                pe.wait_ge(gb_d0c, c + 1)
                pe.wait_ge(gb_eg, c + 1)
                pe.wait_ge(gb_ks, c + 1)
                for l in range(1, 7):
                    e = 12 * c + 2 * (l - 1)
                    for a in range(2):
                        if l > 1:
                            pe.wait_ge(gb_dm, 10 * c + 2 * (l - 2) + a + 1)
                        pe.wait_ge(gb_lm, LEVELS * c + l)
                        for j in range(n2):
                            h = n2 * a + j
                            mm = mm1(bank(4 * a, j), cut(l - 1)[:, h, :], Dm[:, h, :])
                        mm.then_inc(gb_t1, 1)
                    if l == 1:
                        pe.wait_ge(gb_qkr, c + 1)
                        pe.wait_ge(gb_vb, c + 1)
                    update_rows(LEVELS * c + l - 1)
                    for a in range(2):
                        pe.wait_ge(gb_t1c, e + a + 1)
                        if l > 1:
                            pe.wait_ge(gb_ddc, e + a - 1)
                        for j in range(n2):
                            h = n2 * a + j
                            if l < 6:
                                mm1(bank(4 * a + 1, j), DT[:, h, :], T1[:, h, :])
                            mm = mm1(bank(4 * a + 2, j), T1[:, h, :], DT[:, h, :])
                        mm.then_inc(gb_dd, 1)
                pe.wait_ge(gb_ddc, 12 * (c + 1))
                pe.wait_ge(sa_kv, 2 * LEVELS * (c + 1))
                for h in range(HB):
                    mm = mm1(bank(7, h), DT[:, h, :], vbB[:, h, :])
                mm.then_inc(gb_vn, 1)
                if c < NB - 1:
                    gdn_starts(c + 1)
                pe.wait_ge(gb_qg, c + 1)
                for h in range(HB):
                    pe.matmul(bank(4, h), stB[:, h, :], qgB[:, h, :], start=True, stop=False)
                    if h == 0:
                        pe.wait_ge(gb_vnc, c + 1)
                    mm = pe.matmul(bank(4, h), T1[:, h, :], QKr[:, h, :], start=False, stop=True)
                mm.then_inc(gb_o, 1)
                for h in range(HB):
                    mm = mm1(bank(5, h), kdB[:, h, :], T1[:, h, :])
                mm.then_inc(gb_s, 1)

            def samples_e():
                pe.wait_ge(ga_oc, NB)
                pe.wait_ge(ga_sc, NB)
                pe.wait_ge(hn_done, 2 * HB)
                R = HB * TS
                for h in range(HB):
                    mm1(banks(6, 1)[:, h * P:(h + 1) * P], row_of(32 + h)(96), small[:, TOK - P:TOK])
                    mm = mm1(banks(7, 1)[:, h * P:(h + 1) * P], row_of(64 + h)(96), small[:, TOK - P:TOK])
                mm.then_inc(sa_bc, 1)
                pe.wait_ge(sa_diag, 2)
                mm1(banks(3, 1)[:, 0:R], ones[:], qkS[:].rearrange("p h b -> p (h b)"))
                for q in range(2):
                    r = slice(q * DKA, (q + 1) * DKA)
                    mm = mm1(banks(4 + q, 1)[:, 0:HP * TS], ones[r, :], qkA[r].rearrange("p h b -> p (h b)"))
                mm.then_inc(sa_qk, 1)
                pe.wait_ge(sa_diag, 3)
                for r in range(R):
                    mm = pe.matmul(banks(0, 1)[0:2 * R, 0:DV], kqd[:, r, :], stB_s[:, r % TS, r // TS, :],
                                   start=r == 0, stop=r == R - 1)
                mm.then_inc(sa_ks, 1)
                pe.wait_ge(e_loaded, 96)
                for r in range(HP * TS):
                    mm = pe.matmul(banks(1, 1)[0:HA * TS, 0:DV], qdA[:, r, :], stA_s[:, r % TS, r // TS, :],
                                   start=r == 0, stop=r == HP * TS - 1)
                mm.then_inc(sa_ks, 1)
                pe.wait_ge(sa_ksc, 2)
                turn(banks(2, 1)[:, 0:2 * R], kqR[:], 2 * R)
                turn(banks(2, 1)[:, 2 * R:2 * R + HA * TS], qaR[:], HA * TS).then_inc(sa_kst, 1)
                for h in range(HA):
                    mm = turn(banks(1, 1)[0:TS, h * P:(h + 1) * P], prE[:, AV + h, TP:TOK], P)
                mm.then_inc(sa_r, 1)
                pe.wait_ge(sa_vn, 1)
                turn(banks(0, 1)[0:R, 0:DV], vnS[:].rearrange("p h b -> p (h b)"), P).then_inc(sa_r, 1)

            def update_rows(j):
                if j >= 2:
                    pe.wait_ge(sa_kv, 2 * (j - 1))
                out = banks(7 if j % 2 else 3, 1)
                if j < STEPS_A:
                    for q in range(2):
                        mm = mm1(out[q * DKA:(q + 1) * DKA, 0:HP * P], ident[0:TS, j:j + 1].to_broadcast([TS, DKA]),
                                 vaR[:].rearrange("p (h q) v -> p q h v", q=2)[:, q])
                else:
                    for e in range(2):
                        mm = mm1(out[:, e * P:(e + 1) * P], row_of(2 * (j - STEPS_A) + e)(HB * TS), vnR[:])
                mm.then_inc(sa_b, 1)

            def out_norm_e():
                pe.wait_ge(gb_oc, NB)
                pe.wait_ge(gb_sc, NB)
                for n in range(HA + HB):
                    unit_sum(2 * HB + n)

            def project_o(s):
                b = FIRST["mix_o0"]
                for n in range(O_TILES):
                    early = n < 2 * KR
                    if n >= 2 * KR and (n - 2 * KR) % 3 == 0:
                        m = (n - 2 * KR) // 3
                        pe.wait_ge(o_loaded, 96)
                        pe.wait_ge(xo_ready, m + 1)
                        pe.wait_ge(po_read, 2 * KR)
                        if m:
                            pe.wait_ge(rg_sig, 2 * m)
                        for a in range(2):
                            for half in range(2):
                                mm = mm1(pair(2 + a)[:, half, :], wrg[:, a, m, :],
                                         prO[:, OX + m, half * HALF:(half + 1) * HALF])
                        mm.then_inc(rg_z, 1)
                    if n == 1:
                        norm(s)
                    if n == 3:
                        pe.wait_ge(ln_ready, s + 1)
                    if early and n >= 4:
                        pe.wait_ge(po_read, n - 3)
                    elif not early:
                        pe.wait_ge(po_read, n - 1)
                    unit(b + n, b + n, h_hi_tile, h_lo_tile, KD, pair(n % 4 if early else n % 2), True, True,
                         (lambda k: pe.wait_ge(h_lo, KD * s + k + 1)) if n == 0 else None)

            def rows_o():
                pe.wait_ge(po_read, O_TILES)
                pe.wait_ge(rg_sig, 2 * KR)
                for tiles, at in ((OV, 0), (OK, 4)):
                    for c in range(NB):
                        for m in range(KC):
                            mm = turn(banks(at + c, 1)[:, m * P:(m + 1) * P], prO[:, tiles + m, c * P:(c + 1) * P], P)
                        mm.then_inc(kv_t, 1)
                for n, tiles in enumerate((OQ, OK, OV)):
                    pe.wait_ge(v_rows, n + 1)
                    for m in range(KC):
                        mm = turn(banks(n, 1)[0:TS, m * P:(m + 1) * P], prO[:, tiles + m, TP:TOK], P)
                    mm.then_inc(row_t, 1)
                pe.wait_ge(v_rows, NB)
                pe.wait_ge(rg_od, KR)
                for m in range(KR):
                    mm = turn(banks(3, 1)[0:1 + TS, m * P:(m + 1) * P], prO[:, OX + m, TP - 1:TOK], P)
                mm.then_inc(row_t, 1)
                pe.wait_ge(k_rows, 1)
                for m in range(KR):
                    mm = turn(banks(4, 1)[0:TAIL, m * P:(m + 1) * P], tailO[:, m, :], P)
                mm.then_inc(row_t, 1)

            def stick():
                pe.wait_ge(v_rows, NB + 3)
                pe.wait_ge(k_rows, NB + 2)
                for h in range(HC + 2):
                    if h < HC:
                        r = slice(h % 2 * HDC, (h % 2 + 1) * HDC)
                        if h:
                            pe.wait_ge(sk_read, h)
                        for n, (at, w) in enumerate(SCORE):
                            mm = mm1(banks(0, 3)[:, at:at + w], prO[r, OK + h // 2, n * P:(n + 1) * P],
                                     prO[r, OQ + h // 2, n * P:TP])
                        mm.then_inc(sk_z, 1)
                    if 1 <= h <= HC:
                        a = (h - 1) % 2
                        if h > 1:
                            pe.wait_ge(sk_add, h - 1)
                        pe.wait_ge(sk_sp, h)
                        later = [skR[:, 0:TP - P], skR[:, TP - P:], skX[:, a, SCORE[3][0]:SCORE[3][0] + P]]
                        for n, (at, w) in enumerate(SCORE):
                            acc = banks(3, 3)[:, at:at + w]
                            mm = pe.matmul(acc, after[:], skX[:, a, at:at + w], start=True, stop=n == NB - 1)
                            if n < NB - 1:
                                mm = pe.matmul(acc[:, P:], ones[:], later[n], start=False, stop=True)
                        mm.then_inc(sk_acc, 1)
                    if h < HC:
                        if h:
                            pe.wait_ge(sm_kq, h)
                        mm1(banks(7, 1), row_of(h)(TS), rowS[:, 0, :]).then_inc(sm_q, 1)
                    if h >= 2:
                        n = h - 2
                        r = slice(n % 2 * HDC, (n % 2 + 1) * HDC)
                        if n:
                            pe.wait_ge(sk_oc, n)
                        pe.wait_ge(sk_mask, n + 1)
                        for c, (at, w) in enumerate(SCORE):
                            mm = pe.matmul(banks(6, 1)[r, c * P:TP], vtok[:, c, n * HDC:(n + 1) * HDC],
                                           skY[:, n % 3, at:at + w], start=c == 0, stop=c == NB - 1)
                        mm.then_inc(sk_o, 1)

            def samples_o():
                pe.wait_ge(sm_step, 2)
                pe.wait_ge(sk_add, HC)
                n = TS * HC
                x = [smS[:, 0, p].rearrange("p b h -> p (b h)") for p in range(PAGES)]
                for p in range(PAGES):
                    acc = banks(3, 1)[:, p * n:(p + 1) * n]
                    mm = pe.matmul(acc, after[:], x[p], start=True, stop=p == PAGES - 1)
                    for later in range(p + 1, PAGES):
                        mm = pe.matmul(acc, ones[:], x[later], start=False, stop=later == PAGES - 1)
                mm.then_inc(sm_sum, 1)
                pe.wait_ge(sm_w, 1)
                pe.wait_ge(o_consts, 10 + TS)
                for b in range(TS):
                    pe.wait_ge(page_loaded[b % 4], 16 * PAGES * ((b + TS) // 4 + 1))
                    for p in range(PAGES):
                        mm = pe.matmul(banks(4, 1)[0:n, :], smW[:, p, b].rearrange("p b h -> p (b h)"),
                                       pages[:, b % 4, p, :], start=b + p == 0, stop=b == TS - 1 and p == PAGES - 1)
                    mm.then_inc(sm_pv, 1)
                pe.wait_ge(sm_step, 4)
                for m in range(KC):
                    mm = mm1(banks(5, 1)[:, m * TS:(m + 1) * TS], smO[:, m * P:(m + 1) * P], of_sample[:])
                mm.then_inc(sm_sum, 1)

            def turn(dst, src, n):
                return pe.transpose(dst, src, ident[0:n, 0:n])

            pe.wait_ge(consts, 3)
            pe.wait_ge(p_loaded, 16 * (len(ROWS_A) + len(ROWS_B)))
            turn(banks(5, 1)[:, 0:NA], prow_a[:], NA)
            turn(banks(5, 1)[:, NA:NPRM], prow_b[:], NPRM - NA).then_inc(setup_t, 1)
            pe.wait_ge(x_loaded, 16 * (NB + 1))
            for m in range(KD):
                mm = turn(banks(4, 1)[:, m * TS:(m + 1) * TS], xsrow[:, m * P:(m + 1) * P], TS)
            mm.then_inc(setup_t, 1)
            for m in range(KD):
                if m >= 4:
                    pe.wait_ge(x_ready, m - 3)
                for b in range(NB):
                    mm = turn(banks(m % 4, 1)[:, b * P:(b + 1) * P], xrow[:, b, m * P:(m + 1) * P], P)
                mm.then_inc(setup_t, 1)
            pe.wait_ge(s_loaded, 48)
            n = TS * (CW - 1)
            for m in range(QKV):
                turn(banks(6, 1)[:, m * n:(m + 1) * n], hrow_g[:, m * P:(m + 1) * P], n)
            for m in range(KR):
                turn(banks(6, 1)[:, (QKV + m) * n:(QKV + m + 1) * n], hrow_r[:, m * P:(m + 1) * P], n)
                at = (QKV + KR) * n + m * TS
                mm = turn(banks(6, 1)[:, at:at + TS], hrow_0[:, m * P:(m + 1) * P], TS)
            mm.then_inc(setup_t, 1)
            pe.wait_ge(x_ready, KD)
            for s, (name, f) in enumerate(STAGES):
                if name == "ffn":
                    ffn_in(s, f)
                    ffn_down(s, f)
                elif name == "mix_e":
                    project_e(s)
                    turned_e()
                    samples_e()
                    pe.wait_ge(sa_rc, 2)
                    pe.wait_ge(sa_o, 2)
                    gdn_starts(0)
                    for c in range(NB):
                        gdn(c)
                    out_norm_e()
                    out_proj(s, "out_e0", HA + HB, lambda m: oE[:, AR + m, :],
                             lambda m: oE[:, AV + m if m < HA else BV + m - HA, :])
                elif name == "mix_o":
                    project_o(s)
                    rows_o()
                    stick()
                    samples_o()
                    out_proj(s, "out_o0", O_PARTS + KC + KR, lambda m: oO[:, OK + m if m < KC else OX + m - KC, :],
                             lambda m: oO[:, OQ + m if m < KC else OY + m - KC, :])
            norm(LAST_NORM)
            for m in range(KD):
                pe.wait_ge(y_ready, m + 1)
                if m >= 4:
                    pe.wait_ge(y_row, m - 3)
                y = tmp[:, m % 4, :]
                turn(banks(4 + m // 4, 1)[0:TS, (m % 4) * P:(m % 4 + 1) * P], y[:, TP:TOK], P)
                for b in range(NB):
                    mm = turn(banks(m % 4, 1)[:, b * P:(b + 1) * P], y[:, b * P:(b + 1) * P], P)
                mm.then_inc(y_t, 1)


_OUTS = ["y_prompt", "y_sample", "gla_p", "gla_s", "gdn_p", "gdn_s", "gcv_p", "gcv_s",
         "sbk_p", "sbk_s", "sbv_p", "sbv_s", "rgh_p", "rgh_s", "rgc_p", "rgc_s"]


def _shapes(a):
    bp, tp, dm = a["x_prompt"]
    bs = a["x_sample"][0]
    gla, gdn, conv = a["state_gla"][2:], a["state_gdn"][2:], a["state_gdn_conv"][2:]
    kv, h, rc = a["cache_sb_k"][3:], a["state_rg_h"][2:], a["state_rg_conv"][2:]
    ne, no = a["state_gla"][0], a["state_rg_h"][0]
    return [(bp, tp, dm), tuple(a["x_sample"]), (ne, bp) + gla, (ne, bs) + gla, (ne, bp) + gdn, (ne, bs) + gdn,
            (ne, bp) + conv, (ne, bs) + conv, (no, bp, tp) + kv, (no, bs, 1) + kv, (no, bp, tp) + kv,
            (no, bs, 1) + kv, (no, bp) + h, (no, bs) + h, (no, bp) + rc, (no, bs) + rc]


def kernel(**inputs):
    import numpy as _np
    import concourse.bacc as _bacc
    from concourse import mybir as _mybir
    from concourse.bass_utils import run_bass_kernel_spmd as _run

    nc = _bacc.Bacc("TRN2", target_bir_lowering=False, num_devices=1)
    arrays, ins, outs = {}, {}, {}
    for name, value in inputs.items():
        a = _np.ascontiguousarray(value)
        arrays[f"in_{name}"] = a
        ins[name] = nc.dram_tensor(f"in_{name}", a.shape, _mybir.dt.from_np(a.dtype), kind="ExternalInput").ap()
    shapes = _shapes({k: tuple(a.shape) for k, a in inputs.items()})
    for name, shape in zip(_OUTS, shapes):
        outs[name] = nc.dram_tensor(f"out_{name}", shape, F32, kind="ExternalOutput").ap()
    build_step(nc, ins, outs)
    r = _run(nc, [arrays], core_ids=[0])
    return tuple(r.results[0][f"out_{name}"] for name in _OUTS)
```
